# Optimizing a Trainium2 kernel written in Bass

```python
import math
import jax, jax.numpy as jnp
from jax import lax
import numpy as np

D_MODEL = 1024
BATCH = 1
SEQ = 512
DEPTH = 2

P_DIM = 256
D_FF = 2816
ML_HEADS = 4
ML_QK_DIM = 64
ML_V_DIM = 128
ML_CHUNK = 64
SW_Q_HEADS = 8
SW_KV_HEADS = 2
SW_HEAD_DIM = 64
WINDOW = 128
REL_BUCKETS = 32
REL_MAX_DIST = 128
EPS = 1e-6

ML_QK_W = ML_HEADS * ML_QK_DIM
ML_V_W = ML_HEADS * ML_V_DIM
SW_Q_W = SW_Q_HEADS * SW_HEAD_DIM
SW_KV_W = SW_KV_HEADS * SW_HEAD_DIM
SPLITS = (ML_QK_W, ML_QK_W, ML_V_W, ML_V_W, ML_HEADS, ML_HEADS, SW_Q_W, SW_KV_W, SW_KV_W, D_MODEL, D_MODEL)
D_IN = 2 * ML_QK_W + 2 * ML_V_W + 2 * ML_HEADS + SW_Q_W + 2 * SW_KV_W + 2 * D_MODEL


def rmsnorm(x, g):
    xf = x.astype(jnp.float32)
    y = xf * lax.rsqrt(jnp.mean(xf * xf, axis=-1, keepdims=True) + EPS)
    return (y * g.astype(jnp.float32)).astype(x.dtype)

def swiglu_ffn(x, wi, wo):
    g, u = jnp.split(x @ wi, 2, axis=-1)
    return (jax.nn.silu(g) * u) @ wo

def t5_bucket(dist):
    max_exact = REL_BUCKETS // 2
    d = np.maximum(dist, 0)
    large = max_exact + (np.log(np.maximum(d, 1) / max_exact) / np.log(REL_MAX_DIST / max_exact)
                         * (REL_BUCKETS - max_exact)).astype(np.int32)
    large = np.minimum(large, REL_BUCKETS - 1)
    return np.where(d < max_exact, d, large).astype(np.int32)

def mlstm_chunkwise(q, k, v, i_pre, f_pre):
    B, S, H, dk = q.shape
    dv = v.shape[-1]
    L = ML_CHUNK
    NC = S // L
    f32 = jnp.float32
    qc = q.astype(f32).reshape(B, NC, L, H, dk)
    kc = (k.astype(f32) / math.sqrt(dk)).reshape(B, NC, L, H, dk)
    vc = v.astype(f32).reshape(B, NC, L, H, dv)
    log_i = jnp.swapaxes(i_pre.astype(f32).reshape(B, NC, L, H), 2, 3)
    log_f = jnp.swapaxes(jax.nn.log_sigmoid(f_pre.astype(f32)).reshape(B, NC, L, H), 2, 3)
    b = jnp.cumsum(log_f, axis=-1)
    g = b[..., -1]
    a = g[..., None] - b + log_i
    m_loc = jnp.max(a, axis=-1)
    w = jnp.exp(a - m_loc[..., None])
    C_loc = jnp.einsum('bnhl,bnlhk,bnlhv->bnhkv', w, kc, vc)
    n_loc = jnp.einsum('bnhl,bnlhk->bnhk', w, kc)

    def step(carry, xs):
        C, n, m = carry
        g_c, m_c, C_c, n_c = xs
        m_new = jnp.maximum(g_c + m, m_c)
        s_old = jnp.exp(g_c + m - m_new)
        s_new = jnp.exp(m_c - m_new)
        C_new = s_old[..., None, None] * C + s_new[..., None, None] * C_c
        n_new = s_old[..., None] * n + s_new[..., None] * n_c
        return (C_new, n_new, m_new), (C, n, m)

    init = (jnp.zeros((B, H, dk, dv), f32), jnp.zeros((B, H, dk), f32), jnp.zeros((B, H), f32))
    xs = (jnp.moveaxis(g, 1, 0), jnp.moveaxis(m_loc, 1, 0), jnp.moveaxis(C_loc, 1, 0), jnp.moveaxis(n_loc, 1, 0))
    _, (C_prev, n_prev, m_prev) = lax.scan(step, init, xs)
    C_prev = jnp.moveaxis(C_prev, 0, 1)
    n_prev = jnp.moveaxis(n_prev, 0, 1)
    m_prev = jnp.moveaxis(m_prev, 0, 1)

    causal = jnp.tril(jnp.ones((L, L), dtype=bool))
    D = b[..., :, None] - b[..., None, :] + log_i[..., None, :]
    D = jnp.where(causal, D, -jnp.inf)
    e = b + m_prev[..., None]
    m_t = jnp.maximum(jnp.max(D, axis=-1), e)
    W = jnp.exp(D - m_t[..., None]) * jnp.einsum('bnthd,bnshd->bnhts', qc, kc)
    s_inter = jnp.exp(e - m_t)
    num = (jnp.einsum('bnhts,bnshv->bnthv', W, vc)
           + jnp.swapaxes(s_inter, 2, 3)[..., None] * jnp.einsum('bnthd,bnhdv->bnthv', qc, C_prev))
    den = jnp.sum(W, axis=-1) + s_inter * jnp.einsum('bnthd,bnhd->bnht', qc, n_prev)
    denom = jnp.maximum(jnp.abs(den), jnp.exp(-m_t))
    h = num / jnp.swapaxes(denom, 2, 3)[..., None]
    return h.reshape(B, S, H, dv).astype(q.dtype)

def swa_sink_attention(q, k, v, q_gain, k_gain, sinks, rel_bias):
    B, S, Hq, d = q.shape
    Hkv = k.shape[2]
    G = Hq // Hkv
    Wn = WINDOW
    NB = S // Wn
    f32 = jnp.float32
    q = rmsnorm(q, q_gain)
    k = rmsnorm(k, k_gain)
    qb = q.astype(f32).reshape(B, NB, Wn, Hkv, G, d) * (d ** -0.5)
    kb = k.astype(f32).reshape(B, NB, Wn, Hkv, d)
    vb = v.astype(f32).reshape(B, NB, Wn, Hkv, d)
    shift = lambda t: jnp.concatenate([jnp.zeros_like(t[:, :1]), t[:, :-1]], axis=1)
    kk = jnp.concatenate([shift(kb), kb], axis=2)
    vv = jnp.concatenate([shift(vb), vb], axis=2)
    logits = jnp.einsum('bnqkgd,bnskd->bnkgqs', qb, kk)
    dist = np.arange(Wn)[:, None] + Wn - np.arange(2 * Wn)[None, :]
    in_window = (dist >= 0) & (dist < Wn)
    bias = rel_bias.astype(f32)[t5_bucket(dist)]
    bias = jnp.transpose(bias, (2, 0, 1)).reshape(Hkv, G, Wn, 2 * Wn)
    key_pos = np.arange(NB)[:, None] * Wn - Wn + np.arange(2 * Wn)[None, :]
    valid = in_window[None] & (key_pos >= 0)[:, None, :]
    logits = jnp.where(valid[None, :, None, None], logits + bias, -jnp.inf)
    sink = sinks.astype(f32).reshape(Hkv, G)[None, None, :, :, None, None]
    m = jnp.maximum(jnp.max(logits, axis=-1, keepdims=True), sink)
    pr = jnp.exp(logits - m)
    denom = jnp.sum(pr, axis=-1, keepdims=True) + jnp.exp(sink - m)
    out = jnp.einsum('bnkgqs,bnskd->bnqkgd', pr / denom, vv)
    return out.reshape(B, S, Hq * d).astype(q.dtype)

def first_inputs(seed: int = 0) -> dict:
    key = jax.random.key(seed)
    ks = jax.random.split(key, 24)
    f32 = jnp.float32
    nrm = lambda k, shape, fan_in: jax.random.normal(k, shape, f32) * (fan_in ** -0.5)
    gain = lambda k, shape: 1.0 + 0.05 * jax.random.normal(k, shape, f32)
    return {
        "x": jax.random.normal(ks[0], (BATCH, SEQ, D_MODEL), f32),
        "p": jax.random.normal(ks[1], (DEPTH, BATCH, SEQ, P_DIM), f32),
        "ffn1_norm": gain(ks[2], (DEPTH, D_MODEL)),
        "ffn1_wi": nrm(ks[3], (DEPTH, D_MODEL, 2 * D_FF), D_MODEL),
        "ffn1_wo": nrm(ks[4], (DEPTH, D_FF, D_MODEL), D_FF),
        "mix_norm": gain(ks[5], (DEPTH, D_MODEL)),
        "w_in": nrm(ks[6], (DEPTH, D_MODEL, D_IN), D_MODEL),
        "b_igate": 0.1 * jax.random.normal(ks[7], (DEPTH, ML_HEADS), f32),
        "b_fgate": jnp.linspace(3.0, 6.0, ML_HEADS, dtype=f32)[None, :] + 0.1 * jax.random.normal(ks[8], (DEPTH, ML_HEADS), f32),
        "ml_out_norm": gain(ks[9], (DEPTH, ML_HEADS, ML_V_DIM)),
        "q_norm": gain(ks[10], (DEPTH, SW_HEAD_DIM)),
        "k_norm": gain(ks[11], (DEPTH, SW_HEAD_DIM)),
        "sinks": 0.5 * jax.random.normal(ks[12], (DEPTH, SW_Q_HEADS), f32),
        "rel_bias": 0.5 * jax.random.normal(ks[13], (REL_BUCKETS, SW_Q_HEADS), f32),
        "w_a": nrm(ks[14], (DEPTH, ML_V_W, D_MODEL), ML_V_W),
        "w_b": nrm(ks[15], (DEPTH, SW_Q_W, D_MODEL), SW_Q_W),
        "w_out": nrm(ks[16], (DEPTH, D_MODEL, D_MODEL), D_MODEL),
        "ffn2_norm": gain(ks[17], (DEPTH, D_MODEL)),
        "ffn2_wi": nrm(ks[18], (DEPTH, D_MODEL, 2 * D_FF), D_MODEL),
        "ffn2_wo": nrm(ks[19], (DEPTH, D_FF, D_MODEL), D_FF),
        "ple_norm": gain(ks[20], (DEPTH, D_MODEL)),
        "w_ple_gate": nrm(ks[21], (DEPTH, D_MODEL, D_MODEL), D_MODEL),
        "w_ple": nrm(ks[22], (DEPTH, P_DIM, D_MODEL), P_DIM),
    }

def first_block(x, p, ffn1_norm, ffn1_wi, ffn1_wo, mix_norm, w_in, b_igate, b_fgate, ml_out_norm,
              q_norm, k_norm, sinks, rel_bias, w_a, w_b, w_out, ffn2_norm, ffn2_wi, ffn2_wo,
              ple_norm, w_ple_gate, w_ple):
    B, S, _ = x.shape
    offsets = [int(o) for o in np.cumsum(SPLITS)[:-1]]
    for i in range(DEPTH):
        x = x + 0.5 * swiglu_ffn(rmsnorm(x, ffn1_norm[i]), ffn1_wi[i], ffn1_wo[i])
        u = rmsnorm(x, mix_norm[i])
        z = u @ w_in[i]
        mq, mk, mv, mo, mi, mf, sq, sk, sv, ga, gb = jnp.split(z, offsets, axis=-1)
        hA = mlstm_chunkwise(mq.reshape(B, S, ML_HEADS, ML_QK_DIM),
                             mk.reshape(B, S, ML_HEADS, ML_QK_DIM),
                             mv.reshape(B, S, ML_HEADS, ML_V_DIM),
                             mi + b_igate[i], mf + b_fgate[i])
        hA = rmsnorm(hA, ml_out_norm[i]).reshape(B, S, ML_V_W)
        yA = (jax.nn.sigmoid(mo) * hA) @ w_a[i]
        hB = swa_sink_attention(sq.reshape(B, S, SW_Q_HEADS, SW_HEAD_DIM),
                                sk.reshape(B, S, SW_KV_HEADS, SW_HEAD_DIM),
                                sv.reshape(B, S, SW_KV_HEADS, SW_HEAD_DIM),
                                q_norm[i], k_norm[i], sinks[i], rel_bias)
        yB = hB @ w_b[i]
        mixed = jax.nn.sigmoid(ga) * yA + jax.nn.sigmoid(gb) * yB
        x = x + mixed @ w_out[i]
        x = x + 0.5 * swiglu_ffn(rmsnorm(x, ffn2_norm[i]), ffn2_wi[i], ffn2_wo[i])
        gate = jax.nn.sigmoid(rmsnorm(x, ple_norm[i]) @ w_ple_gate[i])
        x = x + gate * (p[i] @ w_ple[i])
    return x


CHUNK = 128
D_MIX = D_MODEL
GMLP_HEADS = 4
GMLP_HEAD_DIM = 64
GMLP_W = GMLP_HEADS * GMLP_HEAD_DIM
SSD_HEADS = 6
SSD_HEAD_DIM = 64
SSD_W = SSD_HEADS * SSD_HEAD_DIM
SSD_GROUPS = 2
SSD_STATE = 64
SSD_CONV = 4
SSD_XBC = SSD_W + 2 * SSD_GROUPS * SSD_STATE
MLA_HEADS = 6
MLA_NOPE = 64
MLA_ROPE = 32
MLA_V = 64
MLA_W = MLA_HEADS * MLA_V
MLA_Q_RANK = 384
MLA_KV_RANK = 256
ROPE_BASE = 10000.0
D_FF_2 = 4 * D_MODEL
IN_WIDTHS = (2 * GMLP_W, SSD_W, SSD_XBC, SSD_HEADS, MLA_Q_RANK, MLA_KV_RANK, MLA_ROPE)
D_IN_2 = sum(IN_WIDTHS)


def rmsnorm_2(x, g):
    xf = x.astype(jnp.float32)
    var = jnp.mean(xf * xf, axis=-1, keepdims=True)
    return (xf * lax.rsqrt(var + EPS)).astype(x.dtype) * g

def split_cols(proj):
    idx, acc = [], 0
    for w in IN_WIDTHS[:-1]:
        acc += w
        idx.append(acc)
    return jnp.split(proj, idx, axis=-1)

def rope_tables(S):
    half = MLA_ROPE // 2
    pos = jnp.arange(S, dtype=jnp.float32)
    inv_freq = jnp.power(ROPE_BASE, -jnp.arange(half, dtype=jnp.float32) / half)
    ang = pos[:, None] * inv_freq[None, :]
    return jnp.cos(ang), jnp.sin(ang)

def apply_rope(x, cos, sin):
    c = cos[None, :, None, :].astype(x.dtype)
    s = sin[None, :, None, :].astype(x.dtype)
    x1, x2 = jnp.split(x, 2, axis=-1)
    return jnp.concatenate([x1 * c - x2 * s, x2 * c + x1 * s], axis=-1)

def gmlp_mixer(uv, v_norm_g, w_s, b_s):
    Bsz, S, _ = uv.shape
    nc = S // CHUNK
    uv = jax.nn.gelu(uv)
    u, v = jnp.split(uv, 2, axis=-1)
    v = rmsnorm_2(v, v_norm_g).reshape(Bsz, nc, CHUNK, GMLP_HEADS, GMLP_HEAD_DIM)
    causal = jnp.tril(jnp.ones((CHUNK, CHUNK), dtype=w_s.dtype))
    mixed = jnp.einsum('hts,bcshd->bcthd', w_s * causal, v)
    mixed = mixed + b_s.T[None, None, :, :, None]
    return u * mixed.reshape(Bsz, S, GMLP_W)

def causal_depthwise_conv(x, w, b):
    K, C = w.shape
    out = lax.conv_general_dilated(
        x, w[:, None, :], window_strides=(1,), padding=((K - 1, 0),),
        dimension_numbers=('NWC', 'WIO', 'NWC'), feature_group_count=C)
    return out + b

def ssd_mixer(z, xbc, dt_raw, conv_w, conv_b, dt_bias, a_log, d_skip, norm_g):
    Bsz, S, _ = xbc.shape
    nc = S // CHUNK
    hpg = SSD_HEADS // SSD_GROUPS
    xbc = jax.nn.silu(causal_depthwise_conv(xbc, conv_w, conv_b))
    xs, Bm, Cm = jnp.split(xbc, [SSD_W, SSD_W + SSD_GROUPS * SSD_STATE], axis=-1)
    xs_c = xs.reshape(Bsz, nc, CHUNK, SSD_HEADS, SSD_HEAD_DIM)
    B_c = Bm.reshape(Bsz, nc, CHUNK, SSD_GROUPS, SSD_STATE)
    C_c = Cm.reshape(Bsz, nc, CHUNK, SSD_GROUPS, SSD_STATE)
    dt = jax.nn.softplus((dt_raw + dt_bias).astype(jnp.float32))
    A = -jnp.exp(a_log.astype(jnp.float32))
    dt_h = dt.reshape(Bsz, nc, CHUNK, SSD_HEADS).transpose(0, 1, 3, 2)
    a_h = jnp.cumsum(dt_h * A[None, None, :, None], axis=-1)
    causal = jnp.tril(jnp.ones((CHUNK, CHUNK), dtype=bool))
    seg = a_h[..., :, None] - a_h[..., None, :]
    decay = jnp.exp(jnp.where(causal, seg, -jnp.inf))
    cb = jnp.einsum('bctgn,bcsgn->bcgts', C_c, B_c)
    cb_h = jnp.repeat(cb, hpg, axis=2)
    w = cb_h * decay * dt_h[:, :, :, None, :]
    y_diag = jnp.einsum('bchts,bcshp->bcthp', w, xs_c)
    B_h = jnp.repeat(B_c, hpg, axis=3)
    C_h = jnp.repeat(C_c, hpg, axis=3)
    decay_to_end = jnp.exp(a_h[..., -1:] - a_h) * dt_h
    states = jnp.einsum('bchs,bcshn,bcshp->bchpn', decay_to_end, B_h, xs_c)
    chunk_decay = jnp.exp(a_h[..., -1])

    def step(h, inp):
        dec, st = inp
        return dec[:, :, None, None] * h + st, h

    h0 = jnp.zeros((Bsz, SSD_HEADS, SSD_HEAD_DIM, SSD_STATE), states.dtype)
    _, h_prev = lax.scan(step, h0, (chunk_decay.transpose(1, 0, 2), states.transpose(1, 0, 2, 3, 4)))
    h_prev = h_prev.transpose(1, 0, 2, 3, 4)
    y_off = jnp.einsum('bcthn,bchpn,bcht->bcthp', C_h, h_prev, jnp.exp(a_h))
    y = y_diag + y_off + xs_c * d_skip[:, None]
    y = y.reshape(Bsz, S, SSD_W).astype(z.dtype)
    yg = (y * jax.nn.silu(z)).reshape(Bsz, S, SSD_GROUPS, SSD_W // SSD_GROUPS)
    return rmsnorm_2(yg, norm_g.reshape(SSD_GROUPS, -1)).reshape(Bsz, S, SSD_W)

def causal_block_attention(q, k, v, scale):
    Bsz, S, H, Dqk = q.shape
    nq = S // CHUNK
    qb = q.reshape(Bsz, nq, CHUNK, H, Dqk).transpose(1, 0, 3, 2, 4)
    k_pos = jnp.arange(S)

    def one_block(args):
        q_blk, blk = args
        s = jnp.einsum('bhqd,bkhd->bhqk', q_blk, k).astype(jnp.float32) * scale
        q_pos = blk * CHUNK + jnp.arange(CHUNK)
        s = jnp.where(k_pos[None, :] <= q_pos[:, None], s, -jnp.inf)
        p = jax.nn.softmax(s, axis=-1).astype(v.dtype)
        return jnp.einsum('bhqk,bkhd->bqhd', p, v)

    out = lax.map(one_block, (qb, jnp.arange(nq)))
    return out.transpose(1, 0, 2, 3, 4).reshape(Bsz, S, H, v.shape[-1])

def mla_mixer(c_q, c_kv, k_rope_raw, q_norm_g, w_qb, kv_norm_g, w_kvb, cos, sin):
    Bsz, S, _ = c_q.shape
    q = (rmsnorm_2(c_q, q_norm_g) @ w_qb).reshape(Bsz, S, MLA_HEADS, MLA_NOPE + MLA_ROPE)
    kv = (rmsnorm_2(c_kv, kv_norm_g) @ w_kvb).reshape(Bsz, S, MLA_HEADS, MLA_NOPE + MLA_V)
    q_nope, q_rope = jnp.split(q, [MLA_NOPE], axis=-1)
    k_nope, v = jnp.split(kv, [MLA_NOPE], axis=-1)
    q_rope = apply_rope(q_rope, cos, sin)
    k_rope = apply_rope(k_rope_raw[:, :, None, :], cos, sin)
    q = jnp.concatenate([q_nope, q_rope], axis=-1)
    k = jnp.concatenate([k_nope, jnp.broadcast_to(k_rope, (Bsz, S, MLA_HEADS, MLA_ROPE))], axis=-1)
    scale = 1.0 / math.sqrt(MLA_NOPE + MLA_ROPE)
    out = causal_block_attention(q, k, v, scale)
    return out.reshape(Bsz, S, MLA_W)

def squared_relu_mlp(h, w1, w2):
    return jnp.square(jax.nn.relu(h @ w1)) @ w2

def second_inputs(seed: int = 0) -> dict:
    key = jax.random.key(seed)
    ks = jax.random.split(key, 21)

    def nrm(k, shape, scale):
        return jax.random.normal(k, shape, jnp.float32) * scale

    def gain(k, shape):
        return 1.0 + 0.02 * jax.random.normal(k, shape, jnp.float32)

    dt0 = jnp.exp(jax.random.uniform(ks[8], (DEPTH, SSD_HEADS), jnp.float32,
                                     math.log(1e-3), math.log(1e-1)))
    dt_bias = dt0 + jnp.log(-jnp.expm1(-dt0))
    a_log = jnp.log(jax.random.uniform(ks[9], (DEPTH, SSD_HEADS), jnp.float32, 1.0, 16.0))
    return {
        "x": nrm(ks[0], (BATCH, SEQ, D_MODEL), 1.0),
        "norm_mix_g": gain(ks[1], (DEPTH, D_MODEL)),
        "w_in": nrm(ks[2], (DEPTH, D_MODEL, D_IN_2), D_MODEL ** -0.5),
        "gmlp_v_norm_g": gain(ks[3], (DEPTH, GMLP_W)),
        "gmlp_w_s": nrm(ks[4], (DEPTH, GMLP_HEADS, CHUNK, CHUNK), CHUNK ** -0.5),
        "gmlp_b_s": gain(ks[5], (DEPTH, GMLP_HEADS, CHUNK)),
        "ssd_conv_w": nrm(ks[6], (DEPTH, SSD_CONV, SSD_XBC), SSD_CONV ** -0.5),
        "ssd_conv_b": nrm(ks[7], (DEPTH, SSD_XBC), 0.02),
        "ssd_dt_bias": dt_bias,
        "ssd_a_log": a_log,
        "ssd_d": 1.0 + 0.1 * jax.random.normal(ks[10], (DEPTH, SSD_HEADS), jnp.float32),
        "ssd_norm_g": gain(ks[11], (DEPTH, SSD_W)),
        "mla_q_norm_g": gain(ks[12], (DEPTH, MLA_Q_RANK)),
        "mla_w_qb": nrm(ks[13], (DEPTH, MLA_Q_RANK, MLA_HEADS * (MLA_NOPE + MLA_ROPE)), MLA_Q_RANK ** -0.5),
        "mla_kv_norm_g": gain(ks[14], (DEPTH, MLA_KV_RANK)),
        "mla_w_kvb": nrm(ks[15], (DEPTH, MLA_KV_RANK, MLA_HEADS * (MLA_NOPE + MLA_V)), MLA_KV_RANK ** -0.5),
        "w_out": nrm(ks[16], (DEPTH, D_MIX, D_MODEL), D_MIX ** -0.5),
        "norm_mlp_g": gain(ks[17], (DEPTH, D_MODEL)),
        "mlp_w1": nrm(ks[18], (DEPTH, D_MODEL, D_FF_2), D_MODEL ** -0.5),
        "mlp_w2": nrm(ks[19], (DEPTH, D_FF_2, D_MODEL), D_FF_2 ** -0.5),
        "final_norm_g": gain(ks[20], (D_MODEL,)),
    }

def second_block(x, norm_mix_g, w_in, gmlp_v_norm_g, gmlp_w_s, gmlp_b_s, ssd_conv_w, ssd_conv_b,
              ssd_dt_bias, ssd_a_log, ssd_d, ssd_norm_g, mla_q_norm_g, mla_w_qb, mla_kv_norm_g,
              mla_w_kvb, w_out, norm_mlp_g, mlp_w1, mlp_w2, final_norm_g):
    S = x.shape[1]
    cos, sin = rope_tables(S)
    for l in range(DEPTH):
        h = rmsnorm_2(x, norm_mix_g[l])
        uv, z, xbc, dt_raw, c_q, c_kv, k_rope = split_cols(h @ w_in[l])
        y_a = gmlp_mixer(uv, gmlp_v_norm_g[l], gmlp_w_s[l], gmlp_b_s[l])
        y_b = ssd_mixer(z, xbc, dt_raw, ssd_conv_w[l], ssd_conv_b[l], ssd_dt_bias[l],
                        ssd_a_log[l], ssd_d[l], ssd_norm_g[l])
        y_c = mla_mixer(c_q, c_kv, k_rope, mla_q_norm_g[l], mla_w_qb[l], mla_kv_norm_g[l],
                        mla_w_kvb[l], cos, sin)
        mix = jnp.concatenate([y_a, y_b, y_c], axis=-1)
        x = x + mix @ w_out[l]
        x = x + squared_relu_mlp(rmsnorm_2(x, norm_mlp_g[l]), mlp_w1[l], mlp_w2[l])
    return rmsnorm_2(x, final_norm_g)


def setup_inputs(seed=0):
    out = dict(first_inputs(seed))
    for name, value in second_inputs(seed + 1).items():
        if name != "x":
            out[name + "_2"] = value
    return out


def reference(
    x, p, ffn1_norm, ffn1_wi, ffn1_wo, mix_norm, w_in, b_igate, b_fgate, ml_out_norm, q_norm,
    k_norm, sinks, rel_bias, w_a, w_b, w_out, ffn2_norm, ffn2_wi, ffn2_wo, ple_norm, w_ple_gate,
    w_ple, norm_mix_g_2, w_in_2, gmlp_v_norm_g_2, gmlp_w_s_2, gmlp_b_s_2, ssd_conv_w_2,
    ssd_conv_b_2, ssd_dt_bias_2, ssd_a_log_2, ssd_d_2, ssd_norm_g_2, mla_q_norm_g_2, mla_w_qb_2,
    mla_kv_norm_g_2, mla_w_kvb_2, w_out_2, norm_mlp_g_2, mlp_w1_2, mlp_w2_2, final_norm_g_2,
):
    x = first_block(
        x, p, ffn1_norm, ffn1_wi, ffn1_wo, mix_norm, w_in, b_igate, b_fgate, ml_out_norm,
        q_norm, k_norm, sinks, rel_bias, w_a, w_b, w_out, ffn2_norm, ffn2_wi, ffn2_wo, ple_norm,
        w_ple_gate, w_ple,
    )
    return second_block(
        x, norm_mix_g_2, w_in_2, gmlp_v_norm_g_2, gmlp_w_s_2, gmlp_b_s_2, ssd_conv_w_2,
        ssd_conv_b_2, ssd_dt_bias_2, ssd_a_log_2, ssd_d_2, ssd_norm_g_2, mla_q_norm_g_2,
        mla_w_qb_2, mla_kv_norm_g_2, mla_w_kvb_2, w_out_2, norm_mlp_g_2, mlp_w1_2, mlp_w2_2,
        final_norm_g_2,
    )


_drawn_inputs = setup_inputs


def setup_inputs(seed=0):
    import zlib

    import numpy as np

    out = dict(_drawn_inputs(seed))
    spreads = {}
    factors = {'b_igate': 64.0,
     'q_norm': 6.9,
     'k_norm': 5.016,
     'sinks': 8.0,
     'ple_norm': 3.348,
     'norm_mix_g_2': 3.145,
     'gmlp_v_norm_g_2': 8.0,
     'gmlp_b_s_2': 8.0,
     'ssd_conv_b_2': 3.773,
     'ssd_norm_g_2': 18.49,
     'mla_q_norm_g_2': 8.0,
     'mla_kv_norm_g_2': 8.0,
     'norm_mlp_g_2': 2.956,
     'final_norm_g_2': 7.833,
     'ssd_d_2': 8.0}
    for name, (base, spread) in spreads.items():
        noise = np.random.default_rng([zlib.crc32(name.encode()), seed]).standard_normal(out[name].shape)
        drawn = base * np.exp(spread * noise) if base else spread * noise
        out[name] = __import__('jax').numpy.asarray(drawn.astype(out[name].dtype))
    for name, factor in factors.items():
        out[name] = (out[name] * factor).astype(out[name].dtype)
    return out
```

```python
from contextlib import ExitStack

import concourse.bass as bass
from concourse import mybir

F32 = mybir.dt.float32
F32R = mybir.dt.float32r
ALU = mybir.AluOpType
ACT = mybir.ActivationFunctionType
AX = mybir.AxisListType

P = 128
S = 512
D = 1024
KT = D // P
NT = S // P
EPS = 1e-6
NEG = -1e30

D_FF = 2816
FT = D_FF // P
ML_H = 4
SW_H = 8
SW_KV = 2
SW_G = SW_H // SW_KV
GATE_COL = 1536
SQ_COL = 1544
SK_COL = 2056
SV_COL = 2184
GA_COL = 2312
GB_COL = 3336
FT2 = 4 * D // P
HALF2 = FT2 // 2
SSD_H = 6
MLA_H = 6
MLA_D = 96
DT_COL = 1536
CQ_COL = 1542
KR_COL = 2182
MLA_SCALE = 1.0 / float(MLA_D) ** 0.5

RAW_SLOTS = 2
SPLIT_SLOTS = 4
TILE_BANKS = 4
AHEAD = SPLIT_SLOTS - 1
SLAB = 1024

B1_SLABS, B1_TILES = 192, 180
B2_SLABS, B2_TILES = 96, 88
S_FFN1, S_IN, S_GATED, S_OUT, S_FFN2, S_PLE = 0, 66, 84, 108, 116, 182
T_FFN1, T_IN, T_GATED, T_OUT, T_FFN2, T_PLE = 0, 52, 70, 102, 110, 162
S2_IN, S2_QB, S2_KVB, S2_OUT, S2_MLP = 0, 18, 21, 24, 32
T2_IN, T2_QB, T2_KVB, T2_OUT, T2_MLP = 0, 18, 24, 30, 38

R_FFN1, R_MIX, R_FFN2, R_PLE, R_MLOUT, R_QN, R_KN, R1 = 0, 8, 16, 24, 32, 36, 37, 38
Q_MIX, Q_MLP, Q_CQ, Q_CKV, Q_SSD, Q_GV, Q_CB, Q_CW, R2 = 0, 8, 16, 19, 21, 24, 26, 31, 51

C_IDENT, C_BD64, C_DUP0, C_DUP1, C_MQS, C_MSQ, C_ROT, C_TRI = [P * n for n in range(8)]

TOEP = 384


class Block1:
    base_slab, slabs, base_tile, tiles = 0, B1_SLABS, 0, B1_TILES
    norms, base_norm = 4, 0


class Block2:
    base_slab, slabs = 2 * B1_SLABS, B2_SLABS
    base_tile, tiles = 2 * B1_TILES, B2_TILES
    norms, base_norm = 2, 8


def at(layer, per_layer, const, i=None, step=0):
    e = const if layer is None else layer * per_layer + const
    return e if i is None else e + i * step


def program(nc, a):
    ctx = ExitStack()
    with ctx:
        cursor = [16512]

        def place(name, shape, dt=F32, offset=None):
            size = 4
            for n in shape[1:]:
                size *= n
            if offset is None:
                offset = cursor[0]
                cursor[0] += (size + 31) // 32 * 32
            return nc.alloc_sbuf_tensor_at(name, shape, dt, offset=offset)

        def sem(name):
            return ctx.enter_context(nc.semaphore(name))

        x_sb = place("x_sb", [P, KT, S])
        xh = place("xh", [P, KT, S], F32R)
        xl = place("xl", [P, KT, S], F32R)
        raw = [place(f"raw{n}", [P, SLAB]) for n in range(RAW_SLOTS)]
        wh = [place(f"wh{n}", [P, SLAB], F32R) for n in range(SPLIT_SLOTS)]
        wl = [place(f"wl{n}", [P, SLAB], F32R) for n in range(SPLIT_SLOTS)]
        tmp = [place(f"tmp{n}", [P, S]) for n in range(4)]
        rstd = place("rstd", [P, S])
        acc = place("acc", [P, S])
        var = place("var", [P, S])
        const = place("const", [P, 8 * P])
        ones = place("ones", [P, P])
        p1 = place("p1", [P, 2 * R1])
        p2 = place("p2", [P, 2 * R2 + KT])
        par1 = place("par1", [P, R1])
        par2 = place("par2", [P, R2])
        gate_raw = place("gate_raw", [P, KT, 8])
        gate_h = place("gate_h", [P, KT, 8], F32R)
        gate_l = place("gate_l", [P, KT, 8], F32R)
        b_gate = place("b_gate", [ML_H, 2, 2])
        b_gate_now = place("b_gate_now", [ML_H, 2])
        sinks = place("sinks", [P, 2, SW_H])
        sinks_now = place("sinks_now", [P, SW_H])
        c_col = place("c_col", [P, NT, ML_H])
        small = place("small", [P, 64])
        d_skip = place("d_skip", [P, 2, 3])
        d_skip_now = place("d_skip_now", [P, 3])
        dt_bias = place("dt_bias", [SSD_H, 2])
        dt_a = place("dt_a", [SSD_H, 2])
        dt_now = place("dt_now", [SSD_H, 2])
        bs_rows = place("bs_rows", [4, 2, P])
        bs_now = place("bs_now", [4, P])
        a_col = place("a_col", [P, NT, SSD_H])
        dt_col = place("dt_col", [P, NT, SSD_H])
        bias_at = cursor[0]
        bias = place("bias", [P, SW_H, 2 * P])
        rope = place("rope", [MLA_D, 2, S], offset=bias_at)
        region = cursor[0]

        def at_kb(name, kb, shape, dt=F32):
            return place(name, shape, dt, offset=region + int(kb * 1024))

        hh = at_kb("hh", 0, [P, FT, S], F32R)
        hl = at_kb("hl", 44, [P, FT, S], F32R)
        squares = at_kb("squares", 0, [P, KT, S])
        x_tok = at_kb("x_tok", 0, [P, NT, D])
        rows1 = at_kb("rows1", 16, [2 * R1, P])
        rows2 = at_kb("rows2", 17, [2 * R2 + KT, P])
        onehot = at_kb("onehot", 18, [32, TOEP])
        pad = at_kb("pad", 20, [P, TOEP])
        rel = at_kb("rel", 22, [32, SW_H])
        toep = at_kb("toep", 24, [P, SW_H, TOEP])
        proj = at_kb("proj", 0, [P, 18, S])
        hah = at_kb("hah", 0, [P, ML_H, S], F32R)
        hal = at_kb("hal", 8, [P, ML_H, S], F32R)
        hbh = at_kb("hbh", 16, [P, 4, S], F32R)
        mv_tok = at_kb("mv_tok", 36, [P, NT, S])
        sv_tok = at_kb("sv_tok", 44, [P, NT, P])
        kk = at_kb("kk", 46, [P, SW_KV, S])
        num_sb = at_kb("num_sb", 50, [P, ML_H, S])
        hbl = at_kb("hbl", 50, [P, 4, S], F32R)
        ml_w = at_kb("ml_w", 58, [P, 1280])
        ml_p = at_kb("ml_p", 63, [P, 1280])
        inv = at_kb("inv", 68, [P, ML_H, S])
        neg_m = at_kb("neg_m", 76, [P, S])
        neg_md = at_kb("neg_md", 78, [P, S])
        emt_bc = at_kb("emt_bc", 80, [P, S])
        abs_den = at_kb("abs_den", 82, [P, S])
        ml_rows = [at_kb(f"ml_row{n}", 68 + 2 * n, [ML_H, S]) for n in range(4)]
        ml_rows += [at_kb(f"ml_row{4 + n}", 58 + 2 * n, [ML_H, S]) for n in range(5)]
        qk_sq = at_kb("qk_sq", 58, [P, 5, S])
        lg = at_kb("lg", 68, [P, 2, SW_G, 2 * P])
        pt_sb = at_kb("pt_sb", 76, [P, 2, SW_G, P])
        mh = at_kb("mh", 24, [P, KT, S], F32R)
        ml = at_kb("ml", 58, [P, KT, S], F32R)
        gate_sg = at_kb("gate_sg", 0, [P, KT, S])
        p_tok = at_kb("p_tok", 16, [P, NT, 2 * P])
        pth = at_kb("pth", 20, [P, 2, S], F32R)
        ptl = at_kb("ptl", 24, [P, 2, S], F32R)
        proj2 = at_kb("proj2", 0, [P, 18, S])
        q96 = at_kb("q96", 0, [MLA_D, MLA_H, S])
        k96 = at_kb("k96", 12, [MLA_D, MLA_H, S])
        conv = at_kb("conv", 36, [P, 5, S])
        xs_tok = at_kb("xs_tok", 46, [P, NT, 384])
        v_tok = at_kb("v_tok", 46, [P, NT, 384])
        cqh = at_kb("cqh", 52, [P, 3, S], F32R)
        cql = at_kb("cql", 58, [P, 3, S], F32R)
        ckh = at_kb("ckh", 64, [P, 2, S], F32R)
        ckl = at_kb("ckl", 68, [P, 2, S], F32R)
        gv_sq = at_kb("gv_sq", 72, [P, 2, S])
        gv_tok = at_kb("gv_tok", 76, [P, NT, 2 * P])
        ws_t = at_kb("ws_t", 80, [P, 4, P])
        ws_raw = at_kb("ws_raw", 82, [P, 4, P])
        cb = at_kb("cb", 72, [P, 1280])
        sd_w = at_kb("sd_w", 77, [P, 1280])
        sd_p = at_kb("sd_p", 82, [P, 1280])
        y_sq = at_kb("y_sq", 77, [P, 3, S])
        c_sq = at_kb("c_sq", 72, [P, 5, S])
        k_rot = at_kb("k_rot", 36, [P, S])
        rot_sin = at_kb("rot_sin", 38, [P, S])
        v_ft = at_kb("v_ft", 40, [P, 2, S])
        prob = at_kb("prob", 72, [P, 2, S])
        prob_t = at_kb("prob_t", 76, [P, NT, S])
        y_sb = at_kb("y_sb", 16, [P, KT, S])
        out_tok = at_kb("out_tok", 32, [P, NT, D])
        assert region + 88 * 1024 <= nc.sbuf_usable_end, (region + 88 * 1024, nc.sbuf_usable_end)

        ident = const[:, C_IDENT:C_IDENT + P]
        bd64 = const[:, C_BD64:C_BD64 + P]
        dup = [const[:, c:c + P] for c in (C_DUP0, C_DUP1)]
        mask_qs = const[:, C_MQS:C_MQS + P]
        mask_sq = const[:, C_MSQ:C_MSQ + P]
        rot96 = const[0:MLA_D, C_ROT:C_ROT + MLA_D]
        tri_st = const[:, C_TRI:C_TRI + P]

        bank = [ctx.enter_context(nc.psum_tensor(f"bank{n}", [P, S], F32)) for n in range(4)]
        mb = ctx.enter_context(nc.psum_tensor("mb", [P, 4, S], F32))
        B4, B5, B6, B7 = (mb[:, n, :] for n in range(4))

        scratch = nc.dram_tensor("toeplitz_rows", [SW_H, P, TOEP], F32, kind="Internal").ap()

        names = """split_done slab_used hi_ready tile_ready tile_evacuated setup_x setup_const setup_small
            setup_t setup_copied rel_psum toep_row toep_out toep_in consts_ready
            x_final sq_ready ss_ready ss_psum inv_var rstd_ready xl_ready
            silu_done hidden_ready gate_landed gate_split gates_psum gate_pre log1p ml_rows_done emt_done
            v_turned v_copied c_turned c_copied bc_ready bc_copied w_ready sc_ready p_ready pv_done abs_done
            head_done num_sq ml_ss ml_ss_read ml_inv ml_rs mo_done ha_ready
            qk_squared qk_ss qk_ss_read qk_inv qk_rs qk_normed kk_psum kk_copied
            lg_ready lg_read mx_ready ex_ready pn_ready pt_ready pt_copied o_ready o_done
            sig_done mixed_ready p_landed p_turned pt_split sg_done kr_landed
            gelu_done gv_squared gv_ss gv_inv gv_rs gv_normed gv_turned gv_copied ws_landed ws_turned ws_copied
            gm_psum gm_done conv_done conv_silu z_silu xs_turned xs_copied
            dt_pre dt_log dt_rows_done dcol_turned dcol_copied cb_ready cb_copied abc_ready abc_copied sw_ready
            sp_ready y_psum y_done y_squared y_ss y_ss_read y_inv y_rs ssd_done
            c_squared c_ss c_inv c_rs c_split rope_landed rot_psum rot_read rot_done
            kv_done vt_psum vt_copied al_ready am_ready ae_ready ap_ready at_ready at_copied ao_ready ao_done
            fin_y fin_turned fin_copied stored""".split()
        sm = {n: sem(n) for n in names}
        raw_landed = [sem(f"raw_landed{n}") for n in range(RAW_SLOTS)]
        s = type("Sems", (), sm)

        def tiles_out(B, L, t, i=None, step=0):
            return at(L, B.tiles, B.base_tile + t + 1 + TILE_BANKS, i, step)

        def tiles_in(B, L, t, i=None, step=0):
            return at(L, B.tiles, B.base_tile + t + 1, i, step)

        def norm_no(B, L, k):
            return at(L, B.norms, B.base_norm + k + 1)

        block = ctx.enter_context(nc.Block())

        @block.sync
        def _(sp):
            def load(B, L, n, view, src, i=None, step=0):
                need = sp.lower_val(at(L, B.slabs, B.base_slab + n + 1, i, step))
                sp.dma_start(view(raw[n % RAW_SLOTS]), src).wait_op(s.split_done, need, "sem-ge")\
                  .then_inc(raw_landed[n % RAW_SLOTS], 16)

            def as3(kt, c):
                return lambda r: r[:, 0:kt * c].rearrange("p (k c) -> p k c", k=kt)

            def cols(w, L, c0, width, i=None, step=0):
                c = c0 if i is None else i * step + c0
                sl = slice(c0, c0 + width) if i is None else bass.ds(c, width)
                return w[bass.ds(L, 1), :, sl].rearrange("l (k p) c -> p (l k) c", p=P)

            def rows2c(w, L, r0, c0, i=None, step=0):
                sl = slice(r0, r0 + 2 * P) if i is None else bass.ds(i * step + r0, 2 * P)
                return w[bass.ds(L, 1), sl, c0:c0 + S].rearrange("l (k p) c -> p (l k) c", p=P)

            sp.dma_start(const[:], a["const_pack"]).then_inc(s.setup_const, 16)
            sp.dma_start(x_tok[:], a["x"].rearrange("b (t p) d -> p (b t) d", p=P)).then_inc(s.setup_x, 16)

            def row(dst, r0, n, src):
                sp.dma_start(dst[r0:r0 + n, :], src.rearrange("(r c) -> r c", c=P)).then_inc(s.setup_small, 16)

            for l in range(2):
                for r0, n, name in ((R_FFN1, 8, "ffn1_norm"), (R_MIX, 8, "mix_norm"), (R_FFN2, 8, "ffn2_norm"),
                                    (R_PLE, 8, "ple_norm")):
                    row(rows1, l * R1 + r0, n, a[name][l])
                sp.dma_start(rows1[l * R1 + R_MLOUT:l * R1 + R_MLOUT + ML_H, :], a["ml_out_norm"][l])\
                  .then_inc(s.setup_small, 16)
                for r0, name in ((R_QN, "q_norm"), (R_KN, "k_norm")):
                    for half in range(2):
                        sp.dma_start(rows1[l * R1 + r0:l * R1 + r0 + 1, half * 64:half * 64 + 64],
                                     a[name][l:l + 1]).then_inc(s.setup_small, 16)
                for r0, n, name in ((Q_MIX, 8, "norm_mix_g_2"), (Q_MLP, 8, "norm_mlp_g_2"), (Q_CQ, 3, "mla_q_norm_g_2"),
                                    (Q_CKV, 2, "mla_kv_norm_g_2"), (Q_SSD, 3, "ssd_norm_g_2"),
                                    (Q_GV, 2, "gmlp_v_norm_g_2"), (Q_CB, 5, "ssd_conv_b_2")):
                    row(rows2, l * R2 + r0, n, a[name][l])
                for k in range(4):
                    row(rows2, l * R2 + Q_CW + 5 * k, 5, a["ssd_conv_w_2"][l, k])
            row(rows2, 2 * R2, KT, a["final_norm_g_2"])
            with nc.allow_non_contiguous_dma("parameters of a few bytes"):
                sp.dma_start(b_gate[:, :, 0:1], a["b_igate"].rearrange("l (h o) -> h l o", o=1)).then_inc(s.setup_small, 16)
                sp.dma_start(b_gate[:, :, 1:2], a["b_fgate"].rearrange("l (h o) -> h l o", o=1)).then_inc(s.setup_small, 16)
                sp.dma_start(dt_bias[:, :, None], a["ssd_dt_bias_2"].rearrange("l (h o) -> h l o", o=1))\
                  .then_inc(s.setup_small, 16)
                sp.dma_start(dt_a[:, :, None], a["ssd_a_log_2"].rearrange("l (h o) -> h l o", o=1)).then_inc(s.setup_small, 16)
                sp.dma_start(bs_rows[:], a["gmlp_b_s_2"].rearrange("l h t -> h l t")).then_inc(s.setup_small, 16)
                sp.dma_start(sinks[:].rearrange("p l h -> p (l h)"),
                             a["sinks"].rearrange("(o l) h -> o (l h)", o=1).to_broadcast([P, 2 * SW_H]))\
                  .then_inc(s.setup_small, 16)
                for half in range(2):
                    src = a["ssd_d_2"].rearrange("l (i two) -> two l i", two=2)[half:half + 1]
                    sp.dma_start(d_skip[half * 64:half * 64 + 64], src.to_broadcast([64, 2, 3])).then_inc(s.setup_small, 16)
                sp.dma_start(rel[:], a["rel_bias"]).then_inc(s.setup_small, 16)
                sp.dma_start(onehot[:], a["onehot"]).then_inc(s.setup_small, 16)
                sp.dma_start(pad[:], a["pad"]).then_inc(s.setup_small, 16)
            def ffn(L, wi, wo, n):
                with sp.Fori(0, FT // 2) as i:
                    for f in range(2):
                        for part in range(2):
                            load(Block1, L, n + 2 * f + part, as3(KT, P),
                                 cols(wi, L, part * D_FF + f * P, P, i, 2 * P), i, 4)
                for half in range(2):
                    n0 = n + 2 * FT + half * (FT // 2)
                    with sp.Fori(0, 2) as i:
                        for q in range(4):
                            load(Block1, L, n0 + q, as3(2, S), rows2c(wo, L, q * 2 * P, half * S, i, 8 * P), i, 4)
                    for q in range(8, FT // 2):
                        load(Block1, L, n0 + q, as3(2, S), rows2c(wo, L, q * 2 * P, half * S))

            with sp.Fori(0, 2) as L:
                need = sp.lower_val(L + 1)
                with nc.allow_non_contiguous_dma("eight columns"):
                    sp.dma_start(gate_raw[:], cols(a["w_in"], L, GATE_COL, 8)).wait_op(s.gate_split, need, "sem-ge")\
                      .then_inc(s.gate_landed, 16)
                ffn(L, a["ffn1_wi"], a["ffn1_wo"], S_FFN1)
                with sp.Fori(0, 3) as i:
                    for u in range(4):
                        load(Block1, L, S_IN + u, as3(KT, P), cols(a["w_in"], L, u * P, P, i, 4 * P), i, 4)
                for u in range(6):
                    load(Block1, L, S_IN + 12 + u, as3(KT, P), cols(a["w_in"], L, SQ_COL + u * P, P))
                with sp.Fori(0, 2) as i:
                    for jj in range(2):
                        n = S_GATED + 6 * jj
                        for k in range(2):
                            load(Block1, L, n + k, as3(KT, P),
                                 cols(a["w_in"], L, GA_COL + (2 * jj + k) * P, P, i, 4 * P), i, 12)
                        for k in range(2):
                            load(Block1, L, n + 2 + k, as3(KT, P),
                                 cols(a["w_in"], L, GB_COL + (2 * jj + k) * P, P, i, 4 * P), i, 12)
                        load(Block1, L, n + 4, as3(4, 2 * P), cols(a["w_a"], L, jj * 2 * P, 2 * P, i, 4 * P), i, 12)
                        load(Block1, L, n + 5, as3(4, 2 * P), cols(a["w_b"], L, jj * 2 * P, 2 * P, i, 4 * P), i, 12)
                with sp.Fori(0, 2) as i:
                    for j in range(4):
                        load(Block1, L, S_OUT + j, as3(KT, P), cols(a["w_out"], L, j * P, P, i, 4 * P), i, 4)
                ffn(L, a["ffn2_wi"], a["ffn2_wo"], S_FFN2)
                with sp.Fori(0, 2) as i:
                    for j in range(4):
                        load(Block1, L, S_PLE + j, as3(KT, P), cols(a["w_ple_gate"], L, j * P, P, i, 4 * P), i, 4)
                for d in range(2):
                    load(Block1, L, S_PLE + 8 + d, as3(2, S), cols(a["w_ple"], L, d * S, S))
                need = sp.lower_val(tiles_out(Block1, L, T_FFN2 + 51))
                sp.dma_start(p_tok[:], a["p"][bass.ds(L, 1), 0].rearrange("l (t p) c -> p (l t) c", p=P))\
                  .wait_op(s.tile_evacuated, need, "sem-ge").then_inc(s.p_landed, 16)

            sp.wait_ge(s.lg_read, 16)
            sp.dma_start(rope[:], a["rope_pack"]).then_inc(s.rope_landed, 16)
            with sp.Fori(0, 2) as L:
                B = Block2
                w_in = a["w_in_2"]
                with sp.Fori(0, 3) as i:
                    for u in range(4):
                        load(B, L, S2_IN + u, as3(KT, P), cols(w_in, L, u * P, P, i, 4 * P), i, 4)
                need = sp.lower_val(at(L, B.tiles, B.base_tile + TILE_BANKS))
                sp.dma_start(ws_raw[:], a["gmlp_w_s_2"][bass.ds(L, 1)].rearrange("l h t s -> t (l h) s"))\
                  .wait_op(s.tile_evacuated, need, "sem-ge").then_inc(s.ws_landed, 16)
                view = lambda c0, c1: (lambda r: r[:, 0:KT * MLA_D].rearrange("p (k c) -> p k c", k=KT)[:, :, c0:c1])
                with nc.allow_non_contiguous_dma("six columns"):
                    load(B, L, S2_IN + 12, view(0, SSD_H), cols(w_in, L, DT_COL, SSD_H))
                    sp.dma_start(view(64, MLA_D)(raw[(S2_IN + 12) % RAW_SLOTS]), cols(w_in, L, KR_COL, 32))\
                      .then_inc(s.kr_landed, 16)
                for u in range(5):
                    load(B, L, S2_IN + 13 + u, as3(KT, P), cols(w_in, L, CQ_COL + u * P, P))
                for u in range(3):
                    load(B, L, S2_QB + u, as3(3, 2 * MLA_D), cols(a["mla_w_qb_2"], L, u * 2 * MLA_D, 2 * MLA_D))
                for u in range(3):
                    load(B, L, S2_KVB + u, as3(2, 2 * P), cols(a["mla_w_kvb_2"], L, u * 2 * P, 2 * P))
                with sp.Fori(0, 2) as i:
                    for j in range(4):
                        load(B, L, S2_OUT + j, as3(KT, P), cols(a["w_out_2"], L, j * P, P, i, 4 * P), i, 4)
                for half in range(2):
                    n0 = S2_MLP + half * 2 * HALF2
                    with sp.Fori(0, HALF2 // 4) as i:
                        for f in range(4):
                            load(B, L, n0 + f, as3(KT, P),
                                 cols(a["mlp_w1_2"], L, (half * HALF2 + f) * P, P, i, 4 * P), i, 4)
                    for dh in range(2):
                        with sp.Fori(0, 2) as i:
                            for q in range(4):
                                load(B, L, n0 + HALF2 + 8 * dh + q, as3(2, S),
                                     rows2c(a["mlp_w2_2"], L, half * HALF2 * P + q * 2 * P, dh * S, i, 8 * P), i, 4)

            for t in range(NT):
                sp.wait_ge(s.fin_copied, 2 * t + 2)
                sp.dma_start(a["out"][0, t * P:(t + 1) * P, :], out_tok[:, t, :]).then_inc(s.stored, 16)
            sp.wait_ge(s.stored, 16 * NT)

        @block.gpsimd
        def _(gp):
            gp.memset(ones[:], 1.0).then_inc(s.consts_ready, 1)
            gp.sem_inc(s.split_done, RAW_SLOTS)
            gp.sem_inc(s.slab_used, AHEAD)
            gp.sem_inc(s.tile_evacuated, TILE_BANKS)
            gp.sem_inc(s.gate_split, 1)
            total = 2 * (B1_SLABS + B2_SLABS)
            with gp.Fori(0, total // SPLIT_SLOTS) as n:
                for j in range(SPLIT_SLOTS):
                    gp.wait_ge(s.hi_ready, n * SPLIT_SLOTS + j + 1)
                    gp.tensor_tensor(wl[j][:], raw[j % RAW_SLOTS][:], wh[j][:].bitcast(F32), ALU.subtract)\
                      .then_inc(s.split_done, 1)

        @block.tensor
        def _(pe):
            def take_slab(B, L, n, i=None, step=0):
                pe.wait_ge(s.split_done, at(L, B.slabs, B.base_slab + n + 1 + RAW_SLOTS, i, step))
                return wh[n % SPLIT_SLOTS], wl[n % SPLIT_SLOTS]

            def open_tile(B, L, t, i=None, step=0):
                pe.wait_ge(s.tile_evacuated, at(L, B.tiles, B.base_tile + t + 1, i, step))
                return bank[(B.base_tile + t) % TILE_BANKS]

            def three(out, ah, al, bh, bl, first, last, new=False):
                one = pe.matmul(out, ah, bh, start=first, stop=False)
                if new:
                    one.then_inc(s.slab_used, 1)
                pe.matmul(out, ah, bl, start=False, stop=False)
                return pe.matmul(out, al, bh, start=False, stop=last)

            def unit(B, L, n, t, rh, rl, i=None, step=0, tstep=None, wait_k=None, width=P, kts=KT, c0=0, pitch=P,
                     new=True, done=True, inc=1):
                tstep = step if tstep is None else tstep
                if new:
                    take_slab(B, L, n, i, step)
                out = open_tile(B, L, t, i, tstep)
                h, l = wh[n % SPLIT_SLOTS], wl[n % SPLIT_SLOTS]
                for k in range(kts):
                    if wait_k is not None:
                        pe.wait_ge(s.xl_ready, wait_k(k))
                    c = k * pitch + c0
                    first = pe.matmul(out[0:width, :], h[:, c:c + width], rh[:, k, :], start=k == 0, stop=False)
                    if new and k == 0:
                        first.then_inc(s.slab_used, 1)
                    pe.matmul(out[0:width, :], h[:, c:c + width], rl[:, k, :], start=False, stop=False)
                    if k < kts - 1:
                        pe.matmul(out[0:width, :], l[:, c:c + width], rh[:, k, :], start=False, stop=False)
                last = pe.matmul(out[0:width, :], l[:, c:c + width], rh[:, kts - 1, :], start=False, stop=True)
                last.then_inc(s.tile_ready, inc)
                return last

            def xl_wait(B, L, k):
                base = B.base_norm * KT
                return lambda kt: at(L, B.norms * KT, base + k * KT + kt + 1)

            def sum_squares(B, L, k):
                pe.wait_ge(s.ss_ready, norm_no(B, L, k))
                pe.matmul(B4, ones[:], acc[:], start=True, stop=True).then_inc(s.ss_psum, 1)

            def turn(out, in_, k=P):
                if k == P:
                    return pe.transpose(out, in_, ident)
                return pe.matmul(out, in_, const[0:k, C_IDENT:C_IDENT + k], start=True, stop=True)

            pe.wait_ge(s.setup_const, 16)
            pe.wait_ge(s.consts_ready, 1)
            pe.wait_ge(s.setup_x, 16)
            for j in range(KT):
                if j >= 4:
                    pe.wait_ge(s.setup_copied, j - 3)
                for t in range(NT):
                    last = turn(mb[:, j % 4, t * P:(t + 1) * P], x_tok[:, t, j * P:(j + 1) * P])
                last.then_inc(s.setup_t, 1)
            pe.wait_ge(s.setup_small, 16 * N_SMALL)
            pe.wait_ge(s.setup_copied, 6)
            turn(B4[:, 0:2 * R1], rows1[:], 2 * R1)
            turn(B5[:, 0:2 * R2 + KT], rows2[:], 2 * R2 + KT).then_inc(s.setup_t, 1)
            pe.wait_ge(s.setup_copied, 8)
            for h in range(SW_H):
                if h >= 2:
                    pe.wait_ge(s.toep_row, h - 1)
                pe.matmul(mb[:, 2 + h % 2, 0:TOEP], rel[:, h:h + 1].to_broadcast([32, P]), onehot[:],
                          start=True, stop=True).then_inc(s.rel_psum, 1)

            def ffn(L, k, n, t, wh_count):
                w = xl_wait(Block1, L, k)
                for u in range(4):
                    unit(Block1, L, n + u, t + u, xh, xl, wait_k=w if u == 0 else None)
                    if u == 1:
                        sum_squares(Block1, L, k)
                with pe.Fori(1, FT // 2) as i:
                    for u in range(4):
                        unit(Block1, L, n + u, t + u, xh, xl, i, 4)
                for half in range(2):
                    n0, t0 = n + 2 * FT + half * (FT // 2), t + 2 * FT + 4 * half

                    def down(q, i=None):
                        take_slab(Block1, L, n0 + q, i, 4)
                        h, l = wh[(n0 + q) % SPLIT_SLOTS], wl[(n0 + q) % SPLIT_SLOTS]
                        if half == 0:
                            pe.wait_ge(s.hidden_ready, at(L, 2 * FT, wh_count + 2 * q + 2, i, 8))
                        for kk_ in range(2):
                            kt = 2 * q + kk_ if i is None else i * 8 + (2 * q + kk_)
                            first, end = i is None and q == 0 and kk_ == 0, q == FT // 2 - 1 and kk_ == 1
                            for d in range(4):
                                if first:
                                    open_tile(Block1, L, t0 + d)
                                out = bank[(t0 + d) % TILE_BANKS][:]
                                c = kk_ * S + d * P
                                last = three(out, h[:, c:c + P], l[:, c:c + P], hh[:, kt, :], hl[:, kt, :], first, end,
                                             new=kk_ == 0 and d == 0)
                                if end:
                                    last.then_inc(s.tile_ready, 1)

                    down(0)
                    with pe.Fori(0, 2) as i:
                        for q in range(1, 5):
                            down(q, i)
                    for q in range(9, FT // 2):
                        down(q)

            def mlstm(L):
                pe.wait_ge(s.gate_split, at(L, 1, 2))
                pe.wait_ge(s.inv_var, norm_no(Block1, L, 1))
                for g, out in ((0, B4), (1, B5)):
                    for k in range(KT):
                        last = three(out[0:ML_H, :], gate_h[:, k, 4 * g:4 * g + 4], gate_l[:, k, 4 * g:4 * g + 4],
                                     xh[:, k, :], xl[:, k, :], k == 0, k == KT - 1)
                last.then_inc(s.gates_psum, 1)
                pe.wait_ge(s.tile_evacuated, tiles_out(Block1, L, T_IN + 17))
                for t in range(NT + 1):
                    if t >= 2:
                        pe.wait_ge(s.v_copied, at(L, 5, t - 1))
                    for j in range(4):
                        src = proj[:, 4 + j, t * P:(t + 1) * P] if t < NT else proj[:, 17, j * P:(j + 1) * P]
                        last = turn(mb[:, 2 + t % 2, j * P:(j + 1) * P], src)
                    last.then_inc(s.v_turned, 1)
                pe.wait_ge(s.ml_rows_done, at(L, 1, 1))
                for t in range(NT):
                    last = turn(B5[:, ML_H * t:ML_H * t + ML_H], ml_rows[5][:, t * P:(t + 1) * P], ML_H)
                last.then_inc(s.c_turned, 1)
                pe.wait_ge(s.emt_done, at(L, 1, 1))
                for h in range(ML_H):
                    tile, half = h // 2, 64 * (h % 2)
                    for k, src in ((0, acc), (1, var)):
                        if h or k:
                            pe.wait_ge(s.bc_copied, at(L, 2 * ML_H, 2 * h + k))
                        pe.matmul(B4, const[0:ML_H, C_IDENT + h:C_IDENT + h + 1].to_broadcast([ML_H, P]),
                                  src[0:ML_H, :], start=True, stop=True).then_inc(s.bc_ready, 1)

                    def scores(j):
                        if h or j:
                            pe.wait_ge(s.p_ready, at(L, 16, 4 * h + j))
                        else:
                            pe.wait_ge(s.c_copied, at(L, 1, 1))
                        pe.matmul(B5[:, 0:S - j * P], proj[half:half + 64, 2 + tile, j * P:(j + 1) * P],
                                  proj[half:half + 64, tile, j * P:S], start=True, stop=True).then_inc(s.sc_ready, 1)

                    def values(j):
                        if j == 0 and h:
                            pe.wait_ge(s.head_done, at(L, ML_H, h))
                        if j == 0 and not h:
                            pe.wait_ge(s.v_copied, at(L, 5, 5))
                        pe.wait_ge(s.p_ready, at(L, 16, 4 * h + j + 1))
                        o = ML_OFF[j]
                        pj = ml_p[:, o:o + S - j * P]
                        pe.matmul(B6[:, j * P:S], mv_tok[:, j, h * P:(h + 1) * P], pj, start=j == 0, stop=j == 3)
                        pe.matmul(B7[:, j * P:S], ones[:], pj, start=j == 0, stop=j == 3).then_inc(s.pv_done, 1)

                    scores(0)
                    for j in range(1, 4):
                        scores(j)
                        values(j - 1)
                    values(3)
                pe.wait_ge(s.num_sq, at(L, 1, 1))
                for h in range(ML_H):
                    if h >= 2:
                        pe.wait_ge(s.ml_ss_read, at(L, ML_H, h - 1))
                    pe.matmul(mb[:, h % 2, :], ones[:], inv[:, h, :], start=True, stop=True).then_inc(s.ml_ss, 1)

            def swa(L):
                pe.wait_ge(s.qk_squared, at(L, 1, 1))
                pe.wait_ge(s.ml_ss_read, at(L, ML_H, ML_H))
                for u in range(5):
                    if u >= 2:
                        pe.wait_ge(s.qk_ss_read, at(L, 5, u - 1))
                    pe.matmul(mb[:, u % 2, :], bd64, qk_sq[:, u, :], start=True, stop=True).then_inc(s.qk_ss, 1)
                pe.wait_ge(s.qk_normed, at(L, 1, 1))
                for g in range(SW_KV):
                    last = pe.matmul(mb[:, 2 + g, :], dup[g], proj[:, 16, :], start=True, stop=True)
                last.then_inc(s.kk_psum, 1)
                pe.wait_ge(s.kk_copied, at(L, 1, 1))

                def logits(b):
                    n, g = b // SW_KV, b % SW_KV
                    if b:
                        pe.wait_ge(s.lg_read, at(L, 8, b))
                    lo = 0 if n else P
                    for i in range(SW_G):
                        h = g * SW_G + i
                        half = 64 * (h % 2)
                        out = mb[:, i % 2, (i // 2) * 2 * P + lo:(i // 2) * 2 * P + 2 * P]
                        last = pe.matmul(out, proj[half:half + 64, 12 + h // 2, n * P:(n + 1) * P],
                                         kk[half:half + 64, g, (n - 1) * P + lo:(n + 1) * P], start=True, stop=True)
                    last.then_inc(s.lg_ready, 1)

                logits(0)
                for b in range(8):
                    n, g = b // SW_KV, b % SW_KV
                    if b < 7:
                        logits(b + 1)
                    sides = (0, 1) if n else (1,)
                    pe.wait_ge(s.pn_ready, at(L, 8, b + 1))
                    if b:
                        pe.wait_ge(s.o_done, at(L, 8, b))
                    for side in sides:
                        for i in range(SW_G):
                            last = turn(mb[:, 2 + side, i * P:(i + 1) * P], lg[:, b % 2, i, side * P:(side + 1) * P])
                    last.then_inc(s.pt_ready, 1)
                    pe.wait_ge(s.pt_copied, at(L, 8, b + 1))
                    for par in range(2):
                        for side in sides:
                            rhs = pt_sb[:, side].rearrange("p (i two) q -> p two i q", two=2)[:, par]
                            last = pe.matmul(B6[64 * par:64 * par + 64, 0:2 * P].rearrange("p (i q) -> p i q", i=2),
                                             sv_tok[:, n - 1 + side, g * 64:g * 64 + 64], rhs,
                                             start=side == sides[0], stop=side == 1)
                    last.then_inc(s.o_ready, 1)

            def gated(L):
                with pe.Fori(0, 2) as i:
                    for jj in range(2):
                        n, t = S_GATED + 6 * jj, T_GATED + 8 * jj
                        for u in range(4):
                            unit(Block1, L, n + u, t + u, xh, xl, i, 12, 16)
                        for b, (h_, l_, ready, count) in enumerate(((hah, hal, s.ha_ready, at(L, 1, 1)),
                                                                    (hbh, hbl, s.o_done, at(L, 8, 8)))):
                            pe.wait_ge(ready, count)
                            for d in range(2):
                                unit(Block1, L, n + 4 + b, t + 4 + 2 * b + d, h_, l_, i, 12, 16, kts=4, c0=d * P,
                                     pitch=2 * P, new=d == 0)
                for j in range(KT):
                    if j == 0:
                        pe.wait_ge(s.mixed_ready, at(L, KT, KT))
                    unit(Block1, L, S_OUT + j, T_OUT + j, mh, ml)

            def ple(L):
                w = xl_wait(Block1, L, 3)
                for j in range(KT):
                    unit(Block1, L, S_PLE + j, T_PLE + j, xh, xl, wait_k=w if j == 0 else None)
                    if j == 1:
                        sum_squares(Block1, L, 3)
                pe.wait_ge(s.p_landed, at(L, 16, 16))
                pe.wait_ge(s.inv_var, norm_no(Block1, L, 3))
                for k in range(2):
                    for t in range(NT):
                        last = turn(mb[:, k, t * P:(t + 1) * P], p_tok[:, t, k * P:(k + 1) * P])
                last.then_inc(s.p_turned, 1)
                pe.wait_ge(s.pt_split, at(L, 1, 1))
                for j in range(KT):
                    end = j == KT - 1
                    unit(Block1, L, S_PLE + 8 + j // 4, T_PLE + KT + j, pth, ptl, kts=2, c0=(j % 4) * P, pitch=S,
                         new=j % 4 == 0, inc=3 if end else 1)

            with pe.Fori(0, 2) as L:
                ffn(L, 0, S_FFN1, T_FFN1, 0)
                w = xl_wait(Block1, L, 1)
                for u in range(4):
                    unit(Block1, L, S_IN + u, T_IN + u, xh, xl, wait_k=w if u == 0 else None)
                    if u == 1:
                        sum_squares(Block1, L, 1)
                with pe.Fori(1, 4) as i:
                    for u in range(4):
                        unit(Block1, L, S_IN + u, T_IN + u, xh, xl, i, 4)
                for u in range(16, 18):
                    unit(Block1, L, S_IN + u, T_IN + u, xh, xl)
                mlstm(L)
                swa(L)
                gated(L)
                ffn(L, 2, S_FFN2, T_FFN2, FT)
                ple(L)

            def gmlp(L):
                pe.wait_ge(s.gv_squared, at(L, 1, 1))
                pe.wait_ge(s.inv_var, norm_no(Block2, L, 0))
                for k in range(2):
                    last = pe.matmul(B4, ones[:], gv_sq[:, k, :], start=k == 0, stop=k == 1)
                last.then_inc(s.gv_ss, 1)
                pe.wait_ge(s.ws_landed, at(L, 16, 16))
                for h in range(4):
                    last = turn(B7[:, h * P:(h + 1) * P], ws_raw[:, h, :])
                last.then_inc(s.ws_turned, 1)
                pe.wait_ge(s.gv_normed, at(L, 1, 1))
                for t in range(NT):
                    for k in range(2):
                        o = (t % 2) * 2 * P + k * P
                        last = turn(mb[:, 1 + t // 2, o:o + P], proj2[:, 2 + k, t * P:(t + 1) * P])
                last.then_inc(s.gv_turned, 1)
                pe.wait_ge(s.gv_copied, at(L, 1, 1))
                pe.wait_ge(s.ws_copied, at(L, 1, 1))
                for k in range(2):
                    for c in range(NT):
                        for par in range(2):
                            h = 2 * k + par
                            out = mb[64 * par:64 * par + 64, k, c * P:(c + 1) * P]
                            pe.matmul(out, gv_tok[:, c, h * 64:h * 64 + 64], ws_t[:, h, :], start=True, stop=False)
                            last = pe.matmul(out, const[0:4, C_IDENT + h:C_IDENT + h + 1].to_broadcast([4, 64]),
                                             bs_now[:], start=False, stop=True)
                last.then_inc(s.gm_psum, 1)

            def ssd(L):
                pe.wait_ge(s.conv_silu, at(L, 1, 1))
                pe.wait_ge(s.gm_done, at(L, 1, 1))
                for t in range(NT):
                    for k in range(3):
                        last = turn(mb[:, t, k * P:(k + 1) * P], conv[:, k, t * P:(t + 1) * P])
                last.then_inc(s.xs_turned, 1)
                pe.wait_ge(s.dt_rows_done, at(L, 1, 1))
                pe.wait_ge(s.xs_copied, at(L, 1, 1))
                for t in range(NT):
                    turn(B5[:, t * SSD_H:(t + 1) * SSD_H], acc[0:SSD_H, t * P:(t + 1) * P], SSD_H)
                    last = turn(B5[:, 64 + t * SSD_H:64 + (t + 1) * SSD_H], var[0:SSD_H, t * P:(t + 1) * P], SSD_H)
                last.then_inc(s.dcol_turned, 1)
                for h in range(SSD_H):
                    g, tile, half = h // 3, h // 2, 64 * (h % 2)
                    if h % 3 == 0:
                        for j in range(NT):
                            c = 4 * g + j
                            if c:
                                pe.wait_ge(s.cb_copied, at(L, 8, c))
                            else:
                                pe.wait_ge(s.dcol_copied, at(L, 1, 1))
                            pe.matmul(B5[:, 0:S - j * P], conv[64 * g:64 * g + 64, 3, j * P:(j + 1) * P],
                                      conv[64 * g:64 * g + 64, 4, j * P:S], start=True, stop=True).then_inc(s.cb_ready, 1)
                    if h:
                        pe.wait_ge(s.abc_copied, at(L, SSD_H, h))
                    pe.matmul(B4, const[0:SSD_H, C_IDENT + h:C_IDENT + h + 1].to_broadcast([SSD_H, P]), acc[0:SSD_H, :],
                              start=True, stop=True).then_inc(s.abc_ready, 1)
                    out = mb[half:half + 64, 2 + tile % 2, :]
                    for j in range(NT):
                        pe.wait_ge(s.sp_ready, at(L, 24, 4 * h + j + 1))
                        if j == 0 and h == 4:
                            pe.wait_ge(s.y_done, at(L, 3, 1))
                        o = ML_OFF[j]
                        last = pe.matmul(out[:, j * P:S], xs_tok[:, j, h * 64:h * 64 + 64], sd_p[:, o:o + S - j * P],
                                         start=j == 0, stop=j == 3)
                    last.then_inc(s.y_psum, 1)
                pe.wait_ge(s.y_squared, at(L, 1, 1))
                pe.matmul(B4, ones[:], y_sq[:, 0, :], start=True, stop=False)
                pe.matmul(B4, ones[0:64, :], y_sq[0:64, 1, :], start=False, stop=True)
                pe.matmul(mb[0:64, 1, :], ones[:, 0:64], y_sq[:, 0, :], start=True, stop=False)
                pe.matmul(mb[0:64, 1, :], ones[0:64, 0:64], y_sq[0:64, 1, :], start=False, stop=True)
                pe.matmul(mb[64:P, 1, :], ones[:, 0:64], y_sq[:, 2, :], start=True, stop=False)
                pe.matmul(mb[64:P, 1, :], ones[64:P, 0:64], y_sq[64:P, 1, :], start=False, stop=True)
                pe.matmul(B6, ones[:], y_sq[:, 2, :], start=True, stop=False)
                pe.matmul(B6, ones[64:P, :], y_sq[64:P, 1, :], start=False, stop=True).then_inc(s.y_ss, 1)

            def mla(L):
                B = Block2
                pe.wait_ge(s.c_squared, at(L, 1, 1))
                pe.wait_ge(s.y_ss_read, at(L, 1, 1))
                for k in range(3):
                    pe.matmul(B4, ones[:], c_sq[:, k, :], start=k == 0, stop=k == 2)
                for k in range(2):
                    last = pe.matmul(B5, ones[:], c_sq[:, 3 + k, :], start=k == 0, stop=k == 1)
                last.then_inc(s.c_ss, 1)
                pe.wait_ge(s.rope_landed, 16)
                pe.matmul(B6[0:MLA_D, :], rot96, proj2[0:MLA_D, 12, :], start=True, stop=True).then_inc(s.rot_psum, 1)
                pe.wait_ge(s.c_split, at(L, 1, 1))
                for h in range(MLA_H):
                    unit(B, L, S2_QB + h // 2, T2_QB + h, cqh, cql, kts=3, width=MLA_D, c0=(h % 2) * MLA_D,
                         pitch=2 * MLA_D, new=h % 2 == 0)
                for u in range(MLA_H + 1):
                    if u < MLA_H:
                        unit(B, L, S2_KVB + u // 2, T2_KVB + u, ckh, ckl, kts=2, c0=(u % 2) * P, pitch=2 * P,
                             new=u % 2 == 0)
                    if u == 0:
                        continue
                    h = u - 1
                    pe.wait_ge(s.tile_evacuated, tiles_out(B, L, T2_QB + h))
                    pe.wait_ge(s.rot_read, at(L, 1 + MLA_H, max(1, h)))
                    pe.matmul(mb[0:MLA_D, 2 + (h + 1) % 2, :], rot96, q96[:, h, :], start=True, stop=True)\
                      .then_inc(s.rot_psum, 1)
                    pe.wait_ge(s.kv_done, at(L, MLA_H, h + 1))
                    if h >= 2:
                        pe.wait_ge(s.vt_copied, at(L, MLA_H, h - 1))
                    for t in range(NT):
                        last = pe.matmul(mb[:, h % 2, t * 64:(t + 1) * 64], v_ft[64:P, h % 2, t * P:(t + 1) * P],
                                         const[64:P, C_IDENT + 64:C_IDENT + P], start=True, stop=True)
                    last.then_inc(s.vt_psum, 1)
                pe.wait_ge(s.rot_done, at(L, 1 + MLA_H, 1 + MLA_H))
                pe.wait_ge(s.vt_copied, at(L, MLA_H, MLA_H))
                for h in range(MLA_H):
                    half = 64 * (h % 2)

                    def logits(n):
                        c = 4 * h + n
                        if c >= 2:
                            pe.wait_ge(s.ae_ready, at(L, 24, c - 1))
                        out = mb[:, n % 2, :]
                        pe.matmul(out[:, 0:(n + 1) * P], q96[:, h, n * P:(n + 1) * P], k96[:, h, 0:(n + 1) * P],
                                  start=True, stop=False)
                        pe.matmul(out[:, n * P:(n + 1) * P], ident, mask_qs, start=False, stop=True)\
                          .then_inc(s.al_ready, 1)

                    def turned(n):
                        c = 4 * h + n
                        pe.wait_ge(s.ap_ready, at(L, 24, c + 1))
                        if c:
                            pe.wait_ge(s.at_copied, at(L, 24, c))
                        for j in range(n + 1):
                            last = turn(B6[:, j * P:(j + 1) * P], prob[:, n % 2, j * P:(j + 1) * P])
                        last.then_inc(s.at_ready, 1)

                    logits(0)
                    logits(1)
                    turned(0)
                    logits(2)
                    turned(1)
                    logits(3)
                    turned(2)
                    turned(3)
                    pe.wait_ge(s.at_copied, at(L, 24, 4 * h + 4))
                    if h:
                        pe.wait_ge(s.ao_done, at(L, MLA_H, h))
                    for j in range(NT):
                        last = pe.matmul(B7[half:half + 64, j * P:S], v_tok[:, j, h * 64:h * 64 + 64],
                                         prob_t[:, j, j * P:S], start=j == 0, stop=j == 3)
                    last.then_inc(s.ao_ready, 1)

            with pe.Fori(0, 2) as L:
                B = Block2
                w = xl_wait(B, L, 0)
                for u in range(4):
                    unit(B, L, S2_IN + u, T2_IN + u, xh, xl, wait_k=w if u == 0 else None)
                    if u == 1:
                        sum_squares(B, L, 0)
                with pe.Fori(1, 3) as i:
                    for u in range(4):
                        unit(B, L, S2_IN + u, T2_IN + u, xh, xl, i, 4)
                for u in range(12, 18):
                    wide = MLA_D if u == 12 else P
                    unit(B, L, S2_IN + u, T2_IN + u, xh, xl, width=wide, pitch=wide)
                gmlp(L)
                ssd(L)
                mla(L)
                pe.wait_ge(s.ao_done, at(L, MLA_H, MLA_H))
                for j in range(KT):
                    unit(B, L, S2_OUT + j, T2_OUT + j, xh, xl)
                w = xl_wait(B, L, 1)
                for half in range(2):
                    n0, t0 = S2_MLP + half * 2 * HALF2, T2_MLP + half * (HALF2 + 8)
                    for u in range(4):
                        unit(B, L, n0 + u, t0 + u, xh, xl, wait_k=w if u == 0 and half == 0 else None)
                        if u == 1 and half == 0:
                            sum_squares(B, L, 1)
                    with pe.Fori(1, HALF2 // 4) as i:
                        for u in range(4):
                            unit(B, L, n0 + u, t0 + u, xh, xl, i, 4)
                    for dh in range(2):
                        n1, t1 = n0 + HALF2 + 8 * dh, t0 + HALF2 + 4 * dh

                        def down(q, i=None):
                            take_slab(B, L, n1 + q, i, 4)
                            h, l = wh[(n1 + q) % SPLIT_SLOTS], wl[(n1 + q) % SPLIT_SLOTS]
                            if dh == 0:
                                pe.wait_ge(s.hidden_ready,
                                           at(L, FT2, 4 * FT + half * HALF2 + 2 * q + 2, i, 8))
                            for kk_ in range(2):
                                kt = 2 * q + kk_ if i is None else i * 8 + (2 * q + kk_)
                                first, end = i is None and q == 0 and kk_ == 0, q == 7 and kk_ == 1
                                for d in range(4):
                                    if first:
                                        open_tile(B, L, t1 + d)
                                    out = bank[(B.base_tile + t1 + d) % TILE_BANKS][:]
                                    c = kk_ * S + d * P
                                    last = three(out, h[:, c:c + P], l[:, c:c + P], hh[:, kt, :], hl[:, kt, :],
                                                 first, end, new=kk_ == 0 and d == 0)
                                    if end:
                                        last.then_inc(s.tile_ready, 3 if half and dh and d == 3 else 1)

                        for q in range(8):
                            down(q)

            pe.wait_ge(s.ss_ready, 13)
            pe.matmul(B4, ones[:], acc[:], start=True, stop=True).then_inc(s.ss_psum, 1)
            pe.wait_ge(s.fin_y, 1)
            for c in range(2 * NT):
                t, side = c // 2, c % 2
                if c >= 4:
                    pe.wait_ge(s.fin_copied, c - 3)
                for j in range(4):
                    last = turn(mb[:, c % 4, j * P:(j + 1) * P], y_sb[:, 4 * side + j, t * P:(t + 1) * P])
                last.then_inc(s.fin_turned, 1)

        @block.scalar
        def _(act):
            def round_hi(B, L, n, i=None, step=0):
                if n >= B.slabs:
                    return
                act.wait_ge(raw_landed[n % RAW_SLOTS],
                            at(L, 8 * B.slabs, 8 * (B.base_slab + n - n % 2) + 16, i, 8 * step))
                act.wait_ge(s.slab_used, at(L, B.slabs, B.base_slab + n + 1, i, step))
                if B is Block2 and n == S2_IN + 12:
                    act.wait_ge(s.kr_landed, at(L, 16, 16))
                act.activation(wh[n % SPLIT_SLOTS][:], raw[n % RAW_SLOTS][:], ACT.Copy).then_inc(s.hi_ready, 1)

            def ahead(B, L, n, count, i=None, step=0):
                for k in range(count):
                    round_hi(B, L, n + k + AHEAD, i, step)

            def norm(B, L, k):
                no = norm_no(B, L, k)
                act.wait_ge(s.x_final, no)
                for q in range(2):
                    last = act.activation(squares[:, 4 * q:4 * q + 4, :], x_sb[:, 4 * q:4 * q + 4, :], ACT.Square)
                last.then_inc(s.sq_ready, 1)

            def norm_root(B, L, k):
                act.wait_ge(s.inv_var, norm_no(B, L, k))
                act.activation(rstd[:], var[:], ACT.Sqrt).then_inc(s.rstd_ready, 1)

            def ffn(L, k, n, t, silu0):
                norm(Block1, L, k)
                ahead(Block1, L, n, 2)
                norm_root(Block1, L, k)

                def pair(f, i=None):
                    act.wait_ge(s.tile_evacuated, tiles_out(Block1, L, t + 2 * f, i, 4))
                    act.activation(tmp[f % 2][:], tmp[f % 2][:], ACT.Silu).then_inc(s.silu_done, 1)

                pair(0)
                ahead(Block1, L, n + 2, 2)
                pair(1)
                with act.Fori(1, FT // 2) as i:
                    for f in range(2):
                        round_hi(Block1, L, n + 2 * f + AHEAD, i, 4)
                        pair(f, i)
                        round_hi(Block1, L, n + 2 * f + 1 + AHEAD, i, 4)
                n0 = n + 2 * FT
                with act.Fori(0, 5) as i:
                    ahead(Block1, L, n0, 4, i, 4)
                ahead(Block1, L, n0 + 20, 2)

            def mlstm(L):
                act.wait_ge(s.tile_evacuated, tiles_out(Block1, L, T_IN + 11))
                act.activation(proj[:, 8:12, :], proj[:, 8:12, :], ACT.Sigmoid).then_inc(s.mo_done, 1)
                fp, ig, e1, e2 = ml_rows[0:4]
                act.wait_ge(s.gate_pre, at(L, 1, 1))
                act.activation(e1[:], fp[:], ACT.Abs)
                act.drain()
                act.activation(e2[:], e1[:], ACT.Exp, scale=-1.0)
                act.drain()
                act.activation(e1[:], e2[:], ACT.Ln, bias=1.0).then_inc(s.log1p, 1)
                act.wait_ge(s.ml_rows_done, at(L, 1, 1))
                act.activation(var[0:ML_H, :], ml_rows[7][:], ACT.Exp, scale=-1.0).then_inc(s.emt_done, 1)
                for h in range(ML_H):
                    act.wait_ge(s.bc_copied, at(L, 2 * ML_H, 2 * h + 1))
                    if h:
                        act.wait_ge(s.p_ready, at(L, 16, 4 * h))
                    else:
                        act.wait_ge(s.c_copied, at(L, 1, 1))
                    for j in range(NT):
                        o = ML_OFF[j]
                        last = act.activation(ml_w[:, o:o + P], neg_md[:, j * P:(j + 1) * P], ACT.Exp,
                                              bias=c_col[:, j, h:h + 1])
                        if j < NT - 1:
                            last = act.activation(ml_w[:, o + P:o + S - j * P], neg_m[:, (j + 1) * P:S], ACT.Exp,
                                                  bias=c_col[:, j, h:h + 1])
                        last.then_inc(s.w_ready, 1)
                    act.wait_ge(s.pv_done, at(L, 16, 4 * h + 4))
                    if h:
                        act.wait_ge(s.head_done, at(L, ML_H, h))
                    act.activation(abs_den[:], B7, ACT.Abs).then_inc(s.abs_done, 1)
                act.wait_ge(s.head_done, at(L, ML_H, ML_H))
                act.activation(inv[:], num_sb[:], ACT.Square).then_inc(s.num_sq, 1)
                act.wait_ge(s.ml_inv, at(L, 1, 1))
                act.activation(inv[:], inv[:], ACT.Sqrt).then_inc(s.ml_rs, 1)

            def swa(L):
                act.wait_ge(s.ha_ready, at(L, 1, 1))
                act.activation(qk_sq[:], proj[:, 12:17, :], ACT.Square).then_inc(s.qk_squared, 1)
                act.wait_ge(s.qk_inv, at(L, 1, 1))
                act.activation(qk_sq[:], qk_sq[:], ACT.Sqrt).then_inc(s.qk_rs, 1)
                for b in range(8):
                    n = b // SW_KV
                    lo = 0 if n else P
                    act.wait_ge(s.mx_ready, at(L, 8, b + 1))
                    for i in range(SW_G):
                        act.activation(lg[:, b % 2, i, lo:2 * P], lg[:, b % 2, i, lo:2 * P], ACT.Exp,
                                       bias=small[:, 4 + i:5 + i], accum_out=small[:, 12 + i:13 + i])
                    act.activation(small[:, 16:20], small[:, 8:12], ACT.Exp).then_inc(s.ex_ready, 1)

            def gated(L):
                with act.Fori(0, 2) as i:
                    for jj in range(2):
                        n, t = S_GATED + 6 * jj, T_GATED + 8 * jj
                        for u in range(4):
                            round_hi(Block1, L, n + u + AHEAD, i, 12)
                            act.wait_ge(s.tile_evacuated, tiles_out(Block1, L, t + u, i, 16))
                            act.activation(tmp[u][:], tmp[u][:], ACT.Sigmoid).then_inc(s.sig_done, 1)
                        ahead(Block1, L, n + 4, 2, i, 12)
                ahead(Block1, L, S_OUT, 8)

            def ple(L):
                norm(Block1, L, 3)
                ahead(Block1, L, S_PLE, 2)
                norm_root(Block1, L, 3)
                for j in range(KT):
                    act.wait_ge(s.tile_evacuated, tiles_out(Block1, L, T_PLE + j))
                    act.activation(gate_sg[:, j, :], gate_sg[:, j, :], ACT.Sigmoid).then_inc(s.sg_done, 1)
                    if j >= 2:
                        round_hi(Block1, L, S_PLE + j + AHEAD)

            act.wait_ge(s.toep_row, SW_H)
            act.dma_start(scratch.rearrange("h p c -> p h c"), toep[:]).then_inc(s.toep_out, 16)
            act.wait_ge(s.toep_out, 16)
            act.dma_start(bias[:], bass.AP(scratch.tensor, P - 1, [[TOEP - 1, P], [P * TOEP, SW_H], [1, 2 * P]]))\
               .then_inc(s.toep_in, 16)
            with act.Fori(0, 2) as L:
                for n in range(AHEAD):
                    round_hi(Block1, L, n)
                ffn(L, 0, S_FFN1, T_FFN1, 0)
                norm(Block1, L, 1)
                ahead(Block1, L, S_IN, 2)
                norm_root(Block1, L, 1)
                ahead(Block1, L, S_IN + 2, 16)
                mlstm(L)
                swa(L)
                gated(L)
                ffn(L, 2, S_FFN2, T_FFN2, FT)
                ple(L)

            def gmlp(L):
                for u in range(4):
                    act.wait_ge(s.tile_evacuated, tiles_out(Block2, L, T2_IN + u))
                    last = act.activation(proj2[:, u, :], proj2[:, u, :], ACT.Gelu_apprx_tanh)
                last.then_inc(s.gelu_done, 1)
                act.drain()
                act.activation(gv_sq[:], proj2[:, 2:4, :], ACT.Square).then_inc(s.gv_squared, 1)
                act.wait_ge(s.tile_evacuated, tiles_out(Block2, L, T2_IN + 6))
                act.activation(proj2[:, 4:7, :], proj2[:, 4:7, :], ACT.Silu).then_inc(s.z_silu, 1)
                act.wait_ge(s.conv_done, at(L, 1, 1))
                act.activation(conv[:], conv[:], ACT.Silu).then_inc(s.conv_silu, 1)
                act.wait_ge(s.gv_inv, at(L, 1, 1))
                act.activation(tmp[1][:], tmp[0][:], ACT.Sqrt).then_inc(s.gv_rs, 1)

            def ssd(L):
                act.wait_ge(s.dt_pre, at(L, 1, 1))
                act.activation(tmp[3][0:SSD_H, :], tmp[2][0:SSD_H, :], ACT.Abs)
                act.drain()
                act.activation(tmp[1][0:SSD_H, :], tmp[3][0:SSD_H, :], ACT.Exp, scale=-1.0)
                act.activation(small[0:SSD_H, 1:2], dt_now[:, 1:2], ACT.Exp)
                act.drain()
                act.activation(tmp[3][0:SSD_H, :], tmp[1][0:SSD_H, :], ACT.Ln, bias=1.0).then_inc(s.dt_log, 1)
                for h in range(SSD_H):
                    act.wait_ge(s.abc_copied, at(L, SSD_H, h + 1))
                    if h:
                        act.wait_ge(s.sp_ready, at(L, 24, 4 * h))
                    for j in range(NT):
                        o = ML_OFF[j]
                        last = act.activation(sd_w[:, o:o + P], tmp[1][:, j * P:(j + 1) * P], ACT.Exp,
                                              bias=a_col[:, j, h:h + 1])
                        if j < NT - 1:
                            last = act.activation(sd_w[:, o + P:o + S - j * P], tmp[0][:, (j + 1) * P:S], ACT.Exp,
                                                  bias=a_col[:, j, h:h + 1])
                        last.then_inc(s.sw_ready, 1)
                act.wait_ge(s.y_done, at(L, 3, 3))
                act.activation(y_sq[:], proj2[:, 4:7, :], ACT.Square).then_inc(s.y_squared, 1)
                act.wait_ge(s.y_inv, at(L, 1, 1))
                act.activation(y_sq[:], y_sq[:], ACT.Sqrt).then_inc(s.y_rs, 1)

            def mla(L):
                act.wait_ge(s.ssd_done, at(L, 1, 1))
                act.activation(c_sq[:], proj2[:, 13:18, :], ACT.Square).then_inc(s.c_squared, 1)
                act.wait_ge(s.c_inv, at(L, 1, 1))
                act.activation(acc[:], tmp[0][:], ACT.Sqrt)
                act.activation(var[:], tmp[1][:], ACT.Sqrt).then_inc(s.c_rs, 1)
                ahead(Block2, L, S2_QB, 6)
                for h in range(MLA_H):
                    for n in range(NT):
                        c = 4 * h + n
                        act.wait_ge(s.am_ready, at(L, 24, c + 1))
                        if c >= 2:
                            act.wait_ge(s.at_ready, at(L, 24, c - 1))
                        w = (n + 1) * P
                        act.activation(prob[:, n % 2, 0:w], mb[:, n % 2, 0:w], ACT.Exp,
                                       bias=small[:, 32 + n:33 + n], scale=MLA_SCALE,
                                       accum_out=small[:, 36 + n:37 + n]).then_inc(s.ae_ready, 1)

            with act.Fori(0, 2) as L:
                B = Block2
                for n in range(AHEAD):
                    round_hi(B, L, n)
                norm(B, L, 0)
                ahead(B, L, S2_IN, 2)
                norm_root(B, L, 0)
                ahead(B, L, S2_IN + 2, 16)
                gmlp(L)
                ssd(L)
                mla(L)
                ahead(B, L, S2_OUT, 8)
                norm(B, L, 1)
                ahead(B, L, S2_MLP, 2)
                norm_root(B, L, 1)
                ahead(B, L, S2_MLP + 2, 2)
                with act.Fori(1, 2 * FT2 // 4 - 1) as i:
                    ahead(B, L, S2_MLP, 4, i, 4)
                ahead(B, L, B2_SLABS - 4, 4)
            act.wait_ge(s.x_final, 13)
            for q in range(2):
                last = act.activation(squares[:, 4 * q:4 * q + 4, :], x_sb[:, 4 * q:4 * q + 4, :], ACT.Square)
            last.then_inc(s.sq_ready, 1)
            act.wait_ge(s.inv_var, 13)
            act.activation(rstd[:], var[:], ACT.Sqrt).then_inc(s.rstd_ready, 1)

        @block.vector
        def _(dve):
            def split(hi, lo, src):
                dve.tensor_copy(hi, src)
                dve.drain()
                return dve.tensor_tensor(lo, src, hi.bitcast(F32), ALU.subtract)

            def invert(out, sums, scale):
                dve.tensor_scalar(out, sums, scale, EPS, ALU.mult, ALU.add)
                dve.drain()
                return dve.reciprocal(out, out)

            def read_tile(B, L, t, out, scale, i=None, step=0, rows=(0, P), inc=1):
                dve.wait_ge(s.tile_ready, tiles_in(B, L, t, i, step))
                r0, r1 = rows
                return dve.tensor_tensor(out, bank[(B.base_tile + t) % TILE_BANKS][r0:r1, :], scale[r0:r1, :], ALU.mult)\
                          .then_inc(s.tile_evacuated, inc)

            def norm(B, L, k, g):
                no = norm_no(B, L, k)
                dve.drain().then_inc(s.x_final, 1)
                for j in range(KT):
                    dve.tensor_scalar(xh[:, j, :], x_sb[:, j, :], g[:, j:j + 1], None, ALU.mult)
                    dve.drain()
                    dve.scalar_tensor_tensor(out=xl[:, j, :], in0=x_sb[:, j, :], scalar=g[:, j:j + 1],
                                             in1=xh[:, j, :].bitcast(F32), op0=ALU.mult, op1=ALU.subtract)\
                       .then_inc(s.xl_ready, 1)
                norm_scale(no)

            def scaled_tile(B, L, k, t, out, i=None, step=0, rows=(0, P), inc=1):
                dve.wait_ge(s.rstd_ready, norm_no(B, L, k))
                return read_tile(B, L, t, out, rstd, i, step, rows, inc)

            def norm_scale(no):
                dve.wait_ge(s.sq_ready, no)
                dve.tensor_reduce(acc[:], squares[:].rearrange("p j t -> p t j"), AX.X, ALU.add).then_inc(s.ss_ready, 1)
                dve.wait_ge(s.ss_psum, no)
                invert(var[:], B4, 1.0 / D).then_inc(s.inv_var, 1)

            def add_x(B, L, t, j, scale=1.0, inc=1):
                dve.wait_ge(s.tile_ready, tiles_in(B, L, t))
                dve.scalar_tensor_tensor(out=x_sb[:, j, :], in0=bank[(B.base_tile + t) % TILE_BANKS][:], scalar=scale,
                                         in1=x_sb[:, j, :], op0=ALU.mult, op1=ALU.add).then_inc(s.tile_evacuated, inc)

            for j in range(KT):
                dve.wait_ge(s.setup_t, j + 1)
                dve.tensor_copy(x_sb[:, j, :], mb[:, j % 4, :]).then_inc(s.setup_copied, 1)
            dve.wait_ge(s.setup_t, KT + 1)
            dve.tensor_copy(p1[:], B4[:, 0:2 * R1])
            dve.tensor_copy(p2[:], B5[:, 0:2 * R2 + KT])
            for h in range(SW_H):
                dve.wait_ge(s.rel_psum, h + 1)
                dve.tensor_tensor(toep[:, h, :], mb[:, 2 + h % 2, 0:TOEP], pad[:], ALU.add).then_inc(s.toep_row, 1)
            dve.wait_ge(s.toep_out, 16)
            dve.drain()

            def ffn(L, k, g, t, silu0):
                norm(Block1, L, k, g)
                def pair(f, i=None):
                    gs, us = tmp[f % 2], tmp[2 + f % 2]
                    scaled_tile(Block1, L, k, t + 2 * f, gs[:], i, 4)
                    scaled_tile(Block1, L, k, t + 2 * f + 1, us[:], i, 4)
                    dve.drain()
                    dve.wait_ge(s.silu_done, at(L, 2 * FT, silu0 + f + 1, i, 2))
                    dve.tensor_tensor(us[:], us[:], gs[:], ALU.mult)
                    dve.drain()
                    j = f if i is None else i * 2 + f
                    split(hh[:, j, :], hl[:, j, :], us[:]).then_inc(s.hidden_ready, 1)

                with dve.Fori(0, FT // 2) as i:
                    for f in range(2):
                        pair(f, i)
                for j in range(KT):
                    add_x(Block1, L, t + 2 * FT + j, j, 0.5)

            def mlstm(L):
                fp, ig, e1, e2, fc, cc, mm, mt, lf = ml_rows
                dve.wait_ge(s.gates_psum, at(L, 1, 1))
                dve.tensor_tensor(ig[:], B4[0:ML_H, :], rstd[0:ML_H, :], ALU.mult)
                dve.tensor_tensor(fp[:], B5[0:ML_H, :], rstd[0:ML_H, :], ALU.mult)
                dve.drain()
                dve.tensor_scalar(ig[:], ig[:], b_gate_now[:, 0:1], None, ALU.add)
                dve.tensor_scalar(fp[:], fp[:], b_gate_now[:, 1:2], None, ALU.add).then_inc(s.gate_pre, 1)
                for t in range(NT + 1):
                    dve.wait_ge(s.v_turned, at(L, 5, t + 1))
                    dst = mv_tok[:, t, :] if t < NT else sv_tok[:].rearrange("p t c -> p (t c)")
                    dve.tensor_copy(dst, mb[:, 2 + t % 2, :]).then_inc(s.v_copied, 1)
                dve.tensor_scalar(lf[:], fp[:], 0.0, None, ALU.min)
                dve.drain()
                dve.wait_ge(s.log1p, at(L, 1, 1))
                dve.tensor_tensor(lf[:], lf[:], e1[:], ALU.subtract)
                dve.drain()
                dve.tensor_tensor_scan(fc[:], ones[0:ML_H, 0:1].to_broadcast([ML_H, S]), lf[:], 0.0, ALU.mult, ALU.add)
                dve.drain()
                dve.tensor_tensor(cc[:], ig[:], fc[:], ALU.subtract)
                dve.drain()
                dve.tensor_tensor_scan(mm[:], cc[:], cc[:], 0.0, ALU.max, ALU.max)
                dve.drain()
                dve.tensor_scalar(acc[0:ML_H, :], mm[:], -1.0, None, ALU.mult)
                dve.tensor_tensor(mt[:], mm[:], fc[:], ALU.add).then_inc(s.ml_rows_done, 1)
                dve.wait_ge(s.c_turned, at(L, 1, 1))
                dve.tensor_copy(c_col[:].rearrange("p t h -> p (t h)"), B5[:, 0:NT * ML_H]).then_inc(s.c_copied, 1)
                for h in range(ML_H):
                    dve.wait_ge(s.bc_ready, at(L, 2 * ML_H, 2 * h + 1))
                    if h:
                        dve.wait_ge(s.w_ready, at(L, 16, 4 * h))
                    dve.tensor_copy(neg_m[:], B4)
                    dve.tensor_tensor(neg_md[:].rearrange("p (t q) -> p t q", t=NT), B4.rearrange("p (t q) -> p t q", t=NT),
                                      mask_sq[:, None, :].to_broadcast([P, NT, P]), ALU.add).then_inc(s.bc_copied, 1)
                    dve.wait_ge(s.bc_ready, at(L, 2 * ML_H, 2 * h + 2))
                    dve.tensor_copy(emt_bc[:], B4).then_inc(s.bc_copied, 1)
                    for j in range(NT):
                        e = 4 * h + j
                        dve.wait_ge(s.w_ready, at(L, 16, e + 1))
                        dve.wait_ge(s.sc_ready, at(L, 16, e + 1))
                        if h:
                            dve.wait_ge(s.pv_done, at(L, 16, e - 3))
                        o, w = ML_OFF[j], S - j * P
                        dve.scalar_tensor_tensor(out=ml_p[:, o:o + w], in0=B5[:, 0:w], scalar=0.125,
                                                 in1=ml_w[:, o:o + w], op0=ALU.mult, op1=ALU.mult).then_inc(s.p_ready, 1)
                    dve.wait_ge(s.pv_done, at(L, 16, 4 * h + 4))
                    dve.tensor_copy(num_sb[:, h, :], B6)
                    dve.wait_ge(s.abs_done, at(L, ML_H, h + 1))
                    dve.tensor_tensor(tmp[h][:], abs_den[:], emt_bc[:], ALU.max)
                    dve.drain()
                    dve.scalar_tensor_tensor(out=tmp[h][:], in0=tmp[h][:], scalar=EPS, in1=tmp[h][:], op0=ALU.mult,
                                             op1=ALU.mult).then_inc(s.head_done, 1)
                for h in range(ML_H):
                    dve.wait_ge(s.ml_ss, at(L, ML_H, h + 1))
                    dve.scalar_tensor_tensor(out=inv[:, h, :], in0=mb[:, h % 2, :], scalar=1.0 / P, in1=tmp[h][:],
                                             op0=ALU.mult, op1=ALU.add).then_inc(s.ml_ss_read, 1)
                dve.drain()
                dve.reciprocal(inv[:], inv[:]).then_inc(s.ml_inv, 1)
                dve.wait_ge(s.ml_rs, at(L, 1, 1))
                dve.wait_ge(s.mo_done, at(L, 1, 1))
                for h in range(ML_H):
                    dve.scalar_tensor_tensor(out=num_sb[:, h, :], in0=num_sb[:, h, :], scalar=par1[:, R_MLOUT + h:R_MLOUT + h + 1],
                                             in1=inv[:, h, :], op0=ALU.mult, op1=ALU.mult)
                    dve.drain()
                    dve.tensor_tensor(num_sb[:, h, :], num_sb[:, h, :], proj[:, 8 + h, :], ALU.mult)
                    dve.drain()
                    last = split(hah[:, h, :], hal[:, h, :], num_sb[:, h, :])
                last.then_inc(s.ha_ready, 1)

            def swa(L):
                for u in range(5):
                    dve.wait_ge(s.qk_ss, at(L, 5, u + 1))
                    dve.tensor_scalar(qk_sq[:, u, :], mb[:, u % 2, :], 1.0 / 64, EPS, ALU.mult, ALU.add)\
                       .then_inc(s.qk_ss_read, 1)
                dve.drain()
                dve.reciprocal(qk_sq[:], qk_sq[:]).then_inc(s.qk_inv, 1)
                dve.tensor_scalar(small[:, 0:1], par1[:, R_QN:R_QN + 1], 0.125, None, ALU.mult)
                dve.drain()
                dve.wait_ge(s.qk_rs, at(L, 1, 1))
                for u in range(5):
                    gain = small[:, 0:1] if u < 4 else par1[:, R_KN:R_KN + 1]
                    last = dve.scalar_tensor_tensor(out=proj[:, 12 + u, :], in0=proj[:, 12 + u, :], scalar=gain,
                                                    in1=qk_sq[:, u, :], op0=ALU.mult, op1=ALU.mult)
                last.then_inc(s.qk_normed, 1)
                dve.wait_ge(s.kk_psum, at(L, 1, 1))
                for g in range(SW_KV):
                    last = dve.tensor_copy(kk[:, g, :], mb[:, 2 + g, :])
                last.then_inc(s.kk_copied, 1)

                def of_side(buf, side):
                    return buf.rearrange("p (i two) k -> p two i k", two=2)[:, side]

                def biased(b):
                    n, g = b // SW_KV, b % SW_KV
                    lo = 0 if n else P
                    buf = lg[:, b % 2, :, lo:2 * P]
                    dve.wait_ge(s.lg_ready, at(L, 8, b + 1))
                    for side in range(2):
                        last = dve.tensor_tensor(of_side(lg[:, b % 2], side)[:, :, lo:2 * P],
                                                 mb[:, side, :].rearrange("p (i k) -> p i k", i=2)[:, :, lo:2 * P],
                                                 of_side(bias[:, g * SW_G:(g + 1) * SW_G], side)[:, :, lo:2 * P], ALU.add)
                    last.then_inc(s.lg_read, 1)
                    dve.drain()
                    dve.tensor_reduce(small[:, 20:24], buf, AX.X, ALU.max)
                    dve.drain()
                    dve.tensor_tensor(small[:, 20:24], small[:, 20:24], sinks_now[:, g * SW_G:g * SW_G + SW_G], ALU.max)
                    dve.drain()
                    dve.tensor_scalar(small[:, 4:8], small[:, 20:24], -1.0, None, ALU.mult)
                    dve.tensor_tensor(small[:, 8:12], sinks_now[:, g * SW_G:g * SW_G + SW_G], small[:, 20:24],
                                      ALU.subtract).then_inc(s.mx_ready, 1)

                biased(0)
                for b in range(8):
                    n, g = b // SW_KV, b % SW_KV
                    lo = 0 if n else P
                    dve.wait_ge(s.ex_ready, at(L, 8, b + 1))
                    dve.tensor_tensor(small[:, 24:28], small[:, 12:16], small[:, 16:20], ALU.add)
                    dve.drain()
                    dve.reciprocal(small[:, 28:32], small[:, 24:28])
                    dve.drain()
                    for i in range(SW_G):
                        last = dve.tensor_scalar(lg[:, b % 2, i, lo:2 * P], lg[:, b % 2, i, lo:2 * P],
                                                 small[:, 28 + i:29 + i], None, ALU.mult)
                    last.then_inc(s.pn_ready, 1)
                    if b < 7:
                        biased(b + 1)
                    dve.wait_ge(s.pt_ready, at(L, 8, b + 1))
                    for side in ((0, 1) if n else (1,)):
                        last = dve.tensor_copy(pt_sb[:, side].rearrange("p i q -> p (i q)"), mb[:, 2 + side, :])
                    last.then_inc(s.pt_copied, 1)
                    dve.wait_ge(s.o_ready, at(L, 8, b + 1))
                    src = B6[:, 0:2 * P].rearrange("p (i q) -> p i q", i=2)
                    split(hbh[:, 2 * g:2 * g + 2, n * P:(n + 1) * P], hbl[:, 2 * g:2 * g + 2, n * P:(n + 1) * P], src)\
                        .then_inc(s.o_done, 1)

            def gated(L):
                with dve.Fori(0, 2) as i:
                    for jj in range(2):
                        t = T_GATED + 8 * jj
                        for u in range(4):
                            read_tile(Block1, L, t + u, tmp[u][:], rstd, i, 16)
                        for u in range(4):
                            dve.wait_ge(s.sig_done, at(L, 16, 4 * jj + u + 1, i, 8))
                            read_tile(Block1, L, t + 4 + u, tmp[u][:], tmp[u], i, 16)
                        dve.drain()
                        for d in range(2):
                            dve.tensor_tensor(tmp[d][:], tmp[d][:], tmp[2 + d][:], ALU.add)
                        dve.drain()
                        for d in range(2):
                            j = i * 4 + (2 * jj + d)
                            split(mh[:, j, :], ml[:, j, :], tmp[d][:]).then_inc(s.mixed_ready, 1)
                        dve.drain()
                for j in range(KT):
                    add_x(Block1, L, T_OUT + j, j)

            def ple(L):
                norm(Block1, L, 3, par1[:, R_PLE:R_PLE + KT])
                for j in range(KT):
                    scaled_tile(Block1, L, 3, T_PLE + j, gate_sg[:, j, :])
                dve.wait_ge(s.p_turned, at(L, 1, 1))
                for k in range(2):
                    last = split(pth[:, k, :], ptl[:, k, :], mb[:, k, :])
                last.then_inc(s.pt_split, 1)
                for j in range(KT):
                    dve.wait_ge(s.sg_done, at(L, KT, j + 1))
                    read_tile(Block1, L, T_PLE + KT + j, tmp[j % 4][:], gate_sg[:, j, :], inc=3 if j == KT - 1 else 1)
                    dve.drain()
                    dve.tensor_tensor(x_sb[:, j, :], x_sb[:, j, :], tmp[j % 4][:], ALU.add)

            with dve.Fori(0, 2) as L:
                dve.tensor_copy(par1[:], p1[:, bass.ds(L * R1, R1)])
                dve.tensor_copy(b_gate_now[:, None, :], b_gate[:, bass.ds(L, 1), :])
                dve.tensor_copy(sinks_now[:, None, :], sinks[:, bass.ds(L, 1), :])
                dve.drain()
                ffn(L, 0, par1[:, R_FFN1:R_FFN1 + KT], T_FFN1, 0)
                dve.wait_ge(s.gate_landed, at(L, 16, 16))
                split(gate_h[:], gate_l[:], gate_raw[:]).then_inc(s.gate_split, 1)
                norm(Block1, L, 1, par1[:, R_MIX:R_MIX + KT])
                for u in range(18):
                    scaled_tile(Block1, L, 1, T_IN + u, proj[:, u, :])
                mlstm(L)
                dve.wait_ge(s.toep_in, 16)
                swa(L)
                gated(L)
                ffn(L, 2, par1[:, R_FFN2:R_FFN2 + KT], T_FFN2, FT)
                ple(L)

            def gmlp(L):
                dve.wait_ge(s.gv_ss, at(L, 1, 1))
                invert(tmp[0][:], B4, 1.0 / (2 * P)).then_inc(s.gv_inv, 1)
                dve.wait_ge(s.ws_turned, at(L, 1, 1))
                dve.tensor_tensor(ws_t[:], B7.rearrange("p (h t) -> p h t", h=4),
                                  tri_st[:, None, :].to_broadcast([P, 4, P]), ALU.mult).then_inc(s.ws_copied, 1)
                dve.wait_ge(s.gv_rs, at(L, 1, 1))
                for k in range(2):
                    last = dve.scalar_tensor_tensor(out=proj2[:, 2 + k, :], in0=proj2[:, 2 + k, :],
                                                    scalar=par2[:, Q_GV + k:Q_GV + k + 1], in1=tmp[1][:], op0=ALU.mult,
                                                    op1=ALU.mult)
                last.then_inc(s.gv_normed, 1)
                dve.wait_ge(s.gv_turned, at(L, 1, 1))
                for q in range(2):
                    last = dve.tensor_copy(gv_tok[:, 2 * q:2 * q + 2, :].rearrange("p t c -> p (t c)"), mb[:, 1 + q, :])
                last.then_inc(s.gv_copied, 1)
                dve.wait_ge(s.gm_psum, at(L, 1, 1))
                for k in range(2):
                    dve.tensor_tensor(tmp[k][:], mb[:, k, :], proj2[:, k, :], ALU.mult)
                    dve.drain()
                    last = split(xh[:, k, :], xl[:, k, :], tmp[k][:])
                last.then_inc(s.gm_done, 1)

            def convolve(L):
                for k in range(5):
                    w = lambda tap: par2[:, Q_CW + 5 * tap + k:Q_CW + 5 * tap + k + 1]
                    dve.tensor_scalar(conv[:, k, :], proj2[:, 7 + k, :], w(3), par2[:, Q_CB + k:Q_CB + k + 1], ALU.mult,
                                      ALU.add)
                    for tap in range(3):
                        lag = 3 - tap
                        dve.drain()
                        last = dve.scalar_tensor_tensor(out=conv[:, k, lag:S], in0=proj2[:, 7 + k, 0:S - lag], scalar=w(tap),
                                                        in1=conv[:, k, lag:S], op0=ALU.mult, op1=ALU.add)
                last.then_inc(s.conv_done, 1)

            def ssd(L):
                pre, e1 = tmp[2][0:SSD_H, :], tmp[3][0:SSD_H, :]
                dve.tensor_scalar(pre, proj2[0:SSD_H, 12, :], dt_now[:, 0:1], None, ALU.add).then_inc(s.dt_pre, 1)
                dve.wait_ge(s.xs_turned, at(L, 1, 1))
                for t in range(NT):
                    last = dve.tensor_copy(xs_tok[:, t, :], mb[:, t, 0:384])
                last.then_inc(s.xs_copied, 1)
                dve.wait_ge(s.dt_log, at(L, 1, 1))
                dve.scalar_tensor_tensor(out=var[0:SSD_H, :], in0=pre, scalar=0.0, in1=e1, op0=ALU.max, op1=ALU.add)
                dve.tensor_scalar(small[0:SSD_H, 2:3], small[0:SSD_H, 1:2], -1.0, None, ALU.mult)
                dve.drain()
                dve.tensor_scalar(tmp[0][0:SSD_H, :], var[0:SSD_H, :], small[0:SSD_H, 2:3], None, ALU.mult)
                dve.drain()
                dve.tensor_tensor_scan(acc[0:SSD_H, :], ones[0:SSD_H, 0:1].to_broadcast([SSD_H, S]), tmp[0][0:SSD_H, :], 0.0,
                                       ALU.mult, ALU.add).then_inc(s.dt_rows_done, 1)
                dve.wait_ge(s.dcol_turned, at(L, 1, 1))
                dve.tensor_scalar(a_col[:].rearrange("p t h -> p (t h)"), B5[:, 0:NT * SSD_H], -1.0, None, ALU.mult)
                dve.tensor_copy(dt_col[:].rearrange("p t h -> p (t h)"), B5[:, 64:64 + NT * SSD_H]).then_inc(s.dcol_copied, 1)
                dve.drain()
                for h in range(SSD_H):
                    g, tile = h // 3, h // 2
                    if h % 3 == 0:
                        for j in range(NT):
                            o, w = ML_OFF[j], S - j * P
                            dve.wait_ge(s.cb_ready, at(L, 8, 4 * g + j + 1))
                            dve.tensor_copy(cb[:, o:o + w], B5[:, 0:w]).then_inc(s.cb_copied, 1)
                    dve.wait_ge(s.abc_ready, at(L, SSD_H, h + 1))
                    if h:
                        dve.wait_ge(s.sw_ready, at(L, 24, 4 * h))
                    dve.tensor_copy(tmp[0][:], B4)
                    dve.tensor_tensor(tmp[1][:].rearrange("p (t q) -> p t q", t=NT), B4.rearrange("p (t q) -> p t q", t=NT),
                                      mask_sq[:, None, :].to_broadcast([P, NT, P]), ALU.add).then_inc(s.abc_copied, 1)
                    dve.drain()
                    for j in range(NT):
                        o, w = ML_OFF[j], S - j * P
                        dve.wait_ge(s.sw_ready, at(L, 24, 4 * h + j + 1))
                        if h and j == 0:
                            dve.wait_ge(s.y_psum, at(L, SSD_H, h))
                        dve.scalar_tensor_tensor(out=sd_p[:, o:o + w], in0=cb[:, o:o + w], scalar=dt_col[:, j, h:h + 1],
                                                 in1=sd_w[:, o:o + w], op0=ALU.mult, op1=ALU.mult).then_inc(s.sp_ready, 1)
                    if h % 2:
                        dve.wait_ge(s.y_psum, at(L, SSD_H, h + 1))
                        if h == 1:
                            dve.wait_ge(s.z_silu, at(L, 1, 1))
                        dve.scalar_tensor_tensor(out=conv[:, tile, :], in0=conv[:, tile, :], scalar=d_skip_now[:, tile:tile + 1],
                                                 in1=mb[:, 2 + tile % 2, :], op0=ALU.mult, op1=ALU.add)
                        dve.drain()
                        dve.tensor_tensor(proj2[:, 4 + tile, :], proj2[:, 4 + tile, :], conv[:, tile, :], ALU.mult)\
                           .then_inc(s.y_done, 1)
                dve.wait_ge(s.y_ss, at(L, 1, 1))
                for k in range(3):
                    last = dve.tensor_scalar(y_sq[:, k, :], mb[:, k, :], 1.0 / 192, EPS, ALU.mult, ALU.add)
                last.then_inc(s.y_ss_read, 1)
                dve.drain()
                dve.reciprocal(y_sq[:], y_sq[:]).then_inc(s.y_inv, 1)
                dve.wait_ge(s.y_rs, at(L, 1, 1))
                for k in range(3):
                    dve.scalar_tensor_tensor(out=tmp[k][:], in0=proj2[:, 4 + k, :], scalar=par2[:, Q_SSD + k:Q_SSD + k + 1],
                                             in1=y_sq[:, k, :], op0=ALU.mult, op1=ALU.mult)
                    dve.drain()
                    last = split(xh[:, 2 + k, :], xl[:, 2 + k, :], tmp[k][:])
                last.then_inc(s.ssd_done, 1)

            def mla(L):
                B = Block2
                for k in range(5):
                    hi, lo = (cqh[:, k, :], cql[:, k, :]) if k < 3 else (ckh[:, k - 3, :], ckl[:, k - 3, :])
                    g = par2[:, Q_CQ + k:Q_CQ + k + 1]
                    dve.tensor_scalar(hi, proj2[:, 13 + k, :], g, None, ALU.mult)
                    dve.drain()
                    last = dve.scalar_tensor_tensor(out=lo, in0=proj2[:, 13 + k, :], scalar=g, in1=hi.bitcast(F32),
                                                    op0=ALU.mult, op1=ALU.subtract)
                last.then_inc(s.c_split, 1)
                dve.wait_ge(s.c_ss, at(L, 1, 1))
                invert(tmp[0][:], B4, 1.0 / 384)
                invert(tmp[1][:], B5, 1.0 / 256).then_inc(s.c_inv, 1)
                rows = slice(64, MLA_D)
                dve.wait_ge(s.rot_psum, at(L, 1 + MLA_H, 1))
                dve.tensor_tensor(rot_sin[rows, :], B6[rows, :], rope[rows, 1, :], ALU.mult).then_inc(s.rot_read, 1)
                dve.tensor_tensor(k_rot[rows, :], proj2[rows, 12, :], rope[rows, 0, :], ALU.mult)
                dve.drain()
                dve.tensor_tensor(k_rot[rows, :], k_rot[rows, :], rot_sin[rows, :], ALU.add).then_inc(s.rot_done, 1)
                dve.wait_ge(s.c_rs, at(L, 1, 1))
                for h in range(MLA_H):
                    read_tile(B, L, T2_QB + h, q96[:, h, :], acc, rows=(0, MLA_D))
                for h in range(MLA_H):
                    t = T2_KVB + h
                    src = bank[(B.base_tile + t) % TILE_BANKS]
                    dve.wait_ge(s.tile_ready, tiles_in(B, L, t))
                    if h >= 2:
                        dve.wait_ge(s.vt_psum, at(L, MLA_H, h - 1))
                    dve.tensor_tensor(k96[0:64, h, :], src[0:64, :], var[0:64, :], ALU.mult)
                    dve.tensor_copy(k96[64:MLA_D, h, :], k_rot[64:MLA_D, :])
                    dve.tensor_tensor(v_ft[64:P, h % 2, :], src[64:P, :], var[64:P, :], ALU.mult).then_inc(s.tile_evacuated, 1)
                    dve.drain().then_inc(s.kv_done, 1)
                    if h < 2:
                        rotate(L, h)
                        continue
                    turned_v(L, h - 2)
                    rotate(L, h)
                turned_v(L, MLA_H - 2)
                turned_v(L, MLA_H - 1)

                def biggest(h, n):
                    c = 4 * h + n
                    dve.wait_ge(s.al_ready, at(L, 24, c + 1))
                    dve.tensor_reduce(small[:, 40 + n:41 + n], mb[:, n % 2, 0:(n + 1) * P], AX.X, ALU.max)
                    dve.drain()
                    dve.tensor_scalar(small[:, 32 + n:33 + n], small[:, 40 + n:41 + n], -MLA_SCALE, None, ALU.mult)\
                       .then_inc(s.am_ready, 1)

                def normed(h, n):
                    c = 4 * h + n
                    dve.wait_ge(s.ae_ready, at(L, 24, c + 1))
                    dve.reciprocal(small[:, 44 + n:45 + n], small[:, 36 + n:37 + n])
                    dve.drain()
                    w = (n + 1) * P
                    dve.tensor_scalar(prob[:, n % 2, 0:w], prob[:, n % 2, 0:w], small[:, 44 + n:45 + n], None, ALU.mult)\
                       .then_inc(s.ap_ready, 1)

                def copied(h, n):
                    c = 4 * h + n
                    dve.wait_ge(s.at_ready, at(L, 24, c + 1))
                    if h:
                        dve.wait_ge(s.ao_ready, at(L, MLA_H, h))
                    dve.tensor_copy(prob_t[:, 0:n + 1, n * P:(n + 1) * P],
                                    B6[:, 0:(n + 1) * P].rearrange("p (j q) -> p j q", j=n + 1)).then_inc(s.at_copied, 1)

                for h in range(MLA_H):
                    half = 64 * (h % 2)
                    biggest(h, 0)
                    for n in range(NT):
                        normed(h, n)
                        if n < NT - 1:
                            biggest(h, n + 1)
                        copied(h, n)
                    dve.wait_ge(s.ao_ready, at(L, MLA_H, h + 1))
                    split(xh[half:half + 64, 5 + h // 2, :], xl[half:half + 64, 5 + h // 2, :], B7[half:half + 64, :])\
                        .then_inc(s.ao_done, 1)

            def rotate(L, h):
                dve.wait_ge(s.rot_psum, at(L, 1 + MLA_H, h + 2))
                dve.tensor_tensor(rot_sin[0:MLA_D, :], mb[0:MLA_D, 2 + (h + 1) % 2, :], rope[:, 1, :], ALU.mult)\
                   .then_inc(s.rot_read, 1)
                dve.tensor_tensor(q96[:, h, :], q96[:, h, :], rope[:, 0, :], ALU.mult)
                dve.drain()
                dve.tensor_tensor(q96[:, h, :], q96[:, h, :], rot_sin[0:MLA_D, :], ALU.add).then_inc(s.rot_done, 1)
                dve.drain()

            def turned_v(L, h):
                dve.wait_ge(s.vt_psum, at(L, MLA_H, h + 1))
                dve.tensor_copy(v_tok[:, :, h * 64:h * 64 + 64], mb[:, h % 2, 0:NT * 64].rearrange("p (t c) -> p t c", t=NT))\
                   .then_inc(s.vt_copied, 1)

            with dve.Fori(0, 2) as L:
                B = Block2
                dve.tensor_copy(par2[:], p2[:, bass.ds(L * R2, R2)])
                dve.tensor_copy(d_skip_now[:, None, :], d_skip[:, bass.ds(L, 1), :])
                dve.tensor_copy(dt_now[:, 0:1], dt_bias[:, bass.ds(L, 1)])
                dve.tensor_copy(dt_now[:, 1:2], dt_a[:, bass.ds(L, 1)])
                dve.tensor_copy(bs_now[:, None, :], bs_rows[:, bass.ds(L, 1), :])
                dve.drain()
                norm(B, L, 0, par2[:, Q_MIX:Q_MIX + KT])
                for u in range(18):
                    rows = (0, MLA_D) if u == 12 else (0, P)
                    scaled_tile(B, L, 0, T2_IN + u, proj2[rows[0]:rows[1], u, :], rows=rows)
                dve.drain()
                convolve(L)
                gmlp(L)
                ssd(L)
                mla(L)
                for j in range(KT):
                    add_x(B, L, T2_OUT + j, j)
                norm(B, L, 1, par2[:, Q_MLP:Q_MLP + KT])
                for half in range(2):
                    t0 = T2_MLP + half * (HALF2 + 8)
                    with dve.Fori(0, HALF2 // 4) as i:
                        for f in range(4):
                            ta, tb = tmp[f % 2], tmp[2 + f % 2]
                            scaled_tile(B, L, 1, t0 + f, ta[:], i, 4)
                            dve.drain()
                            dve.scalar_tensor_tensor(out=tb[:], in0=ta[:], scalar=0.0, in1=ta[:], op0=ALU.max, op1=ALU.mult)
                            dve.drain()
                            j = i * 4 + f
                            split(hh[:, j, :], hl[:, j, :], tb[:]).then_inc(s.hidden_ready, 1)
                    for j in range(KT):
                        add_x(B, L, t0 + HALF2 + j, j, inc=3 if half and j == KT - 1 else 1)

            dve.drain().then_inc(s.x_final, 1)
            norm_scale(13)
            dve.wait_ge(s.rstd_ready, 13)
            for j in range(KT):
                last = dve.scalar_tensor_tensor(out=y_sb[:, j, :], in0=x_sb[:, j, :], scalar=p2[:, 2 * R2 + j:2 * R2 + j + 1],
                                                in1=rstd[:], op0=ALU.mult, op1=ALU.mult)
            last.then_inc(s.fin_y, 1)
            for c in range(2 * NT):
                t, side = c // 2, c % 2
                dve.wait_ge(s.fin_turned, c + 1)
                dve.tensor_copy(out_tok[:, t, side * S:(side + 1) * S], mb[:, c % 4, :]).then_inc(s.fin_copied, 1)


ML_OFF = [0, 512, 896, 1152]
N_SMALL = 2 * (4 + 1 + 4 + 7 + 4) + 1 + 4 + 1 + 1 + 2 + 3


def constants(np):
    pack = np.zeros((P, 8 * P), np.float32)
    r = np.arange(P)
    pack[:, C_IDENT:C_IDENT + P] = np.eye(P)
    pack[:, C_BD64:C_BD64 + P] = r[:, None] // 64 == r[None, :] // 64
    pack[:, C_DUP0:C_DUP0 + P] = r[:, None] == r[None, :] % 64
    pack[:, C_DUP1:C_DUP1 + P] = r[:, None] == 64 + r[None, :] % 64
    pack[:, C_MQS:C_MQS + P] = np.where(r[None, :] <= r[:, None], 0.0, NEG)
    pack[:, C_MSQ:C_MSQ + P] = np.where(r[None, :] >= r[:, None], 0.0, NEG)
    for i in range(16):
        pack[80 + i, C_ROT + 64 + i] = -1.0
        pack[64 + i, C_ROT + 80 + i] = 1.0
    pack[:, C_TRI:C_TRI + P] = r[None, :] >= r[:, None]
    dist = 255 - np.arange(TOEP)
    far = 16 + (np.log(np.maximum(dist, 1) / 16) / np.log(128 / 16) * 16).astype(np.int32)
    bucket = np.where(dist < 16, dist, np.minimum(far, 31))
    inside = (dist >= 0) & (dist < P)
    onehot = ((np.arange(32)[:, None] == bucket[None, :]) & inside[None, :]).astype(np.float32)
    pad = np.broadcast_to(np.where(inside, 0.0, NEG).astype(np.float32), (P, TOEP)).copy()
    rope = np.zeros((MLA_D, 2, S), np.float32)
    rope[:, 0] = 1.0
    inv_freq = np.power(np.float32(10000.0), -np.arange(16, dtype=np.float32) / np.float32(16))
    ang = np.arange(S, dtype=np.float32)[:, None] * inv_freq[None, :]
    for part in (64, 80):
        rope[part:part + 16, 0] = np.cos(ang).T
        rope[part:part + 16, 1] = np.sin(ang).T
    return {"const_pack": pack, "onehot": onehot, "pad": pad, "rope_pack": rope}


_INS = ['x', 'p', 'ffn1_norm', 'ffn1_wi', 'ffn1_wo', 'mix_norm', 'w_in', 'b_igate', 'b_fgate', 'ml_out_norm', 'q_norm',
        'k_norm', 'sinks', 'rel_bias', 'w_a', 'w_b', 'w_out', 'ffn2_norm', 'ffn2_wi', 'ffn2_wo', 'ple_norm', 'w_ple_gate',
        'w_ple', 'norm_mix_g_2', 'w_in_2', 'gmlp_v_norm_g_2', 'gmlp_w_s_2', 'gmlp_b_s_2', 'ssd_conv_w_2', 'ssd_conv_b_2',
        'ssd_dt_bias_2', 'ssd_a_log_2', 'ssd_d_2', 'ssd_norm_g_2', 'mla_q_norm_g_2', 'mla_w_qb_2', 'mla_kv_norm_g_2',
        'mla_w_kvb_2', 'w_out_2', 'norm_mlp_g_2', 'mlp_w1_2', 'mlp_w2_2', 'final_norm_g_2']


def kernel(**inputs):
    import numpy as _np
    import concourse.bacc as _bacc
    from concourse import mybir as _mybir
    from concourse.bass_utils import run_bass_kernel_spmd as _run

    nc = _bacc.Bacc("TRN2", target_bir_lowering=False, num_devices=1)
    arrays, args = {}, {}
    for name, value in [(n, inputs[n]) for n in _INS] + list(constants(_np).items()):
        v = _np.ascontiguousarray(value)
        arrays[f"in_{name}_dram"] = v
        args[name] = nc.dram_tensor(f"in_{name}_dram", v.shape, _mybir.dt.from_np(v.dtype), kind="ExternalInput").ap()
    args["out"] = nc.dram_tensor("out_dram", (1, S, D), _mybir.dt.float32, kind="ExternalOutput").ap()
    program(nc, args)
    r = _run(nc, [arrays], core_ids=[0])
    return r.results[0]["out_dram"]
```

```python
from contextlib import ExitStack

import concourse.bass as bass
from concourse import mybir

F32 = mybir.dt.float32
F32R = mybir.dt.float32r
ALU = mybir.AluOpType
ACT = mybir.ActivationFunctionType
AX = mybir.AxisListType

P = 128
S = 512
D = 1024
KT = D // P
NT = S // P
EPS = 1e-6
NEG = -1e30

D_FF = 2816
FT = D_FF // P
ML_H = 4
SW_H = 8
SW_KV = 2
SW_G = SW_H // SW_KV
GATE_COL = 1536
SQ_COL = 1544
SK_COL = 2056
SV_COL = 2184
GA_COL = 2312
GB_COL = 3336
FT2 = 4 * D // P
HALF2 = FT2 // 2
SSD_H = 6
MLA_H = 6
MLA_D = 96
DT_COL = 1536
CQ_COL = 1542
KR_COL = 2182
MLA_SCALE = 1.0 / float(MLA_D) ** 0.5

RAW_SLOTS = 2
SPLIT_SLOTS = 4
TILE_BANKS = 4
AHEAD = SPLIT_SLOTS - 1
SLAB = 1024

B1_SLABS, B1_TILES = 192, 180
B2_SLABS, B2_TILES = 96, 88
S_FFN1, S_IN, S_GATE, S_A, S_B, S_OUT, S_FFN2, S_PLE = 0, 66, 84, 100, 104, 108, 116, 182
T_FFN1, T_IN, T_GATE, T_A, T_B, T_OUT, T_FFN2, T_PLE = 0, 52, 70, 86, 94, 102, 110, 162
S2_IN, S2_QB, S2_KVB, S2_OUT, S2_MLP = 0, 18, 21, 24, 32
T2_IN, T2_QB, T2_KVB, T2_OUT, T2_MLP = 0, 18, 24, 30, 38
ORDER2 = [0, 1, 2, 3, 7, 8, 9, 10, 11, 12, 4, 5, 6, 13, 14, 15, 16, 17]
U_DT, U_Z, U_C = 9, 10, 13

R_FFN1, R_MIX, R_FFN2, R_PLE, R_MLOUT, R_QN, R_KN, R1 = 0, 8, 16, 24, 32, 36, 37, 38
Q_MIX, Q_MLP, Q_CQ, Q_CKV, Q_SSD, Q_GV, Q_CB, Q_CW, R2 = 0, 8, 16, 19, 21, 24, 26, 31, 51

C_IDENT, C_SEL, C_DUP0, C_DUP1, C_MQS, C_MSQ, C_ROT, C_TRI, C_BACK = [P * n for n in range(9)]
CONSTS = 9 * P

TOEP = 384


class Block1:
    base_slab, slabs, base_tile, tiles = 0, B1_SLABS, 0, B1_TILES
    norms, base_norm = 4, 0


class Block2:
    base_slab, slabs = 2 * B1_SLABS, B2_SLABS
    base_tile, tiles = 2 * B1_TILES, B2_TILES
    norms, base_norm = 2, 8


def at(layer, per_layer, const, i=None, step=0):
    e = const if layer is None else layer * per_layer + const
    return e if i is None else e + i * step


def program(nc, a):
    ctx = ExitStack()
    with ctx:
        cursor = [16512]

        def place(name, shape, dt=F32, offset=None):
            size = 4
            for n in shape[1:]:
                size *= n
            if offset is None:
                offset = cursor[0]
                cursor[0] += (size + 31) // 32 * 32
            return nc.alloc_sbuf_tensor_at(name, shape, dt, offset=offset)

        def sem(name):
            return ctx.enter_context(nc.semaphore(name))

        x_sb = place("x_sb", [P, KT, S])
        xh = place("xh", [P, KT, S], F32R)
        xl = place("xl", [P, KT, S], F32R)
        raw = [place(f"raw{n}", [P, SLAB]) for n in range(RAW_SLOTS)]
        wh = [place(f"wh{n}", [P, SLAB], F32R) for n in range(SPLIT_SLOTS)]
        wl = [place(f"wl{n}", [P, SLAB], F32R) for n in range(SPLIT_SLOTS)]
        tmp = [place(f"tmp{n}", [P, S]) for n in range(4)]
        rstd = place("rstd", [P, S])
        acc = place("acc", [P, S])
        var = place("var", [P, S])
        const = place("const", [P, CONSTS])
        sel4 = place("sel4", [ML_H, P])
        ones = place("ones", [P, P])
        p1 = place("p1", [P, 2 * R1])
        p2 = place("p2", [P, 2 * R2 + KT])
        par1 = place("par1", [P, R1])
        par2 = place("par2", [P, R2])
        gate_raw = place("gate_raw", [P, KT, 8])
        gate_h = place("gate_h", [P, KT, 8], F32R)
        gate_l = place("gate_l", [P, KT, 8], F32R)
        b_gate = place("b_gate", [ML_H, 2, 2])
        b_gate_now = place("b_gate_now", [ML_H, 2])
        sinks = place("sinks", [P, 2, SW_H])
        sinks_now = place("sinks_now", [P, SW_H])
        c_col = place("c_col", [P, NT, ML_H])
        small = place("small", [P, 64])
        d_skip = place("d_skip", [P, 2, 3])
        d_skip_now = place("d_skip_now", [P, 3])
        dt_bias = place("dt_bias", [SSD_H, 2])
        dt_a = place("dt_a", [SSD_H, 2])
        dt_now = place("dt_now", [SSD_H, 2])
        bs_rows = place("bs_rows", [4, 2, P])
        bs_now = place("bs_now", [4, P])
        a_col = place("a_col", [P, NT, SSD_H])
        dt_col = place("dt_col", [P, NT, SSD_H])
        bias_at = cursor[0]
        bias = place("bias", [P, SW_H, 2 * P])
        rope = place("rope", [MLA_D, 2, S], offset=bias_at)
        region = cursor[0]

        def at_kb(name, kb, shape, dt=F32):
            return place(name, shape, dt, offset=region + int(kb * 1024))

        hh = at_kb("hh", 0, [P, FT, S], F32R)
        hl = at_kb("hl", 44, [P, FT, S], F32R)
        squares = at_kb("squares", 0, [P, KT, S])
        x_tok = at_kb("x_tok", 0, [P, NT, D])
        rows1 = at_kb("rows1", 16, [2 * R1, P])
        rows2 = at_kb("rows2", 17, [2 * R2 + KT, P])
        onehot = at_kb("onehot", 18, [32, TOEP])
        pad = at_kb("pad", 20, [P, TOEP])
        rel = at_kb("rel", 22, [32, SW_H])
        toep = at_kb("toep", 24, [P, SW_H, TOEP])
        proj = at_kb("proj", 0, [P, 18, S])
        hah = at_kb("hah", 0, [P, ML_H, S], F32R)
        hal = at_kb("hal", 8, [P, ML_H, S], F32R)
        hbh = at_kb("hbh", 16, [P, 4, S], F32R)
        mv_tok = at_kb("mv_tok", 36, [P, NT, S])
        sv_tok = at_kb("sv_tok", 36, [P, NT, P])
        kk = at_kb("kk", 38, [P, SW_KV, S])
        num_sb = at_kb("num_sb", 50, [P, ML_H, S])
        hbl = at_kb("hbl", 50, [P, 4, S], F32R)
        ml_w = at_kb("ml_w", 58, [P, 1280])
        ml_p = at_kb("ml_p", 63, [P, 1280])
        neg_m = at_kb("neg_m", 76, [P, S])
        neg_md = at_kb("neg_md", 78, [P, S])
        gate = [at_kb(f"gate{n}", kb, [P, S])
                for n, kb in enumerate((80, 82, 84, 86, 44, 46, 48, 42, 58, 60, 62, 64, 66))] + tmp[0:3]
        ml_rows = [at_kb(f"ml_row{n}", 68 + 2 * n, [ML_H, S]) for n in range(4)]
        ml_rows += [at_kb(f"ml_row{4 + n}", 58 + 2 * n, [ML_H, S]) for n in range(5)]
        qk_sq = at_kb("qk_sq", 58, [P, 5, S])
        lg = at_kb("lg", 68, [P, 2, SW_G, 2 * P])
        pt_sb = at_kb("pt_sb", 76, [P, 2, SW_G, P])
        gate_sg = at_kb("gate_sg", 0, [P, KT, S])
        p_tok = at_kb("p_tok", 16, [P, NT, 2 * P])
        pth = at_kb("pth", 20, [P, 2, S], F32R)
        ptl = at_kb("ptl", 24, [P, 2, S], F32R)
        proj2 = at_kb("proj2", 0, [P, 18, S])
        q96 = at_kb("q96", 0, [MLA_D, MLA_H, S])
        k96 = at_kb("k96", 12, [MLA_D, MLA_H, S])
        conv = at_kb("conv", 36, [P, 5, S])
        xs_tok = at_kb("xs_tok", 46, [P, NT, 384])
        v_tok = at_kb("v_tok", 46, [P, NT, 384])
        cqh = at_kb("cqh", 52, [P, 3, S], F32R)
        cql = at_kb("cql", 58, [P, 3, S], F32R)
        ckh = at_kb("ckh", 64, [P, 2, S], F32R)
        ckl = at_kb("ckl", 68, [P, 2, S], F32R)
        gv_sq = at_kb("gv_sq", 72, [P, 2, S])
        gv_tok = at_kb("gv_tok", 76, [P, NT, 2 * P])
        ws_t = at_kb("ws_t", 80, [P, 4, P])
        ws_raw = at_kb("ws_raw", 82, [P, 4, P])
        cb = at_kb("cb", 72, [P, 1280])
        sd_w = at_kb("sd_w", 77, [P, 1280])
        sd_p = at_kb("sd_p", 82, [P, 1280])
        y_sq = at_kb("y_sq", 77, [P, 3, S])
        c_sq = at_kb("c_sq", 14, [P, 5, S])
        k_rot = at_kb("k_rot", 26, [P, S])
        rot_sin = at_kb("rot_sin", 28, [P, S])
        v_ft = at_kb("v_ft", 30, [P, 2, S])
        prob = at_kb("prob", 60, [P, 4, S])
        prob_t = [at_kb(f"prob_t{n}", kb, [P, NT, S]) for n, kb in ((0, 72), (1, 52))]
        y_sb = at_kb("y_sb", 16, [P, KT, S])
        out_tok = at_kb("out_tok", 32, [P, NT, D])
        assert region + 88 * 1024 <= nc.sbuf_usable_end, (region + 88 * 1024, nc.sbuf_usable_end)

        ident = const[:, C_IDENT:C_IDENT + P]
        dup = [const[:, c:c + P] for c in (C_DUP0, C_DUP1)]
        mask_qs = const[:, C_MQS:C_MQS + P]
        mask_sq = const[:, C_MSQ:C_MSQ + P]
        rot96 = const[0:MLA_D, C_ROT:C_ROT + MLA_D]
        tri_st = const[:, C_TRI:C_TRI + P]

        bank = [ctx.enter_context(nc.psum_tensor(f"bank{n}", [P, S], F32)) for n in range(4)]
        mb = ctx.enter_context(nc.psum_tensor("mb", [P, 4, S], F32))
        B4, B5, B6, B7 = (mb[:, n, :] for n in range(4))

        scratch = nc.dram_tensor("toeplitz_rows", [SW_H, P, TOEP], F32, kind="Internal").ap()

        names = """split_done slab_used hi_ready tile_ready tile_evacuated setup_x setup_const setup_small
            setup_t setup_copied rel_psum toep_row toep_out toep_in consts_ready
            x_final sq_ready ss_ready ss_psum inv_var rstd_ready xl_ready
            silu_done hidden_ready gate_landed gate_split gates_psum gate_pre log1p ml_rows_done emt_done
            v_turned v_copied c_turned c_copied bc_ready bc_copied w_ready sc_ready p_ready pv_done abs_done
            head_done num_sq ml_ss ml_inv ml_rs ml_bc ml_bc_read mo_done ha_ready
            qk_squared qk_ss qk_inv qk_rs qk_bc qk_bc_read qk_normed kk_psum kk_copied
            lg_ready lg_read mx_ready ex_ready pn_ready pt_ready pt_copied o_ready o_done
            sig_done mixed_ready p_landed p_turned pt_split sg_done kr_landed
            gelu_done gv_squared gv_ss gv_inv gv_rs gv_normed gv_turned gv_copied ws_landed ws_turned ws_copied
            gm_psum gm_done conv_done conv_silu z_silu xs_turned xs_copied
            dt_pre dt_log dt_rows_done dcol_turned dcol_copied cb_ready cb_copied abc_ready abc_copied sw_ready
            sp_ready y_psum y_done y_squared y_ss y_inv y_rs y_bc ssd_done
            c_squared c_ss c_inv c_rs c_split rope_landed rot_psum rot_read rot_done
            kv_done vt_psum vt_copied al_ready am_ready ae_ready ap_ready at_ready at_copied ao_ready ao_done
            fin_y fin_turned fin_copied stored""".split()
        sm = {n: sem(n) for n in names}
        raw_landed = [sem(f"raw_landed{n}") for n in range(RAW_SLOTS)]
        s = type("Sems", (), sm)

        def tiles_out(B, L, t, i=None, step=0):
            return at(L, B.tiles, B.base_tile + t + 1 + TILE_BANKS, i, step)

        def tiles_in(B, L, t, i=None, step=0):
            return at(L, B.tiles, B.base_tile + t + 1, i, step)

        def norm_no(B, L, k):
            return at(L, B.norms, B.base_norm + k + 1)

        block = ctx.enter_context(nc.Block())

        @block.sync
        def _(sp):
            def load(B, L, n, view, src, i=None, step=0):
                need = sp.lower_val(at(L, B.slabs, B.base_slab + n + 1, i, step))
                sp.dma_start(view(raw[n % RAW_SLOTS]), src).wait_op(s.split_done, need, "sem-ge")\
                  .then_inc(raw_landed[n % RAW_SLOTS], 16)

            def as3(kt, c):
                return lambda r: r[:, 0:kt * c].rearrange("p (k c) -> p k c", k=kt)

            def cols(w, L, c0, width, i=None, step=0):
                c = c0 if i is None else i * step + c0
                sl = slice(c0, c0 + width) if i is None else bass.ds(c, width)
                return w[bass.ds(L, 1), :, sl].rearrange("l (k p) c -> p (l k) c", p=P)

            def rows2c(w, L, r0, c0, i=None, step=0):
                sl = slice(r0, r0 + 2 * P) if i is None else bass.ds(i * step + r0, 2 * P)
                return w[bass.ds(L, 1), sl, c0:c0 + S].rearrange("l (k p) c -> p (l k) c", p=P)

            sp.dma_start(const[:], a["const_pack"]).then_inc(s.setup_const, 16)
            sp.dma_start(x_tok[:], a["x"].rearrange("b (t p) d -> p (b t) d", p=P)).then_inc(s.setup_x, 16)

            def row(dst, r0, n, src):
                sp.dma_start(dst[r0:r0 + n, :], src.rearrange("(r c) -> r c", c=P)).then_inc(s.setup_small, 16)

            for l in range(2):
                for r0, n, name in ((R_FFN1, 8, "ffn1_norm"), (R_MIX, 8, "mix_norm"), (R_FFN2, 8, "ffn2_norm"),
                                    (R_PLE, 8, "ple_norm")):
                    row(rows1, l * R1 + r0, n, a[name][l])
                sp.dma_start(rows1[l * R1 + R_MLOUT:l * R1 + R_MLOUT + ML_H, :], a["ml_out_norm"][l])\
                  .then_inc(s.setup_small, 16)
                for r0, name in ((R_QN, "q_norm"), (R_KN, "k_norm")):
                    for half in range(2):
                        sp.dma_start(rows1[l * R1 + r0:l * R1 + r0 + 1, half * 64:half * 64 + 64],
                                     a[name][l:l + 1]).then_inc(s.setup_small, 16)
                for r0, n, name in ((Q_MIX, 8, "norm_mix_g_2"), (Q_MLP, 8, "norm_mlp_g_2"), (Q_CQ, 3, "mla_q_norm_g_2"),
                                    (Q_CKV, 2, "mla_kv_norm_g_2"), (Q_SSD, 3, "ssd_norm_g_2"),
                                    (Q_GV, 2, "gmlp_v_norm_g_2"), (Q_CB, 5, "ssd_conv_b_2")):
                    row(rows2, l * R2 + r0, n, a[name][l])
                for k in range(4):
                    row(rows2, l * R2 + Q_CW + 5 * k, 5, a["ssd_conv_w_2"][l, k])
            row(rows2, 2 * R2, KT, a["final_norm_g_2"])
            with nc.allow_non_contiguous_dma("parameters of a few bytes"):
                sp.dma_start(b_gate[:, :, 0:1], a["b_igate"].rearrange("l (h o) -> h l o", o=1)).then_inc(s.setup_small, 16)
                sp.dma_start(b_gate[:, :, 1:2], a["b_fgate"].rearrange("l (h o) -> h l o", o=1)).then_inc(s.setup_small, 16)
                sp.dma_start(dt_bias[:, :, None], a["ssd_dt_bias_2"].rearrange("l (h o) -> h l o", o=1))\
                  .then_inc(s.setup_small, 16)
                sp.dma_start(dt_a[:, :, None], a["ssd_a_log_2"].rearrange("l (h o) -> h l o", o=1)).then_inc(s.setup_small, 16)
                sp.dma_start(bs_rows[:], a["gmlp_b_s_2"].rearrange("l h t -> h l t")).then_inc(s.setup_small, 16)
                sp.dma_start(sinks[:].rearrange("p l h -> p (l h)"),
                             a["sinks"].rearrange("(o l) h -> o (l h)", o=1).to_broadcast([P, 2 * SW_H]))\
                  .then_inc(s.setup_small, 16)
                for half in range(2):
                    src = a["ssd_d_2"].rearrange("l (i two) -> two l i", two=2)[half:half + 1]
                    sp.dma_start(d_skip[half * 64:half * 64 + 64], src.to_broadcast([64, 2, 3])).then_inc(s.setup_small, 16)
                sp.dma_start(rel[:], a["rel_bias"]).then_inc(s.setup_small, 16)
                sp.dma_start(sel4[:], a["sel4"]).then_inc(s.setup_small, 16)
                sp.dma_start(onehot[:], a["onehot"]).then_inc(s.setup_small, 16)
                sp.dma_start(pad[:], a["pad"]).then_inc(s.setup_small, 16)
            def ffn(L, wi, wo, n):
                with sp.Fori(0, FT // 2) as i:
                    for f in range(2):
                        for part in range(2):
                            load(Block1, L, n + 2 * f + part, as3(KT, P),
                                 cols(wi, L, part * D_FF + f * P, P, i, 2 * P), i, 4)
                for half in range(2):
                    n0 = n + 2 * FT + half * (FT // 2)
                    with sp.Fori(0, 2) as i:
                        for q in range(4):
                            load(Block1, L, n0 + q, as3(2, S), rows2c(wo, L, q * 2 * P, half * S, i, 8 * P), i, 4)
                    for q in range(8, FT // 2):
                        load(Block1, L, n0 + q, as3(2, S), rows2c(wo, L, q * 2 * P, half * S))

            with sp.Fori(0, 2) as L:
                need = sp.lower_val(L + 1)
                with nc.allow_non_contiguous_dma("eight columns"):
                    sp.dma_start(gate_raw[:], cols(a["w_in"], L, GATE_COL, 8)).wait_op(s.gate_split, need, "sem-ge")\
                      .then_inc(s.gate_landed, 16)
                ffn(L, a["ffn1_wi"], a["ffn1_wo"], S_FFN1)
                with sp.Fori(0, 3) as i:
                    for u in range(4):
                        load(Block1, L, S_IN + u, as3(KT, P), cols(a["w_in"], L, u * P, P, i, 4 * P), i, 4)
                for u in range(6):
                    load(Block1, L, S_IN + 12 + u, as3(KT, P), cols(a["w_in"], L, SQ_COL + u * P, P))
                with sp.Fori(0, 4) as i:
                    for u in range(4):
                        load(Block1, L, S_GATE + u, as3(KT, P), cols(a["w_in"], L, GA_COL + u * P, P, i, 4 * P), i, 4)
                for n, w in ((S_A, "w_a"), (S_B, "w_b")):
                    for u in range(4):
                        load(Block1, L, n + u, as3(4, 2 * P), cols(a[w], L, u * 2 * P, 2 * P))
                with sp.Fori(0, 2) as i:
                    for j in range(4):
                        load(Block1, L, S_OUT + j, as3(KT, P), cols(a["w_out"], L, j * P, P, i, 4 * P), i, 4)
                ffn(L, a["ffn2_wi"], a["ffn2_wo"], S_FFN2)
                with sp.Fori(0, 2) as i:
                    for j in range(4):
                        load(Block1, L, S_PLE + j, as3(KT, P), cols(a["w_ple_gate"], L, j * P, P, i, 4 * P), i, 4)
                for d in range(2):
                    load(Block1, L, S_PLE + 8 + d, as3(2, S), cols(a["w_ple"], L, d * S, S))
                need = sp.lower_val(tiles_out(Block1, L, T_FFN2 + 51))
                sp.dma_start(p_tok[:], a["p"][bass.ds(L, 1), 0].rearrange("l (t p) c -> p (l t) c", p=P))\
                  .wait_op(s.tile_evacuated, need, "sem-ge").then_inc(s.p_landed, 16)

            sp.wait_ge(s.lg_read, 16)
            sp.dma_start(rope[:], a["rope_pack"]).then_inc(s.rope_landed, 16)
            with sp.Fori(0, 2) as L:
                B = Block2
                w_in = a["w_in_2"]
                need = sp.lower_val(at(L, B.tiles, B.base_tile + TILE_BANKS))
                sp.dma_start(ws_raw[:], a["gmlp_w_s_2"][bass.ds(L, 1)].rearrange("l h t s -> t (l h) s"))\
                  .wait_op(s.tile_evacuated, need, "sem-ge").then_inc(s.ws_landed, 16)
                view = lambda c0, c1: (lambda r: r[:, 0:KT * MLA_D].rearrange("p (k c) -> p k c", k=KT)[:, :, c0:c1])
                for u, tile in enumerate(ORDER2):
                    if u == U_DT:
                        with nc.allow_non_contiguous_dma("six columns"):
                            load(B, L, S2_IN + u, view(0, SSD_H), cols(w_in, L, DT_COL, SSD_H))
                            sp.dma_start(view(64, MLA_D)(raw[(S2_IN + u) % RAW_SLOTS]), cols(w_in, L, KR_COL, 32))\
                              .then_inc(s.kr_landed, 16)
                    else:
                        c0 = tile * P if tile < 12 else CQ_COL + (tile - 13) * P
                        load(B, L, S2_IN + u, as3(KT, P), cols(w_in, L, c0, P))
                for u in range(3):
                    load(B, L, S2_QB + u, as3(3, 2 * MLA_D), cols(a["mla_w_qb_2"], L, u * 2 * MLA_D, 2 * MLA_D))
                for u in range(3):
                    load(B, L, S2_KVB + u, as3(2, 2 * P), cols(a["mla_w_kvb_2"], L, u * 2 * P, 2 * P))
                with sp.Fori(0, 2) as i:
                    for j in range(4):
                        load(B, L, S2_OUT + j, as3(KT, P), cols(a["w_out_2"], L, j * P, P, i, 4 * P), i, 4)
                for half in range(2):
                    n0 = S2_MLP + half * 2 * HALF2
                    with sp.Fori(0, HALF2 // 4) as i:
                        for f in range(4):
                            load(B, L, n0 + f, as3(KT, P),
                                 cols(a["mlp_w1_2"], L, (half * HALF2 + f) * P, P, i, 4 * P), i, 4)
                    for dh in range(2):
                        with sp.Fori(0, 2) as i:
                            for q in range(4):
                                load(B, L, n0 + HALF2 + 8 * dh + q, as3(2, S),
                                     rows2c(a["mlp_w2_2"], L, half * HALF2 * P + q * 2 * P, dh * S, i, 8 * P), i, 4)

            for t in range(NT):
                sp.wait_ge(s.fin_copied, 2 * t + 2)
                sp.dma_start(a["out"][0, t * P:(t + 1) * P, :], out_tok[:, t, :]).then_inc(s.stored, 16)
            sp.wait_ge(s.stored, 16 * NT)

        @block.gpsimd
        def _(gp):
            gp.memset(ones[:], 1.0).then_inc(s.consts_ready, 1)
            gp.sem_inc(s.split_done, RAW_SLOTS)
            gp.sem_inc(s.slab_used, AHEAD)
            gp.sem_inc(s.tile_evacuated, TILE_BANKS)
            gp.sem_inc(s.gate_split, 1)
            total = 2 * (B1_SLABS + B2_SLABS)
            with gp.Fori(0, total // SPLIT_SLOTS) as n:
                for j in range(SPLIT_SLOTS):
                    gp.wait_ge(s.hi_ready, n * SPLIT_SLOTS + j + 1)
                    gp.tensor_tensor(wl[j][:], raw[j % RAW_SLOTS][:], wh[j][:].bitcast(F32), ALU.subtract)\
                      .then_inc(s.split_done, 1)

        @block.tensor
        def _(pe):
            def take_slab(B, L, n, i=None, step=0):
                pe.wait_ge(s.split_done, at(L, B.slabs, B.base_slab + n + 1 + RAW_SLOTS, i, step))
                return wh[n % SPLIT_SLOTS], wl[n % SPLIT_SLOTS]

            def open_tile(B, L, t, i=None, step=0):
                pe.wait_ge(s.tile_evacuated, at(L, B.tiles, B.base_tile + t + 1, i, step))
                return bank[(B.base_tile + t) % TILE_BANKS]

            def three(out, ah, al, bh, bl, first, last, new=False):
                one = pe.matmul(out, ah, bh, start=first, stop=False)
                if new:
                    one.then_inc(s.slab_used, 1)
                pe.matmul(out, ah, bl, start=False, stop=False)
                return pe.matmul(out, al, bh, start=False, stop=last)

            def unit(B, L, n, t, rh, rl, i=None, step=0, tstep=None, wait_k=None, width=P, kts=KT, c0=0, pitch=P,
                     new=True, inc=1, part_ready=s.xl_ready):
                tstep = step if tstep is None else tstep
                if new:
                    take_slab(B, L, n, i, step)
                out = open_tile(B, L, t, i, tstep)
                h, l = wh[n % SPLIT_SLOTS], wl[n % SPLIT_SLOTS]
                for k in range(kts):
                    if wait_k is not None:
                        pe.wait_ge(part_ready, wait_k(k))
                    c = k * pitch + c0
                    first = pe.matmul(out[0:width, :], h[:, c:c + width], rh[:, k, :], start=k == 0, stop=False)
                    if new and k == 0:
                        first.then_inc(s.slab_used, 1)
                    pe.matmul(out[0:width, :], h[:, c:c + width], rl[:, k, :], start=False, stop=False)
                    if k < kts - 1:
                        pe.matmul(out[0:width, :], l[:, c:c + width], rh[:, k, :], start=False, stop=False)
                last = pe.matmul(out[0:width, :], l[:, c:c + width], rh[:, kts - 1, :], start=False, stop=True)
                last.then_inc(s.tile_ready, inc)
                return last

            def xl_wait(B, L, k):
                base = B.base_norm * KT
                return lambda kt: at(L, B.norms * KT, base + k * KT + kt + 1)

            def sum_squares(B, L, k):
                pe.wait_ge(s.ss_ready, norm_no(B, L, k))
                pe.matmul(B4, ones[:], acc[:], start=True, stop=True).then_inc(s.ss_psum, 1)

            def turn(out, in_, k=P):
                if k == P:
                    return pe.transpose(out, in_, ident)
                return pe.matmul(out, in_, const[0:k, C_IDENT:C_IDENT + k], start=True, stop=True)

            pe.wait_ge(s.setup_const, 16)
            pe.wait_ge(s.consts_ready, 1)
            pe.wait_ge(s.setup_x, 16)
            for j in range(KT):
                if j >= 4:
                    pe.wait_ge(s.setup_copied, j - 3)
                for t in range(NT):
                    last = turn(mb[:, j % 4, t * P:(t + 1) * P], x_tok[:, t, j * P:(j + 1) * P])
                last.then_inc(s.setup_t, 1)
            pe.wait_ge(s.setup_small, 16 * N_SMALL)
            pe.wait_ge(s.setup_copied, 6)
            turn(B4[:, 0:2 * R1], rows1[:], 2 * R1)
            turn(B5[:, 0:2 * R2 + KT], rows2[:], 2 * R2 + KT).then_inc(s.setup_t, 1)
            pe.wait_ge(s.setup_copied, 8)
            for h in range(SW_H):
                if h >= 2:
                    pe.wait_ge(s.toep_row, h - 1)
                pe.matmul(mb[:, 2 + h % 2, 0:TOEP], rel[:, h:h + 1].to_broadcast([32, P]), onehot[:],
                          start=True, stop=True).then_inc(s.rel_psum, 1)

            def ffn(L, k, n, t, wh_count):
                w = xl_wait(Block1, L, k)
                for u in range(4):
                    unit(Block1, L, n + u, t + u, xh, xl, wait_k=w if u == 0 else None)
                    if u == 1:
                        sum_squares(Block1, L, k)
                with pe.Fori(1, FT // 2) as i:
                    for u in range(4):
                        unit(Block1, L, n + u, t + u, xh, xl, i, 4)
                for half in range(2):
                    n0, t0 = n + 2 * FT + half * (FT // 2), t + 2 * FT + 4 * half

                    def down(q, i=None):
                        take_slab(Block1, L, n0 + q, i, 4)
                        h, l = wh[(n0 + q) % SPLIT_SLOTS], wl[(n0 + q) % SPLIT_SLOTS]
                        if half == 0:
                            pe.wait_ge(s.hidden_ready, at(L, 2 * FT, wh_count + 2 * q + 2, i, 8))
                        for kk_ in range(2):
                            kt = 2 * q + kk_ if i is None else i * 8 + (2 * q + kk_)
                            first, end = i is None and q == 0 and kk_ == 0, q == FT // 2 - 1 and kk_ == 1
                            for d in range(4):
                                if first:
                                    open_tile(Block1, L, t0 + d)
                                out = bank[(t0 + d) % TILE_BANKS][:]
                                c = kk_ * S + d * P
                                last = three(out, h[:, c:c + P], l[:, c:c + P], hh[:, kt, :], hl[:, kt, :], first, end,
                                             new=kk_ == 0 and d == 0)
                                if end:
                                    last.then_inc(s.tile_ready, 1)

                    down(0)
                    with pe.Fori(0, 2) as i:
                        for q in range(1, 5):
                            down(q, i)
                    for q in range(9, FT // 2):
                        down(q)

            def mlstm(L):
                pe.wait_ge(s.gate_split, at(L, 1, 2))
                pe.wait_ge(s.inv_var, norm_no(Block1, L, 1))
                for g, out in ((0, B4), (1, B5)):
                    for k in range(KT):
                        last = three(out[0:ML_H, :], gate_h[:, k, 4 * g:4 * g + 4], gate_l[:, k, 4 * g:4 * g + 4],
                                     xh[:, k, :], xl[:, k, :], k == 0, k == KT - 1)
                last.then_inc(s.gates_psum, 1)
                pe.wait_ge(s.tile_evacuated, tiles_out(Block1, L, T_IN + 11))
                for t in range(NT):
                    if t >= 2:
                        pe.wait_ge(s.v_copied, at(L, 5, t - 1))
                    for j in range(4):
                        last = turn(mb[:, 2 + t % 2, j * P:(j + 1) * P], proj[:, 4 + j, t * P:(t + 1) * P])
                    last.then_inc(s.v_turned, 1)
                for u in range(12, 15):
                    more_in(L, u)
                pe.wait_ge(s.ml_rows_done, at(L, 1, 1))
                for t in range(NT):
                    last = turn(B5[:, ML_H * t:ML_H * t + ML_H], ml_rows[5][:, t * P:(t + 1) * P], ML_H)
                last.then_inc(s.c_turned, 1)
                more_in(L, 15)
                pe.wait_ge(s.emt_done, at(L, 1, 1))

                def minus_m(h):
                    if h:
                        pe.wait_ge(s.bc_copied, at(L, ML_H, h))
                    if h < ML_H:
                        lhs, rhs = const[0:ML_H, C_IDENT + h:C_IDENT + h + 1].to_broadcast([ML_H, P]), acc[0:ML_H, :]
                    else:
                        lhs, rhs = sel4[:], var[0:ML_H, :]
                    pe.matmul(B4, lhs, rhs, start=True, stop=True).then_inc(s.bc_ready, 1)

                minus_m(0)
                for u in range(16, 18):
                    more_in(L, u)
                for h in range(ML_H):
                    tile, half = h // 2, 64 * (h % 2)

                    def scores(j):
                        if h or j:
                            pe.wait_ge(s.p_ready, at(L, 16, 4 * h + j))
                        else:
                            pe.wait_ge(s.c_copied, at(L, 1, 1))
                        pe.matmul(B5[:, 0:S - j * P], proj[half:half + 64, 2 + tile, j * P:(j + 1) * P],
                                  proj[half:half + 64, tile, j * P:S], start=True, stop=True).then_inc(s.sc_ready, 1)

                    def values(j):
                        if j == 0 and h:
                            pe.wait_ge(s.num_sq, at(L, ML_H, h))
                        if j == 0 and not h:
                            pe.wait_ge(s.v_copied, at(L, 5, 4))
                        pe.wait_ge(s.p_ready, at(L, 16, 4 * h + j + 1))
                        o = ML_OFF[j]
                        pj = ml_p[:, o:o + S - j * P]
                        pe.matmul(B6[:, j * P:S], mv_tok[:, j, h * P:(h + 1) * P], pj, start=j == 0, stop=j == 3)
                        pe.matmul(B7[32 * h:32 * h + 32, j * P:S], ones[:, 0:32], pj, start=j == 0, stop=j == 3)\
                          .then_inc(s.pv_done, 1)

                    scores(0)
                    for j in range(1, 4):
                        scores(j)
                        values(j - 1)
                    minus_m(h + 1)
                    values(3)
                    gate_unit(L, 2 * h)
                    if h < ML_H - 1:
                        gate_unit(L, 2 * h + 1)
                pe.wait_ge(s.num_sq, at(L, ML_H, ML_H))
                for h in range(ML_H):
                    last = pe.matmul(B5[32 * h:32 * h + 32, :], ones[:, 0:32], tmp[h][:], start=True, stop=True)
                last.then_inc(s.ml_ss, 1)

            def more_in(L, u):
                unit(Block1, L, S_IN + u, T_IN + u, xh, xl)

            def gate_unit(L, g):
                unit(Block1, L, S_GATE + g, T_GATE + g, xh, xl)

            def branch(L, n, t, h, l):
                for d in range(2):
                    unit(Block1, L, n, t + d, h, l, kts=4, c0=d * P, pitch=2 * P, new=d == 0)

            def swa(L):
                pe.wait_ge(s.qk_squared, at(L, 1, 1))
                for u in range(5):
                    out = B6[32 * u:32 * u + 32, :] if u < 4 else B7[0:32, :]
                    if u == 4:
                        pe.wait_ge(s.abs_done, at(L, 1, 1))
                    last = pe.matmul(out, const[:, C_SEL:C_SEL + 32], qk_sq[:, u, :], start=True, stop=True)
                last.then_inc(s.qk_ss, 1)
                gate_unit(L, 7)
                pe.wait_ge(s.ml_rs, at(L, 1, 1))
                pe.wait_ge(s.qk_inv, at(L, 1, 1))
                for h in range(ML_H):
                    pe.matmul(mb[:, h, :], const[:, C_IDENT + 32 * h:C_IDENT + 32 * h + 1].to_broadcast([P, P]), acc[:],
                              start=True, stop=True).then_inc(s.ml_bc, 1)
                gate_unit(L, 8)
                pe.wait_ge(s.qk_rs, at(L, 1, 1))
                for u in range(5):
                    if u < 4:
                        pe.wait_ge(s.ml_bc_read, at(L, ML_H, u + 1))
                    else:
                        pe.wait_ge(s.qk_bc_read, at(L, 5, 1))
                    src = var[32 * u:32 * u + 32, :] if u < 4 else tmp[3][0:32, :]
                    r = 32 * (u % 4)
                    pe.matmul(mb[:, u % 4, :], const[r:r + 32, C_BACK:C_BACK + P], src, start=True, stop=True)\
                      .then_inc(s.qk_bc, 1)
                gate_unit(L, 9)
                pe.wait_ge(s.qk_normed, at(L, 1, 1))
                for g in range(SW_KV):
                    last = pe.matmul(mb[:, 2 + g, :], dup[g], proj[:, 16, :], start=True, stop=True)
                last.then_inc(s.kk_psum, 1)
                for t in range(NT):
                    last = turn(B5[:, t * P:(t + 1) * P], proj[:, 17, t * P:(t + 1) * P])
                last.then_inc(s.v_turned, 1)
                pe.wait_ge(s.kk_copied, at(L, 1, 1))
                pe.wait_ge(s.v_copied, at(L, 5, 5))

                def logits(b):
                    n, g = b // SW_KV, b % SW_KV
                    if b:
                        pe.wait_ge(s.lg_read, at(L, 8, b))
                    lo = 0 if n else P
                    for i in range(SW_G):
                        h = g * SW_G + i
                        half = 64 * (h % 2)
                        out = mb[:, i % 2, (i // 2) * 2 * P + lo:(i // 2) * 2 * P + 2 * P]
                        last = pe.matmul(out, proj[half:half + 64, 12 + h // 2, n * P:(n + 1) * P],
                                         kk[half:half + 64, g, (n - 1) * P + lo:(n + 1) * P], start=True, stop=True)
                    last.then_inc(s.lg_ready, 1)

                logits(0)
                for b in range(8):
                    n, g = b // SW_KV, b % SW_KV
                    if b < 7:
                        logits(b + 1)
                    if b < 6:
                        gate_unit(L, 10 + b)
                    else:
                        pe.wait_ge(s.ha_ready, at(L, 1, 1))
                        branch(L, S_A + b - 6, T_A + 2 * (b - 6), hah, hal)
                    sides = (0, 1) if n else (1,)
                    pe.wait_ge(s.pn_ready, at(L, 8, b + 1))
                    if b:
                        pe.wait_ge(s.o_done, at(L, 8, b))
                    for side in sides:
                        for i in range(SW_G):
                            last = turn(mb[:, 2 + side, i * P:(i + 1) * P], lg[:, b % 2, i, side * P:(side + 1) * P])
                    last.then_inc(s.pt_ready, 1)
                    pe.wait_ge(s.pt_copied, at(L, 8, b + 1))
                    for par in range(2):
                        for side in sides:
                            rhs = pt_sb[:, side].rearrange("p (i two) q -> p two i q", two=2)[:, par]
                            last = pe.matmul(B6[64 * par:64 * par + 64, 0:2 * P].rearrange("p (i q) -> p i q", i=2),
                                             sv_tok[:, n - 1 + side, g * 64:g * 64 + 64], rhs,
                                             start=side == sides[0], stop=side == 1)
                    last.then_inc(s.o_ready, 1)

            def gated(L):
                for u in range(2, 4):
                    branch(L, S_A + u, T_A + 2 * u, hah, hal)
                for u in range(4):
                    if u == 0:
                        pe.wait_ge(s.o_done, at(L, 8, 8))
                    branch(L, S_B + u, T_B + 2 * u, hbh, hbl)
                for j in range(KT):
                    unit(Block1, L, S_OUT + j, T_OUT + j, xh, xl, part_ready=s.mixed_ready,
                         wait_k=(lambda k: at(L, KT, k + 1)) if j == 0 else None)

            def ple(L):
                w = xl_wait(Block1, L, 3)
                for j in range(KT):
                    unit(Block1, L, S_PLE + j, T_PLE + j, xh, xl, wait_k=w if j == 0 else None)
                    if j == 1:
                        sum_squares(Block1, L, 3)
                pe.wait_ge(s.p_landed, at(L, 16, 16))
                pe.wait_ge(s.inv_var, norm_no(Block1, L, 3))
                for k in range(2):
                    for t in range(NT):
                        last = turn(mb[:, k, t * P:(t + 1) * P], p_tok[:, t, k * P:(k + 1) * P])
                last.then_inc(s.p_turned, 1)
                pe.wait_ge(s.pt_split, at(L, 1, 1))
                for j in range(KT):
                    end = j == KT - 1
                    unit(Block1, L, S_PLE + 8 + j // 4, T_PLE + KT + j, pth, ptl, kts=2, c0=(j % 4) * P, pitch=S,
                         new=j % 4 == 0, inc=3 if end else 1)

            with pe.Fori(0, 2) as L:
                ffn(L, 0, S_FFN1, T_FFN1, 0)
                w = xl_wait(Block1, L, 1)
                for u in range(4):
                    unit(Block1, L, S_IN + u, T_IN + u, xh, xl, wait_k=w if u == 0 else None)
                    if u == 1:
                        sum_squares(Block1, L, 1)
                with pe.Fori(1, 3) as i:
                    for u in range(4):
                        unit(Block1, L, S_IN + u, T_IN + u, xh, xl, i, 4)
                mlstm(L)
                swa(L)
                gated(L)
                ffn(L, 2, S_FFN2, T_FFN2, FT)
                ple(L)

            def more_in2(L, u):
                wide = MLA_D if u == U_DT else P
                unit(Block2, L, S2_IN + u, T2_IN + u, xh, xl, width=wide, pitch=wide)

            def query_unit(L, h):
                unit(Block2, L, S2_QB + h // 2, T2_QB + h, cqh, cql, kts=3, width=MLA_D, c0=(h % 2) * MLA_D,
                     pitch=2 * MLA_D, new=h % 2 == 0)

            def gmlp(L):
                for u in range(4, 6):
                    more_in2(L, u)
                pe.wait_ge(s.gv_squared, at(L, 1, 1))
                pe.wait_ge(s.inv_var, norm_no(Block2, L, 0))
                for k in range(2):
                    last = pe.matmul(B4, ones[:], gv_sq[:, k, :], start=k == 0, stop=k == 1)
                last.then_inc(s.gv_ss, 1)
                pe.wait_ge(s.ws_landed, at(L, 16, 16))
                for h in range(4):
                    last = turn(B7[:, h * P:(h + 1) * P], ws_raw[:, h, :])
                last.then_inc(s.ws_turned, 1)
                for u in range(6, 8):
                    more_in2(L, u)
                pe.wait_ge(s.gv_normed, at(L, 1, 1))
                for t in range(NT):
                    for k in range(2):
                        o = (t % 2) * 2 * P + k * P
                        last = turn(mb[:, 1 + t // 2, o:o + P], proj2[:, 2 + k, t * P:(t + 1) * P])
                last.then_inc(s.gv_turned, 1)
                for u in range(8, 10):
                    more_in2(L, u)
                pe.wait_ge(s.gv_copied, at(L, 1, 1))
                pe.wait_ge(s.ws_copied, at(L, 1, 1))
                for k in range(2):
                    for c in range(NT):
                        for par in range(2):
                            h = 2 * k + par
                            out = mb[64 * par:64 * par + 64, k, c * P:(c + 1) * P]
                            pe.matmul(out, gv_tok[:, c, h * 64:h * 64 + 64], ws_t[:, h, :], start=True, stop=False)
                            last = pe.matmul(out, const[0:4, C_IDENT + h:C_IDENT + h + 1].to_broadcast([4, 64]),
                                             bs_now[:], start=False, stop=True)
                last.then_inc(s.gm_psum, 1)

            def ssd(L):
                more_in2(L, U_Z)
                pe.wait_ge(s.conv_silu, at(L, 1, 1))
                pe.wait_ge(s.gm_done, at(L, 1, 1))
                for t in range(NT):
                    for k in range(3):
                        last = turn(mb[:, t, k * P:(k + 1) * P], conv[:, k, t * P:(t + 1) * P])
                last.then_inc(s.xs_turned, 1)
                more_in2(L, U_Z + 1)
                pe.wait_ge(s.dt_rows_done, at(L, 1, 1))
                pe.wait_ge(s.xs_copied, at(L, 1, 1))
                for t in range(NT):
                    turn(B5[:, t * SSD_H:(t + 1) * SSD_H], acc[0:SSD_H, t * P:(t + 1) * P], SSD_H)
                    last = turn(B5[:, 64 + t * SSD_H:64 + (t + 1) * SSD_H], var[0:SSD_H, t * P:(t + 1) * P], SSD_H)
                last.then_inc(s.dcol_turned, 1)

                def products(g):
                    for j in range(NT):
                        c = 4 * g + j
                        if c:
                            pe.wait_ge(s.cb_copied, at(L, 8, c))
                        else:
                            pe.wait_ge(s.dcol_copied, at(L, 1, 1))
                        pe.matmul(B5[:, 0:S - j * P], conv[64 * g:64 * g + 64, 3, j * P:(j + 1) * P],
                                  conv[64 * g:64 * g + 64, 4, j * P:S], start=True, stop=True).then_inc(s.cb_ready, 1)

                def decays(h):
                    if h:
                        pe.wait_ge(s.abc_copied, at(L, SSD_H, h))
                    pe.matmul(B4, const[0:SSD_H, C_IDENT + h:C_IDENT + h + 1].to_broadcast([SSD_H, P]), acc[0:SSD_H, :],
                              start=True, stop=True).then_inc(s.abc_ready, 1)

                decays(0)
                more_in2(L, U_Z + 2)
                more_in2(L, U_C)
                for h in range(SSD_H):
                    tile, half = h // 2, 64 * (h % 2)
                    if h % 3 == 0:
                        products(h // 3)
                    if h < SSD_H - 1:
                        decays(h + 1)
                    if h < 4:
                        more_in2(L, U_C + 1 + h)
                    else:
                        if h == 4:
                            pe.wait_ge(s.c_split, at(L, 1, 1))
                        for q in (2 * (h - 4), 2 * (h - 4) + 1):
                            query_unit(L, q)
                    out = mb[half:half + 64, 2 + tile % 2, :]
                    for j in range(NT):
                        pe.wait_ge(s.sp_ready, at(L, 24, 4 * h + j + 1))
                        if j == 0 and h == 4:
                            pe.wait_ge(s.y_done, at(L, 3, 1))
                        o = ML_OFF[j]
                        last = pe.matmul(out[:, j * P:S], xs_tok[:, j, h * 64:h * 64 + 64], sd_p[:, o:o + S - j * P],
                                         start=j == 0, stop=j == 3)
                    last.then_inc(s.y_psum, 1)

            def mla(L):
                B = Block2
                pe.wait_ge(s.c_squared, at(L, 1, 1))
                pe.wait_ge(s.abc_copied, at(L, SSD_H, SSD_H))
                for k in range(3):
                    pe.matmul(B4, ones[:], c_sq[:, k, :], start=k == 0, stop=k == 2)
                for k in range(2):
                    last = pe.matmul(B5, ones[:], c_sq[:, 3 + k, :], start=k == 0, stop=k == 1)
                last.then_inc(s.c_ss, 1)
                pe.wait_ge(s.y_squared, at(L, 1, 1))
                for half, k in ((0, 0), (64, 2)):
                    out = B7[half:half + 64, :]
                    pe.matmul(out, ones[:, 0:64], y_sq[:, k, :], start=True, stop=False)
                    last = pe.matmul(out, ones[half:half + 64, 0:64], y_sq[half:half + 64, 1, :], start=False, stop=True)
                last.then_inc(s.y_ss, 1)
                pe.wait_ge(s.rope_landed, 16)
                pe.wait_ge(s.c_inv, at(L, 1, 1))
                pe.matmul(B5[0:MLA_D, :], rot96, proj2[0:MLA_D, 12, :], start=True, stop=True).then_inc(s.rot_psum, 1)
                for h in range(4, MLA_H):
                    query_unit(L, h)
                pe.wait_ge(s.y_rs, at(L, 1, 1))
                for g in range(2):
                    last = pe.matmul(mb[:, 2 + g, :], const[:, C_IDENT + 64 * g:C_IDENT + 64 * g + 1].to_broadcast([P, P]),
                                     tmp[0][:], start=True, stop=True)
                last.then_inc(s.y_bc, 1)
                for u in range(MLA_H + 1):
                    if u < MLA_H:
                        unit(B, L, S2_KVB + u // 2, T2_KVB + u, ckh, ckl, kts=2, c0=(u % 2) * P, pitch=2 * P,
                             new=u % 2 == 0)
                    if u == 0:
                        continue
                    h = u - 1
                    if h == 0:
                        pe.wait_ge(s.ssd_done, at(L, 1, 1))
                    pe.wait_ge(s.tile_evacuated, tiles_out(B, L, T2_QB + h))
                    pe.wait_ge(s.rot_read, at(L, 1 + MLA_H, max(1, h)))
                    pe.matmul(mb[0:MLA_D, 2 + (h + 1) % 2, :], rot96, q96[:, h, :], start=True, stop=True)\
                      .then_inc(s.rot_psum, 1)
                    pe.wait_ge(s.kv_done, at(L, MLA_H, h + 1))
                    if h >= 2:
                        pe.wait_ge(s.vt_copied, at(L, MLA_H, h - 1))
                    for t in range(NT):
                        last = pe.matmul(mb[:, h % 2, t * 64:(t + 1) * 64], v_ft[64:P, h % 2, t * P:(t + 1) * P],
                                         const[64:P, C_IDENT + 64:C_IDENT + P], start=True, stop=True)
                    last.then_inc(s.vt_psum, 1)
                pe.wait_ge(s.rot_done, at(L, 1 + MLA_H, 1 + MLA_H))
                pe.wait_ge(s.vt_copied, at(L, MLA_H, MLA_H))

                def logits(c):
                    h, n = c // NT, c % NT
                    if c >= TILE_BANKS:
                        pe.wait_ge(s.ae_ready, at(L, 24, c - TILE_BANKS + 1))
                    out = bank[c % TILE_BANKS]
                    pe.matmul(out[:, 0:(n + 1) * P], q96[:, h, n * P:(n + 1) * P], k96[:, h, 0:(n + 1) * P],
                              start=True, stop=False)
                    pe.matmul(out[:, n * P:(n + 1) * P], ident, mask_qs, start=False, stop=True).then_inc(s.al_ready, 1)

                def turned(c):
                    n = c % NT
                    pe.wait_ge(s.ap_ready, at(L, 24, c + 1))
                    if c >= 2:
                        pe.wait_ge(s.at_copied, at(L, 24, c - 1))
                    for j in range(n + 1):
                        last = turn(mb[:, c % 2, j * P:(j + 1) * P], prob[:, c % 4, j * P:(j + 1) * P])
                    last.then_inc(s.at_ready, 1)

                def head_out(h):
                    half = 64 * (h % 2)
                    pe.wait_ge(s.at_copied, at(L, 24, 4 * h + 4))
                    if h >= 2:
                        pe.wait_ge(s.ao_done, at(L, MLA_H, h - 1))
                    for j in range(NT):
                        last = pe.matmul(mb[half:half + 64, 2 + h % 2, j * P:S], v_tok[:, j, h * 64:h * 64 + 64],
                                         prob_t[h % 2][:, j, j * P:S], start=j == 0, stop=j == 3)
                    last.then_inc(s.ao_ready, 1)

                for c in range(3):
                    logits(c)
                for c in range(NT * MLA_H):
                    if c + 3 < NT * MLA_H:
                        logits(c + 3)
                    turned(c)
                    if c >= NT and c % NT == 0:
                        head_out(c // NT - 1)
                head_out(MLA_H - 1)

            with pe.Fori(0, 2) as L:
                B = Block2
                w = xl_wait(B, L, 0)
                for u in range(4):
                    unit(B, L, S2_IN + u, T2_IN + u, xh, xl, wait_k=w if u == 0 else None)
                    if u == 1:
                        sum_squares(B, L, 0)
                gmlp(L)
                ssd(L)
                mla(L)
                pe.wait_ge(s.ao_done, at(L, MLA_H, MLA_H))
                for j in range(KT):
                    unit(B, L, S2_OUT + j, T2_OUT + j, xh, xl)
                w = xl_wait(B, L, 1)
                for half in range(2):
                    n0, t0 = S2_MLP + half * 2 * HALF2, T2_MLP + half * (HALF2 + 8)
                    for u in range(4):
                        unit(B, L, n0 + u, t0 + u, xh, xl, wait_k=w if u == 0 and half == 0 else None)
                        if u == 1 and half == 0:
                            sum_squares(B, L, 1)
                    with pe.Fori(1, HALF2 // 4) as i:
                        for u in range(4):
                            unit(B, L, n0 + u, t0 + u, xh, xl, i, 4)
                    for dh in range(2):
                        n1, t1 = n0 + HALF2 + 8 * dh, t0 + HALF2 + 4 * dh

                        def down(q, i=None):
                            take_slab(B, L, n1 + q, i, 4)
                            h, l = wh[(n1 + q) % SPLIT_SLOTS], wl[(n1 + q) % SPLIT_SLOTS]
                            if dh == 0:
                                pe.wait_ge(s.hidden_ready,
                                           at(L, FT2, 4 * FT + half * HALF2 + 2 * q + 2, i, 8))
                            for kk_ in range(2):
                                kt = 2 * q + kk_ if i is None else i * 8 + (2 * q + kk_)
                                first, end = i is None and q == 0 and kk_ == 0, q == 7 and kk_ == 1
                                for d in range(4):
                                    if first:
                                        open_tile(B, L, t1 + d)
                                    out = bank[(B.base_tile + t1 + d) % TILE_BANKS][:]
                                    c = kk_ * S + d * P
                                    last = three(out, h[:, c:c + P], l[:, c:c + P], hh[:, kt, :], hl[:, kt, :],
                                                 first, end, new=kk_ == 0 and d == 0)
                                    if end:
                                        last.then_inc(s.tile_ready, 3 if half and dh and d == 3 else 1)

                        for q in range(8):
                            down(q)

            pe.wait_ge(s.ss_ready, 13)
            pe.matmul(B4, ones[:], acc[:], start=True, stop=True).then_inc(s.ss_psum, 1)
            pe.wait_ge(s.fin_y, 1)
            for c in range(2 * NT):
                t, side = c // 2, c % 2
                if c >= 4:
                    pe.wait_ge(s.fin_copied, c - 3)
                for j in range(4):
                    last = turn(mb[:, c % 4, j * P:(j + 1) * P], y_sb[:, 4 * side + j, t * P:(t + 1) * P])
                last.then_inc(s.fin_turned, 1)

        @block.scalar
        def _(act):
            def round_hi(B, L, n, i=None, step=0):
                if n >= B.slabs:
                    return
                act.wait_ge(raw_landed[n % RAW_SLOTS],
                            at(L, 8 * B.slabs, 8 * (B.base_slab + n - n % 2) + 16, i, 8 * step))
                act.wait_ge(s.slab_used, at(L, B.slabs, B.base_slab + n + 1, i, step))
                if B is Block2 and n == S2_IN + U_DT:
                    act.wait_ge(s.kr_landed, at(L, 16, 16))
                act.activation(wh[n % SPLIT_SLOTS][:], raw[n % RAW_SLOTS][:], ACT.Copy).then_inc(s.hi_ready, 1)

            def ahead(B, L, n, count, i=None, step=0):
                for k in range(count):
                    round_hi(B, L, n + k + AHEAD, i, step)

            def norm(B, L, k):
                no = norm_no(B, L, k)
                act.wait_ge(s.x_final, no)
                for q in range(2):
                    last = act.activation(squares[:, 4 * q:4 * q + 4, :], x_sb[:, 4 * q:4 * q + 4, :], ACT.Square)
                last.then_inc(s.sq_ready, 1)

            def norm_root(B, L, k):
                act.wait_ge(s.inv_var, norm_no(B, L, k))
                act.activation(rstd[:], var[:], ACT.Sqrt).then_inc(s.rstd_ready, 1)

            def ffn(L, k, n, t, silu0):
                norm(Block1, L, k)
                ahead(Block1, L, n, 2)
                norm_root(Block1, L, k)

                def pair(f, i=None):
                    act.wait_ge(s.tile_evacuated, tiles_out(Block1, L, t + 2 * f, i, 4))
                    act.activation(tmp[f % 2][:], tmp[f % 2][:], ACT.Silu).then_inc(s.silu_done, 1)

                pair(0)
                ahead(Block1, L, n + 2, 2)
                pair(1)
                with act.Fori(1, FT // 2) as i:
                    for f in range(2):
                        round_hi(Block1, L, n + 2 * f + AHEAD, i, 4)
                        pair(f, i)
                        round_hi(Block1, L, n + 2 * f + 1 + AHEAD, i, 4)
                n0 = n + 2 * FT
                with act.Fori(0, 5) as i:
                    ahead(Block1, L, n0, 4, i, 4)
                ahead(Block1, L, n0 + 20, 2)

            def mlstm(L):
                act.wait_ge(s.tile_evacuated, tiles_out(Block1, L, T_IN + 11))
                act.activation(proj[:, 8:12, :], proj[:, 8:12, :], ACT.Sigmoid).then_inc(s.mo_done, 1)
                fp, ig, e1, e2 = ml_rows[0:4]
                act.wait_ge(s.gate_pre, at(L, 1, 1))
                act.activation(e1[:], fp[:], ACT.Abs)
                act.drain()
                act.activation(e2[:], e1[:], ACT.Exp, scale=-1.0)
                act.drain()
                act.activation(e1[:], e2[:], ACT.Ln, bias=1.0).then_inc(s.log1p, 1)
                ahead(Block1, L, S_IN + 12, 3)
                act.wait_ge(s.ml_rows_done, at(L, 1, 1))
                act.activation(var[0:ML_H, :], ml_rows[7][:], ACT.Exp, scale=-1.0).then_inc(s.emt_done, 1)
                ahead(Block1, L, S_IN + 15, 1)

                def weights(h):
                    act.wait_ge(s.bc_copied, at(L, ML_H, h + 1))
                    if h == 0:
                        act.wait_ge(s.c_copied, at(L, 1, 1))
                    for j in range(NT):
                        if h:
                            act.wait_ge(s.p_ready, at(L, 16, 4 * h - 3 + j))
                        o = ML_OFF[j]
                        last = act.activation(ml_w[:, o:o + P], neg_md[:, j * P:(j + 1) * P], ACT.Exp,
                                              bias=c_col[:, j, h:h + 1])
                        if j < NT - 1:
                            last = act.activation(ml_w[:, o + P:o + S - j * P], neg_m[:, (j + 1) * P:S], ACT.Exp,
                                                  bias=c_col[:, j, h:h + 1])
                        last.then_inc(s.w_ready, 1)

                weights(0)
                ahead(Block1, L, S_IN + 16, 2)
                for h in range(ML_H):
                    if h < ML_H - 1:
                        weights(h + 1)
                    act.wait_ge(s.head_done, at(L, ML_H, h + 1))
                    act.activation(tmp[h][:], B6, ACT.Square).then_inc(s.num_sq, 1)
                    if h < ML_H - 1:
                        ahead(Block1, L, S_GATE + 2 * h, 2)
                act.activation(acc[:], B7, ACT.Abs).then_inc(s.abs_done, 1)

            def swa(L):
                act.wait_ge(s.tile_evacuated, tiles_out(Block1, L, T_IN + 17))
                act.activation(qk_sq[:], proj[:, 12:17, :], ACT.Square).then_inc(s.qk_squared, 1)
                ahead(Block1, L, S_GATE + 6, 2)
                act.wait_ge(s.ml_inv, at(L, 1, 1))
                act.activation(acc[:], acc[:], ACT.Sqrt).then_inc(s.ml_rs, 1)
                act.wait_ge(s.qk_inv, at(L, 1, 1))
                act.activation(var[:], var[:], ACT.Sqrt)
                act.activation(tmp[3][0:32, :], tmp[3][0:32, :], ACT.Sqrt).then_inc(s.qk_rs, 1)
                gates(L, 0)
                ahead(Block1, L, S_GATE + 8, 2)
                for b in range(8):
                    n = b // SW_KV
                    lo = 0 if n else P
                    act.wait_ge(s.mx_ready, at(L, 8, b + 1))
                    for i in range(SW_G):
                        act.activation(lg[:, b % 2, i, lo:2 * P], lg[:, b % 2, i, lo:2 * P], ACT.Exp,
                                       bias=small[:, 4 + i:5 + i], accum_out=small[:, 12 + i:13 + i])
                    act.activation(small[:, 16:20], small[:, 8:12], ACT.Exp).then_inc(s.ex_ready, 1)
                    ahead(Block1, L, S_GATE + 10 + b, 1)

            def gates(L, branch):
                act.wait_ge(s.tile_evacuated, tiles_out(Block1, L, T_GATE + 8 * branch + 7))
                for j in range(KT):
                    g = gate[8 * branch + j]
                    act.activation(g[:], g[:], ACT.Sigmoid).then_inc(s.sig_done, 1)

            def gated(L):
                ahead(Block1, L, S_A + 2, 2)
                gates(L, 1)
                ahead(Block1, L, S_B, 4)
                ahead(Block1, L, S_OUT, 8)

            def ple(L):
                norm(Block1, L, 3)
                ahead(Block1, L, S_PLE, 2)
                norm_root(Block1, L, 3)
                for j in range(KT):
                    act.wait_ge(s.tile_evacuated, tiles_out(Block1, L, T_PLE + j))
                    act.activation(gate_sg[:, j, :], gate_sg[:, j, :], ACT.Sigmoid).then_inc(s.sg_done, 1)
                    if j >= 2:
                        round_hi(Block1, L, S_PLE + j + AHEAD)

            act.wait_ge(s.toep_row, SW_H)
            act.dma_start(scratch.rearrange("h p c -> p h c"), toep[:]).then_inc(s.toep_out, 16)
            act.wait_ge(s.toep_out, 16)
            act.dma_start(bias[:], bass.AP(scratch.tensor, P - 1, [[TOEP - 1, P], [P * TOEP, SW_H], [1, 2 * P]]))\
               .then_inc(s.toep_in, 16)
            with act.Fori(0, 2) as L:
                for n in range(AHEAD):
                    round_hi(Block1, L, n)
                ffn(L, 0, S_FFN1, T_FFN1, 0)
                norm(Block1, L, 1)
                ahead(Block1, L, S_IN, 2)
                norm_root(Block1, L, 1)
                ahead(Block1, L, S_IN + 2, 10)
                mlstm(L)
                swa(L)
                gated(L)
                ffn(L, 2, S_FFN2, T_FFN2, FT)
                ple(L)

            def gmlp(L):
                for u in range(4):
                    act.wait_ge(s.tile_evacuated, tiles_out(Block2, L, T2_IN + u))
                    last = act.activation(proj2[:, u, :], proj2[:, u, :], ACT.Gelu_apprx_tanh)
                last.then_inc(s.gelu_done, 1)
                act.drain()
                act.activation(gv_sq[:], proj2[:, 2:4, :], ACT.Square).then_inc(s.gv_squared, 1)
                ahead(Block2, L, S2_IN + 4, 2)
                act.wait_ge(s.gv_inv, at(L, 1, 1))
                act.activation(tmp[1][:], tmp[0][:], ACT.Sqrt).then_inc(s.gv_rs, 1)
                ahead(Block2, L, S2_IN + 6, 4)

            def ssd(L):
                act.wait_ge(s.conv_done, at(L, 1, 1))
                act.activation(conv[:], conv[:], ACT.Silu).then_inc(s.conv_silu, 1)
                ahead(Block2, L, S2_IN + U_Z, 1)
                act.wait_ge(s.dt_pre, at(L, 1, 1))
                act.activation(tmp[3][0:SSD_H, :], tmp[2][0:SSD_H, :], ACT.Abs)
                act.drain()
                act.activation(tmp[1][0:SSD_H, :], tmp[3][0:SSD_H, :], ACT.Exp, scale=-1.0)
                act.activation(small[0:SSD_H, 1:2], dt_now[:, 1:2], ACT.Exp)
                act.drain()
                act.activation(tmp[3][0:SSD_H, :], tmp[1][0:SSD_H, :], ACT.Ln, bias=1.0).then_inc(s.dt_log, 1)
                ahead(Block2, L, S2_IN + U_Z + 1, 1)

                def weights(h):
                    act.wait_ge(s.abc_copied, at(L, SSD_H, h + 1))
                    for j in range(NT):
                        if h:
                            act.wait_ge(s.sp_ready, at(L, 24, 4 * h - 3 + j))
                        o = ML_OFF[j]
                        last = act.activation(sd_w[:, o:o + P], tmp[1][:, j * P:(j + 1) * P], ACT.Exp,
                                              bias=a_col[:, j, h:h + 1])
                        if j < NT - 1:
                            last = act.activation(sd_w[:, o + P:o + S - j * P], tmp[0][:, (j + 1) * P:S], ACT.Exp,
                                                  bias=a_col[:, j, h:h + 1])
                        last.then_inc(s.sw_ready, 1)

                weights(0)
                ahead(Block2, L, S2_IN + U_Z + 2, 2)
                act.wait_ge(s.tile_evacuated, tiles_out(Block2, L, T2_IN + U_Z + 2))
                act.activation(proj2[:, 4:7, :], proj2[:, 4:7, :], ACT.Silu).then_inc(s.z_silu, 1)
                for h in range(SSD_H):
                    if h < SSD_H - 1:
                        weights(h + 1)
                    if h == 4:
                        act.wait_ge(s.tile_evacuated, tiles_out(Block2, L, T2_IN + U_C + 4))
                        act.activation(c_sq[:], proj2[:, 13:18, :], ACT.Square).then_inc(s.c_squared, 1)
                    ahead(Block2, L, S2_IN + U_C + 1 + h, 1)

            def mla(L):
                act.wait_ge(s.y_done, at(L, 3, 3))
                act.activation(y_sq[:], conv[:, 0:3, :], ACT.Square).then_inc(s.y_squared, 1)
                act.wait_ge(s.c_inv, at(L, 1, 1))
                act.activation(acc[:], tmp[2][:], ACT.Sqrt)
                act.activation(var[:], tmp[3][:], ACT.Sqrt).then_inc(s.c_rs, 1)
                act.wait_ge(s.y_inv, at(L, 1, 1))
                act.activation(tmp[0][:], tmp[0][:], ACT.Sqrt).then_inc(s.y_rs, 1)
                ahead(Block2, L, S2_QB + 2, 4)
                for h in range(MLA_H):
                    for n in range(NT):
                        c = 4 * h + n
                        act.wait_ge(s.am_ready, at(L, 24, c + 1))
                        if c >= 4:
                            act.wait_ge(s.at_ready, at(L, 24, c - 3))
                        w = (n + 1) * P
                        act.activation(prob[:, c % 4, 0:w], bank[c % TILE_BANKS][:, 0:w], ACT.Exp,
                                       bias=small[:, 32 + n:33 + n], scale=MLA_SCALE,
                                       accum_out=small[:, 36 + n:37 + n]).then_inc(s.ae_ready, 1)

            with act.Fori(0, 2) as L:
                B = Block2
                for n in range(AHEAD):
                    round_hi(B, L, n)
                norm(B, L, 0)
                ahead(B, L, S2_IN, 2)
                norm_root(B, L, 0)
                ahead(B, L, S2_IN + 2, 2)
                gmlp(L)
                ssd(L)
                mla(L)
                ahead(B, L, S2_OUT, 8)
                norm(B, L, 1)
                ahead(B, L, S2_MLP, 2)
                norm_root(B, L, 1)
                ahead(B, L, S2_MLP + 2, 2)
                with act.Fori(1, 2 * FT2 // 4 - 1) as i:
                    ahead(B, L, S2_MLP, 4, i, 4)
                ahead(B, L, B2_SLABS - 4, 4)
            act.wait_ge(s.x_final, 13)
            for q in range(2):
                last = act.activation(squares[:, 4 * q:4 * q + 4, :], x_sb[:, 4 * q:4 * q + 4, :], ACT.Square)
            last.then_inc(s.sq_ready, 1)
            act.wait_ge(s.inv_var, 13)
            act.activation(rstd[:], var[:], ACT.Sqrt).then_inc(s.rstd_ready, 1)

        @block.vector
        def _(dve):
            def split(hi, lo, src):
                dve.tensor_copy(hi, src)
                dve.drain()
                return dve.tensor_tensor(lo, src, hi.bitcast(F32), ALU.subtract)

            def invert(out, sums, scale):
                dve.tensor_scalar(out, sums, scale, EPS, ALU.mult, ALU.add)
                dve.drain()
                return dve.reciprocal(out, out)

            def read_tile(B, L, t, out, scale, i=None, step=0, rows=(0, P), inc=1):
                dve.wait_ge(s.tile_ready, tiles_in(B, L, t, i, step))
                r0, r1 = rows
                return dve.tensor_tensor(out, bank[(B.base_tile + t) % TILE_BANKS][r0:r1, :], scale[r0:r1, :], ALU.mult)\
                          .then_inc(s.tile_evacuated, inc)

            def norm(B, L, k, g):
                no = norm_no(B, L, k)
                dve.drain().then_inc(s.x_final, 1)
                for j in range(KT):
                    dve.tensor_scalar(xh[:, j, :], x_sb[:, j, :], g[:, j:j + 1], None, ALU.mult)
                    dve.drain()
                    dve.scalar_tensor_tensor(out=xl[:, j, :], in0=x_sb[:, j, :], scalar=g[:, j:j + 1],
                                             in1=xh[:, j, :].bitcast(F32), op0=ALU.mult, op1=ALU.subtract)\
                       .then_inc(s.xl_ready, 1)
                norm_scale(no)

            def scaled_tile(B, L, k, t, out, i=None, step=0, rows=(0, P), inc=1):
                dve.wait_ge(s.rstd_ready, norm_no(B, L, k))
                return read_tile(B, L, t, out, rstd, i, step, rows, inc)

            def norm_scale(no):
                dve.wait_ge(s.sq_ready, no)
                dve.tensor_reduce(acc[:], squares[:].rearrange("p j t -> p t j"), AX.X, ALU.add).then_inc(s.ss_ready, 1)
                dve.wait_ge(s.ss_psum, no)
                invert(var[:], B4, 1.0 / D).then_inc(s.inv_var, 1)

            def add_x(B, L, t, j, scale=1.0, inc=1):
                dve.wait_ge(s.tile_ready, tiles_in(B, L, t))
                dve.scalar_tensor_tensor(out=x_sb[:, j, :], in0=bank[(B.base_tile + t) % TILE_BANKS][:], scalar=scale,
                                         in1=x_sb[:, j, :], op0=ALU.mult, op1=ALU.add).then_inc(s.tile_evacuated, inc)

            for j in range(KT):
                dve.wait_ge(s.setup_t, j + 1)
                dve.tensor_copy(x_sb[:, j, :], mb[:, j % 4, :]).then_inc(s.setup_copied, 1)
            dve.wait_ge(s.setup_t, KT + 1)
            dve.tensor_copy(p1[:], B4[:, 0:2 * R1])
            dve.tensor_copy(p2[:], B5[:, 0:2 * R2 + KT])
            for h in range(SW_H):
                dve.wait_ge(s.rel_psum, h + 1)
                dve.tensor_tensor(toep[:, h, :], mb[:, 2 + h % 2, 0:TOEP], pad[:], ALU.add).then_inc(s.toep_row, 1)
            dve.wait_ge(s.toep_out, 16)
            dve.drain()

            def ffn(L, k, g, t, silu0):
                norm(Block1, L, k, g)
                def pair(f, i=None):
                    gs, us = tmp[f % 2], tmp[2 + f % 2]
                    scaled_tile(Block1, L, k, t + 2 * f, gs[:], i, 4)
                    scaled_tile(Block1, L, k, t + 2 * f + 1, us[:], i, 4)
                    dve.drain()
                    dve.wait_ge(s.silu_done, at(L, 2 * FT, silu0 + f + 1, i, 2))
                    dve.tensor_tensor(us[:], us[:], gs[:], ALU.mult)
                    dve.drain()
                    j = f if i is None else i * 2 + f
                    split(hh[:, j, :], hl[:, j, :], us[:]).then_inc(s.hidden_ready, 1)

                with dve.Fori(0, FT // 2) as i:
                    for f in range(2):
                        pair(f, i)
                for j in range(KT):
                    add_x(Block1, L, t + 2 * FT + j, j, 0.5)

            def mlstm(L):
                fp, ig, e1, e2, fc, cc, mm, mt, lf = ml_rows
                dve.wait_ge(s.gates_psum, at(L, 1, 1))
                dve.tensor_tensor(ig[:], B4[0:ML_H, :], rstd[0:ML_H, :], ALU.mult)
                dve.tensor_tensor(fp[:], B5[0:ML_H, :], rstd[0:ML_H, :], ALU.mult)
                dve.drain()
                dve.tensor_scalar(ig[:], ig[:], b_gate_now[:, 0:1], None, ALU.add)
                dve.tensor_scalar(fp[:], fp[:], b_gate_now[:, 1:2], None, ALU.add).then_inc(s.gate_pre, 1)
                for t in range(NT):
                    dve.wait_ge(s.v_turned, at(L, 5, t + 1))
                    dve.tensor_copy(mv_tok[:, t, :], mb[:, 2 + t % 2, :]).then_inc(s.v_copied, 1)
                dve.tensor_scalar(lf[:], fp[:], 0.0, None, ALU.min)
                dve.drain()
                dve.wait_ge(s.log1p, at(L, 1, 1))
                dve.tensor_tensor(lf[:], lf[:], e1[:], ALU.subtract)
                dve.drain()
                dve.tensor_tensor_scan(fc[:], ones[0:ML_H, 0:1].to_broadcast([ML_H, S]), lf[:], 0.0, ALU.mult, ALU.add)
                dve.drain()
                dve.tensor_tensor(cc[:], ig[:], fc[:], ALU.subtract)
                dve.drain()
                dve.tensor_tensor_scan(mm[:], cc[:], cc[:], 0.0, ALU.max, ALU.max)
                dve.drain()
                dve.tensor_scalar(acc[0:ML_H, :], mm[:], -1.0, None, ALU.mult)
                dve.tensor_tensor(mt[:], mm[:], fc[:], ALU.add).then_inc(s.ml_rows_done, 1)
                for u in range(12, 15):
                    more_in(L, u)
                dve.wait_ge(s.c_turned, at(L, 1, 1))
                dve.tensor_copy(c_col[:].rearrange("p t h -> p (t h)"), B5[:, 0:NT * ML_H]).then_inc(s.c_copied, 1)
                more_in(L, 15)

                def minus_m(h):
                    dve.wait_ge(s.bc_ready, at(L, ML_H + 1, h + 1))
                    dve.tensor_copy(neg_m[:], B4)
                    dve.tensor_tensor(neg_md[:].rearrange("p (t q) -> p t q", t=NT), B4.rearrange("p (t q) -> p t q", t=NT),
                                      mask_sq[:, None, :].to_broadcast([P, NT, P]), ALU.add).then_inc(s.bc_copied, 1)

                minus_m(0)
                for u in range(16, 18):
                    more_in(L, u)
                dve.wait_ge(s.mo_done, at(L, 1, 1))
                for h in range(ML_H):
                    for j in range(NT):
                        e = 4 * h + j
                        dve.wait_ge(s.w_ready, at(L, 16, e + 1))
                        dve.wait_ge(s.sc_ready, at(L, 16, e + 1))
                        if h:
                            dve.wait_ge(s.pv_done, at(L, 16, e - 3))
                        o, w = ML_OFF[j], S - j * P
                        dve.scalar_tensor_tensor(out=ml_p[:, o:o + w], in0=B5[:, 0:w], scalar=0.125,
                                                 in1=ml_w[:, o:o + w], op0=ALU.mult, op1=ALU.mult).then_inc(s.p_ready, 1)
                    if h < ML_H - 1:
                        minus_m(h + 1)
                    dve.wait_ge(s.pv_done, at(L, 16, 4 * h + 4))
                    dve.scalar_tensor_tensor(out=num_sb[:, h, :], in0=B6, scalar=par1[:, R_MLOUT + h:R_MLOUT + h + 1],
                                             in1=proj[:, 8 + h, :], op0=ALU.mult, op1=ALU.mult).then_inc(s.head_done, 1)
                    if h < ML_H - 1:
                        for g in (2 * h, 2 * h + 1):
                            gate_tile(L, g)
                dve.wait_ge(s.abs_done, at(L, 1, 1))
                dve.wait_ge(s.bc_ready, at(L, ML_H + 1, ML_H + 1))
                dve.tensor_tensor(acc[:], acc[:], B4, ALU.max)
                dve.drain()
                dve.scalar_tensor_tensor(out=acc[:], in0=acc[:], scalar=EPS, in1=acc[:], op0=ALU.mult, op1=ALU.mult)
                gate_tile(L, 6)
                dve.drain()
                dve.wait_ge(s.ml_ss, at(L, 1, 1))
                dve.scalar_tensor_tensor(out=acc[:], in0=B5, scalar=1.0 / P, in1=acc[:], op0=ALU.mult, op1=ALU.add)
                dve.drain()
                dve.reciprocal(acc[:], acc[:]).then_inc(s.ml_inv, 1)

            def more_in(L, u):
                scaled_tile(Block1, L, 1, T_IN + u, proj[:, u, :])

            def gate_tile(L, g):
                scaled_tile(Block1, L, 1, T_GATE + g, gate[g][:])

            def a_tile(L, j):
                dve.wait_ge(s.sig_done, at(L, 16, j + 1))
                read_tile(Block1, L, T_A + j, gate[j][:], gate[j])

            def swa(L):
                dve.wait_ge(s.qk_ss, at(L, 1, 1))
                dve.tensor_scalar(var[:], B6, 1.0 / 64, EPS, ALU.mult, ALU.add)
                dve.tensor_scalar(tmp[3][0:32, :], B7[0:32, :], 1.0 / 64, EPS, ALU.mult, ALU.add)
                dve.drain()
                dve.reciprocal(var[:], var[:])
                dve.reciprocal(tmp[3][0:32, :], tmp[3][0:32, :]).then_inc(s.qk_inv, 1)
                dve.tensor_scalar(small[:, 0:1], par1[:, R_QN:R_QN + 1], 0.125, None, ALU.mult)
                gate_tile(L, 7)
                for h in range(ML_H):
                    dve.wait_ge(s.ml_bc, at(L, ML_H, h + 1))
                    dve.tensor_tensor(num_sb[:, h, :], num_sb[:, h, :], mb[:, h, :], ALU.mult).then_inc(s.ml_bc_read, 1)
                    dve.drain()
                    last = split(hah[:, h, :], hal[:, h, :], num_sb[:, h, :])
                last.then_inc(s.ha_ready, 1)
                gate_tile(L, 8)
                for u in range(5):
                    gain = small[:, 0:1] if u < 4 else par1[:, R_KN:R_KN + 1]
                    dve.wait_ge(s.qk_bc, at(L, 5, u + 1))
                    dve.scalar_tensor_tensor(out=proj[:, 12 + u, :], in0=proj[:, 12 + u, :], scalar=gain,
                                             in1=mb[:, u % 4, :], op0=ALU.mult, op1=ALU.mult).then_inc(s.qk_bc_read, 1)
                dve.drain().then_inc(s.qk_normed, 1)
                gate_tile(L, 9)
                dve.wait_ge(s.kk_psum, at(L, 1, 1))
                for g in range(SW_KV):
                    last = dve.tensor_copy(kk[:, g, :], mb[:, 2 + g, :])
                last.then_inc(s.kk_copied, 1)
                dve.wait_ge(s.v_turned, at(L, 5, 5))
                dve.tensor_copy(sv_tok[:].rearrange("p t c -> p (t c)"), B5).then_inc(s.v_copied, 1)

                def of_side(buf, side):
                    return buf.rearrange("p (i two) k -> p two i k", two=2)[:, side]

                def biased(b):
                    n, g = b // SW_KV, b % SW_KV
                    lo = 0 if n else P
                    buf = lg[:, b % 2, :, lo:2 * P]
                    dve.wait_ge(s.lg_ready, at(L, 8, b + 1))
                    for side in range(2):
                        last = dve.tensor_tensor(of_side(lg[:, b % 2], side)[:, :, lo:2 * P],
                                                 mb[:, side, :].rearrange("p (i k) -> p i k", i=2)[:, :, lo:2 * P],
                                                 of_side(bias[:, g * SW_G:(g + 1) * SW_G], side)[:, :, lo:2 * P], ALU.add)
                    last.then_inc(s.lg_read, 1)
                    dve.drain()
                    dve.tensor_reduce(small[:, 20:24], buf, AX.X, ALU.max)
                    dve.drain()
                    dve.tensor_tensor(small[:, 20:24], small[:, 20:24], sinks_now[:, g * SW_G:g * SW_G + SW_G], ALU.max)
                    dve.drain()
                    dve.tensor_scalar(small[:, 4:8], small[:, 20:24], -1.0, None, ALU.mult)
                    dve.tensor_tensor(small[:, 8:12], sinks_now[:, g * SW_G:g * SW_G + SW_G], small[:, 20:24],
                                      ALU.subtract).then_inc(s.mx_ready, 1)

                biased(0)
                for b in range(8):
                    n, g = b // SW_KV, b % SW_KV
                    lo = 0 if n else P
                    dve.wait_ge(s.ex_ready, at(L, 8, b + 1))
                    dve.tensor_tensor(small[:, 24:28], small[:, 12:16], small[:, 16:20], ALU.add)
                    dve.drain()
                    dve.reciprocal(small[:, 28:32], small[:, 24:28])
                    dve.drain()
                    for i in range(SW_G):
                        last = dve.tensor_scalar(lg[:, b % 2, i, lo:2 * P], lg[:, b % 2, i, lo:2 * P],
                                                 small[:, 28 + i:29 + i], None, ALU.mult)
                    last.then_inc(s.pn_ready, 1)
                    if b < 7:
                        biased(b + 1)
                    if b < 6:
                        gate_tile(L, 10 + b)
                    else:
                        for j in (2 * (b - 6), 2 * (b - 6) + 1):
                            a_tile(L, j)
                    dve.wait_ge(s.pt_ready, at(L, 8, b + 1))
                    for side in ((0, 1) if n else (1,)):
                        last = dve.tensor_copy(pt_sb[:, side].rearrange("p i q -> p (i q)"), mb[:, 2 + side, :])
                    last.then_inc(s.pt_copied, 1)
                    dve.wait_ge(s.o_ready, at(L, 8, b + 1))
                    src = B6[:, 0:2 * P].rearrange("p (i q) -> p i q", i=2)
                    split(hbh[:, 2 * g:2 * g + 2, n * P:(n + 1) * P], hbl[:, 2 * g:2 * g + 2, n * P:(n + 1) * P], src)\
                        .then_inc(s.o_done, 1)

            def gated(L):
                for j in range(4, KT):
                    a_tile(L, j)
                for j in range(KT):
                    ga, gb = gate[j], gate[KT + j]
                    dve.wait_ge(s.sig_done, at(L, 16, KT + j + 1))
                    read_tile(Block1, L, T_B + j, gb[:], gb)
                    dve.drain()
                    dve.tensor_tensor(ga[:], ga[:], gb[:], ALU.add)
                    dve.drain()
                    split(xh[:, j, :], xl[:, j, :], ga[:]).then_inc(s.mixed_ready, 1)
                for j in range(KT):
                    add_x(Block1, L, T_OUT + j, j)

            def ple(L):
                norm(Block1, L, 3, par1[:, R_PLE:R_PLE + KT])
                for j in range(KT):
                    scaled_tile(Block1, L, 3, T_PLE + j, gate_sg[:, j, :])
                dve.wait_ge(s.p_turned, at(L, 1, 1))
                for k in range(2):
                    last = split(pth[:, k, :], ptl[:, k, :], mb[:, k, :])
                last.then_inc(s.pt_split, 1)
                for j in range(KT):
                    dve.wait_ge(s.sg_done, at(L, KT, j + 1))
                    read_tile(Block1, L, T_PLE + KT + j, tmp[j % 4][:], gate_sg[:, j, :], inc=3 if j == KT - 1 else 1)
                    dve.drain()
                    dve.tensor_tensor(x_sb[:, j, :], x_sb[:, j, :], tmp[j % 4][:], ALU.add)

            with dve.Fori(0, 2) as L:
                dve.tensor_copy(par1[:], p1[:, bass.ds(L * R1, R1)])
                dve.tensor_copy(b_gate_now[:, None, :], b_gate[:, bass.ds(L, 1), :])
                dve.tensor_copy(sinks_now[:, None, :], sinks[:, bass.ds(L, 1), :])
                dve.drain()
                ffn(L, 0, par1[:, R_FFN1:R_FFN1 + KT], T_FFN1, 0)
                dve.wait_ge(s.gate_landed, at(L, 16, 16))
                split(gate_h[:], gate_l[:], gate_raw[:]).then_inc(s.gate_split, 1)
                norm(Block1, L, 1, par1[:, R_MIX:R_MIX + KT])
                for u in range(12):
                    more_in(L, u)
                mlstm(L)
                dve.wait_ge(s.toep_in, 16)
                swa(L)
                gated(L)
                ffn(L, 2, par1[:, R_FFN2:R_FFN2 + KT], T_FFN2, FT)
                ple(L)

            def more_in2(L, u):
                tile = ORDER2[u]
                rows = (0, MLA_D) if u == U_DT else (0, P)
                scaled_tile(Block2, L, 0, T2_IN + u, proj2[rows[0]:rows[1], tile, :], rows=rows)

            def convolve(L, k):
                more_in2(L, 4 + k)
                w = lambda tap: par2[:, Q_CW + 5 * tap + k:Q_CW + 5 * tap + k + 1]
                dve.drain()
                dve.tensor_scalar(conv[:, k, :], proj2[:, 7 + k, :], w(3), par2[:, Q_CB + k:Q_CB + k + 1], ALU.mult,
                                  ALU.add)
                for tap in range(3):
                    lag = 3 - tap
                    dve.drain()
                    last = dve.scalar_tensor_tensor(out=conv[:, k, lag:S], in0=proj2[:, 7 + k, 0:S - lag], scalar=w(tap),
                                                    in1=conv[:, k, lag:S], op0=ALU.mult, op1=ALU.add)
                return last

            def gmlp(L):
                for u in range(4):
                    more_in2(L, u)
                for k in range(2):
                    convolve(L, k)
                dve.wait_ge(s.gv_ss, at(L, 1, 1))
                invert(tmp[0][:], B4, 1.0 / (2 * P)).then_inc(s.gv_inv, 1)
                dve.wait_ge(s.ws_turned, at(L, 1, 1))
                dve.tensor_tensor(ws_t[:], B7.rearrange("p (h t) -> p h t", h=4),
                                  tri_st[:, None, :].to_broadcast([P, 4, P]), ALU.mult).then_inc(s.ws_copied, 1)
                convolve(L, 2)
                dve.wait_ge(s.gv_rs, at(L, 1, 1))
                for k in range(2):
                    last = dve.scalar_tensor_tensor(out=proj2[:, 2 + k, :], in0=proj2[:, 2 + k, :],
                                                    scalar=par2[:, Q_GV + k:Q_GV + k + 1], in1=tmp[1][:], op0=ALU.mult,
                                                    op1=ALU.mult)
                last.then_inc(s.gv_normed, 1)
                convolve(L, 3)
                dve.wait_ge(s.gv_turned, at(L, 1, 1))
                for q in range(2):
                    last = dve.tensor_copy(gv_tok[:, 2 * q:2 * q + 2, :].rearrange("p t c -> p (t c)"), mb[:, 1 + q, :])
                last.then_inc(s.gv_copied, 1)
                convolve(L, 4).then_inc(s.conv_done, 1)
                more_in2(L, U_DT)
                dve.drain()
                dve.tensor_scalar(tmp[2][0:SSD_H, :], proj2[0:SSD_H, 12, :], dt_now[:, 0:1], None, ALU.add)\
                   .then_inc(s.dt_pre, 1)
                dve.wait_ge(s.gm_psum, at(L, 1, 1))
                for k in range(2):
                    last = dve.tensor_tensor(proj2[:, k, :], mb[:, k, :], proj2[:, k, :], ALU.mult)
                last.then_inc(s.gm_done, 1)

            def ssd(L):
                pre, e1 = tmp[2][0:SSD_H, :], tmp[3][0:SSD_H, :]
                more_in2(L, U_Z)
                dve.wait_ge(s.xs_turned, at(L, 1, 1))
                for t in range(NT):
                    last = dve.tensor_copy(xs_tok[:, t, :], mb[:, t, 0:384])
                last.then_inc(s.xs_copied, 1)
                dve.wait_ge(s.dt_log, at(L, 1, 1))
                dve.scalar_tensor_tensor(out=var[0:SSD_H, :], in0=pre, scalar=0.0, in1=e1, op0=ALU.max, op1=ALU.add)
                dve.tensor_scalar(small[0:SSD_H, 2:3], small[0:SSD_H, 1:2], -1.0, None, ALU.mult)
                dve.drain()
                dve.tensor_scalar(tmp[0][0:SSD_H, :], var[0:SSD_H, :], small[0:SSD_H, 2:3], None, ALU.mult)
                dve.drain()
                dve.tensor_tensor_scan(acc[0:SSD_H, :], ones[0:SSD_H, 0:1].to_broadcast([SSD_H, S]), tmp[0][0:SSD_H, :], 0.0,
                                       ALU.mult, ALU.add).then_inc(s.dt_rows_done, 1)
                more_in2(L, U_Z + 1)
                dve.wait_ge(s.dcol_turned, at(L, 1, 1))
                dve.tensor_scalar(a_col[:].rearrange("p t h -> p (t h)"), B5[:, 0:NT * SSD_H], -1.0, None, ALU.mult)
                dve.tensor_copy(dt_col[:].rearrange("p t h -> p (t h)"), B5[:, 64:64 + NT * SSD_H]).then_inc(s.dcol_copied, 1)
                dve.drain()

                def products(g):
                    for j in range(NT):
                        o, w = ML_OFF[j], S - j * P
                        dve.wait_ge(s.cb_ready, at(L, 8, 4 * g + j + 1))
                        dve.tensor_copy(cb[:, o:o + w], B5[:, 0:w]).then_inc(s.cb_copied, 1)

                def decays(h):
                    dve.wait_ge(s.abc_ready, at(L, SSD_H, h + 1))
                    dve.tensor_copy(tmp[0][:], B4)
                    dve.tensor_tensor(tmp[1][:].rearrange("p (t q) -> p t q", t=NT), B4.rearrange("p (t q) -> p t q", t=NT),
                                      mask_sq[:, None, :].to_broadcast([P, NT, P]), ALU.add).then_inc(s.abc_copied, 1)

                def latent(k):
                    more_in2(L, U_C + k)
                    hi, lo = (cqh[:, k, :], cql[:, k, :]) if k < 3 else (ckh[:, k - 3, :], ckl[:, k - 3, :])
                    g = par2[:, Q_CQ + k:Q_CQ + k + 1]
                    dve.drain()
                    dve.tensor_scalar(hi, proj2[:, 13 + k, :], g, None, ALU.mult)
                    dve.drain()
                    return dve.scalar_tensor_tensor(out=lo, in0=proj2[:, 13 + k, :], scalar=g, in1=hi.bitcast(F32),
                                                    op0=ALU.mult, op1=ALU.subtract)

                decays(0)
                more_in2(L, U_Z + 2)
                latent(0)
                for h in range(SSD_H):
                    tile = h // 2
                    if h % 3 == 0:
                        products(h // 3)
                        dve.drain()
                    for j in range(NT):
                        o, w = ML_OFF[j], S - j * P
                        dve.wait_ge(s.sw_ready, at(L, 24, 4 * h + j + 1))
                        if h and j == 0:
                            dve.wait_ge(s.y_psum, at(L, SSD_H, h))
                        dve.scalar_tensor_tensor(out=sd_p[:, o:o + w], in0=cb[:, o:o + w], scalar=dt_col[:, j, h:h + 1],
                                                 in1=sd_w[:, o:o + w], op0=ALU.mult, op1=ALU.mult).then_inc(s.sp_ready, 1)
                    if h < SSD_H - 1:
                        decays(h + 1)
                    if h < 3:
                        latent(1 + h)
                    elif h == 3:
                        latent(4).then_inc(s.c_split, 1)
                    if h % 2:
                        dve.wait_ge(s.y_psum, at(L, SSD_H, h + 1))
                        if h == 1:
                            dve.wait_ge(s.z_silu, at(L, 1, 1))
                        dve.scalar_tensor_tensor(out=conv[:, tile, :], in0=conv[:, tile, :], scalar=d_skip_now[:, tile:tile + 1],
                                                 in1=mb[:, 2 + tile % 2, :], op0=ALU.mult, op1=ALU.add)
                        dve.drain()
                        dve.tensor_tensor(conv[:, tile, :], proj2[:, 4 + tile, :], conv[:, tile, :], ALU.mult)\
                           .then_inc(s.y_done, 1)

            def mla(L):
                B = Block2
                dve.wait_ge(s.c_ss, at(L, 1, 1))
                dve.tensor_scalar(tmp[2][:], B4, 1.0 / 384, EPS, ALU.mult, ALU.add)
                dve.tensor_scalar(tmp[3][:], B5, 1.0 / 256, EPS, ALU.mult, ALU.add)
                dve.wait_ge(s.y_ss, at(L, 1, 1))
                dve.tensor_scalar(tmp[0][:], B7, 1.0 / 192, EPS, ALU.mult, ALU.add)
                dve.drain()
                dve.reciprocal(tmp[2][:], tmp[2][:])
                dve.reciprocal(tmp[3][:], tmp[3][:]).then_inc(s.c_inv, 1)
                dve.reciprocal(tmp[0][:], tmp[0][:]).then_inc(s.y_inv, 1)
                rows = slice(64, MLA_D)
                dve.wait_ge(s.rot_psum, at(L, 1 + MLA_H, 1))
                dve.tensor_tensor(rot_sin[rows, :], B5[rows, :], rope[rows, 1, :], ALU.mult).then_inc(s.rot_read, 1)
                dve.tensor_tensor(k_rot[rows, :], proj2[rows, 12, :], rope[rows, 0, :], ALU.mult)
                dve.drain()
                dve.tensor_tensor(k_rot[rows, :], k_rot[rows, :], rot_sin[rows, :], ALU.add).then_inc(s.rot_done, 1)
                for k in range(2):
                    split(xh[:, k, :], xl[:, k, :], proj2[:, k, :])
                dve.drain()
                dve.wait_ge(s.c_rs, at(L, 1, 1))
                for h in range(MLA_H):
                    read_tile(B, L, T2_QB + h, q96[:, h, :], acc, rows=(0, MLA_D))
                dve.wait_ge(s.y_bc, at(L, 1, 1))
                for k, scale in enumerate((B6, tmp[0][:], B7)):
                    dve.scalar_tensor_tensor(out=tmp[1][:], in0=conv[:, k, :], scalar=par2[:, Q_SSD + k:Q_SSD + k + 1],
                                             in1=scale, op0=ALU.mult, op1=ALU.mult)
                    dve.drain()
                    last = split(xh[:, 2 + k, :], xl[:, 2 + k, :], tmp[1][:])
                    dve.drain()
                last.then_inc(s.ssd_done, 1)
                for h in range(MLA_H):
                    t = T2_KVB + h
                    src = bank[(B.base_tile + t) % TILE_BANKS]
                    dve.wait_ge(s.tile_ready, tiles_in(B, L, t))
                    if h >= 2:
                        dve.wait_ge(s.vt_psum, at(L, MLA_H, h - 1))
                    dve.tensor_tensor(k96[0:64, h, :], src[0:64, :], var[0:64, :], ALU.mult)
                    dve.tensor_copy(k96[64:MLA_D, h, :], k_rot[64:MLA_D, :])
                    dve.tensor_tensor(v_ft[64:P, h % 2, :], src[64:P, :], var[64:P, :], ALU.mult).then_inc(s.tile_evacuated, 1)
                    dve.drain().then_inc(s.kv_done, 1)
                    if h < 2:
                        rotate(L, h)
                        continue
                    turned_v(L, h - 2)
                    rotate(L, h)
                turned_v(L, MLA_H - 2)
                turned_v(L, MLA_H - 1)

                def biggest(c):
                    n = c % NT
                    dve.wait_ge(s.al_ready, at(L, 24, c + 1))
                    dve.tensor_reduce(small[:, 40 + n:41 + n], bank[c % TILE_BANKS][:, 0:(n + 1) * P], AX.X, ALU.max)
                    dve.drain()
                    dve.tensor_scalar(small[:, 32 + n:33 + n], small[:, 40 + n:41 + n], -MLA_SCALE, None, ALU.mult)\
                       .then_inc(s.am_ready, 1)

                def normed(c):
                    n = c % NT
                    dve.wait_ge(s.ae_ready, at(L, 24, c + 1))
                    dve.reciprocal(small[:, 44 + n:45 + n], small[:, 36 + n:37 + n])
                    dve.drain()
                    w = (n + 1) * P
                    dve.tensor_scalar(prob[:, c % 4, 0:w], prob[:, c % 4, 0:w], small[:, 44 + n:45 + n], None, ALU.mult)\
                       .then_inc(s.ap_ready, 1)

                def copied(c):
                    h, n = c // NT, c % NT
                    dve.wait_ge(s.at_ready, at(L, 24, c + 1))
                    if n == 0 and h >= 2:
                        dve.wait_ge(s.ao_ready, at(L, MLA_H, h - 1))
                    dve.tensor_copy(prob_t[h % 2][:, 0:n + 1, n * P:(n + 1) * P],
                                    mb[:, c % 2, 0:(n + 1) * P].rearrange("p (j q) -> p j q", j=n + 1))\
                       .then_inc(s.at_copied, 1)

                def head_split(h):
                    half = 64 * (h % 2)
                    dve.wait_ge(s.ao_ready, at(L, MLA_H, h + 1))
                    split(xh[half:half + 64, 5 + h // 2, :], xl[half:half + 64, 5 + h // 2, :],
                          mb[half:half + 64, 2 + h % 2, :]).then_inc(s.ao_done, 1)

                blocks = NT * MLA_H
                biggest(0)
                biggest(1)
                for c in range(blocks):
                    if c + 2 < blocks:
                        biggest(c + 2)
                    normed(c)
                    copied(c)
                    if c >= NT and c % NT == 1:
                        head_split(c // NT - 1)
                head_split(MLA_H - 1)

            def rotate(L, h):
                dve.wait_ge(s.rot_psum, at(L, 1 + MLA_H, h + 2))
                dve.tensor_tensor(rot_sin[0:MLA_D, :], mb[0:MLA_D, 2 + (h + 1) % 2, :], rope[:, 1, :], ALU.mult)\
                   .then_inc(s.rot_read, 1)
                dve.tensor_tensor(q96[:, h, :], q96[:, h, :], rope[:, 0, :], ALU.mult)
                dve.drain()
                dve.tensor_tensor(q96[:, h, :], q96[:, h, :], rot_sin[0:MLA_D, :], ALU.add).then_inc(s.rot_done, 1)
                dve.drain()

            def turned_v(L, h):
                dve.wait_ge(s.vt_psum, at(L, MLA_H, h + 1))
                dve.tensor_copy(v_tok[:, :, h * 64:h * 64 + 64], mb[:, h % 2, 0:NT * 64].rearrange("p (t c) -> p t c", t=NT))\
                   .then_inc(s.vt_copied, 1)

            with dve.Fori(0, 2) as L:
                B = Block2
                dve.tensor_copy(par2[:], p2[:, bass.ds(L * R2, R2)])
                dve.tensor_copy(d_skip_now[:, None, :], d_skip[:, bass.ds(L, 1), :])
                dve.tensor_copy(dt_now[:, 0:1], dt_bias[:, bass.ds(L, 1)])
                dve.tensor_copy(dt_now[:, 1:2], dt_a[:, bass.ds(L, 1)])
                dve.tensor_copy(bs_now[:, None, :], bs_rows[:, bass.ds(L, 1), :])
                dve.drain()
                norm(B, L, 0, par2[:, Q_MIX:Q_MIX + KT])
                gmlp(L)
                ssd(L)
                mla(L)
                for j in range(KT):
                    add_x(B, L, T2_OUT + j, j)
                norm(B, L, 1, par2[:, Q_MLP:Q_MLP + KT])
                for half in range(2):
                    t0 = T2_MLP + half * (HALF2 + 8)
                    with dve.Fori(0, HALF2 // 4) as i:
                        for f in range(4):
                            ta, tb = tmp[f % 2], tmp[2 + f % 2]
                            scaled_tile(B, L, 1, t0 + f, ta[:], i, 4)
                            dve.drain()
                            dve.scalar_tensor_tensor(out=tb[:], in0=ta[:], scalar=0.0, in1=ta[:], op0=ALU.max, op1=ALU.mult)
                            dve.drain()
                            j = i * 4 + f
                            split(hh[:, j, :], hl[:, j, :], tb[:]).then_inc(s.hidden_ready, 1)
                    for j in range(KT):
                        add_x(B, L, t0 + HALF2 + j, j, inc=3 if half and j == KT - 1 else 1)

            dve.drain().then_inc(s.x_final, 1)
            norm_scale(13)
            dve.wait_ge(s.rstd_ready, 13)
            for j in range(KT):
                last = dve.scalar_tensor_tensor(out=y_sb[:, j, :], in0=x_sb[:, j, :], scalar=p2[:, 2 * R2 + j:2 * R2 + j + 1],
                                                in1=rstd[:], op0=ALU.mult, op1=ALU.mult)
            last.then_inc(s.fin_y, 1)
            for c in range(2 * NT):
                t, side = c // 2, c % 2
                dve.wait_ge(s.fin_turned, c + 1)
                dve.tensor_copy(out_tok[:, t, side * S:(side + 1) * S], mb[:, c % 4, :]).then_inc(s.fin_copied, 1)


ML_OFF = [0, 512, 896, 1152]
N_SMALL = 2 * (4 + 1 + 4 + 7 + 4) + 1 + 4 + 1 + 1 + 2 + 4


def constants(np):
    pack = np.zeros((P, CONSTS), np.float32)
    r = np.arange(P)
    pack[:, C_IDENT:C_IDENT + P] = np.eye(P)
    for half in range(2):
        pack[64 * half:64 * half + 64, C_SEL + 16 * half:C_SEL + 16 * half + 16] = 1.0
        pack[16 * half::32, C_BACK + 64 * half:C_BACK + 64 * half + 64] = 1.0
    sel4 = (np.arange(ML_H)[:, None] == r[None, :] // 32).astype(np.float32)
    pack[:, C_DUP0:C_DUP0 + P] = r[:, None] == r[None, :] % 64
    pack[:, C_DUP1:C_DUP1 + P] = r[:, None] == 64 + r[None, :] % 64
    pack[:, C_MQS:C_MQS + P] = np.where(r[None, :] <= r[:, None], 0.0, NEG)
    pack[:, C_MSQ:C_MSQ + P] = np.where(r[None, :] >= r[:, None], 0.0, NEG)
    for i in range(16):
        pack[80 + i, C_ROT + 64 + i] = -1.0
        pack[64 + i, C_ROT + 80 + i] = 1.0
    pack[:, C_TRI:C_TRI + P] = r[None, :] >= r[:, None]
    dist = 255 - np.arange(TOEP)
    far = 16 + (np.log(np.maximum(dist, 1) / 16) / np.log(128 / 16) * 16).astype(np.int32)
    bucket = np.where(dist < 16, dist, np.minimum(far, 31))
    inside = (dist >= 0) & (dist < P)
    onehot = ((np.arange(32)[:, None] == bucket[None, :]) & inside[None, :]).astype(np.float32)
    pad = np.broadcast_to(np.where(inside, 0.0, NEG).astype(np.float32), (P, TOEP)).copy()
    rope = np.zeros((MLA_D, 2, S), np.float32)
    rope[:, 0] = 1.0
    inv_freq = np.power(np.float32(10000.0), -np.arange(16, dtype=np.float32) / np.float32(16))
    ang = np.arange(S, dtype=np.float32)[:, None] * inv_freq[None, :]
    for part in (64, 80):
        rope[part:part + 16, 0] = np.cos(ang).T
        rope[part:part + 16, 1] = np.sin(ang).T
    return {"const_pack": pack, "sel4": sel4, "onehot": onehot, "pad": pad, "rope_pack": rope}


_INS = ['x', 'p', 'ffn1_norm', 'ffn1_wi', 'ffn1_wo', 'mix_norm', 'w_in', 'b_igate', 'b_fgate', 'ml_out_norm', 'q_norm',
        'k_norm', 'sinks', 'rel_bias', 'w_a', 'w_b', 'w_out', 'ffn2_norm', 'ffn2_wi', 'ffn2_wo', 'ple_norm', 'w_ple_gate',
        'w_ple', 'norm_mix_g_2', 'w_in_2', 'gmlp_v_norm_g_2', 'gmlp_w_s_2', 'gmlp_b_s_2', 'ssd_conv_w_2', 'ssd_conv_b_2',
        'ssd_dt_bias_2', 'ssd_a_log_2', 'ssd_d_2', 'ssd_norm_g_2', 'mla_q_norm_g_2', 'mla_w_qb_2', 'mla_kv_norm_g_2',
        'mla_w_kvb_2', 'w_out_2', 'norm_mlp_g_2', 'mlp_w1_2', 'mlp_w2_2', 'final_norm_g_2']


def kernel(**inputs):
    import numpy as _np
    import concourse.bacc as _bacc
    from concourse import mybir as _mybir
    from concourse.bass_utils import run_bass_kernel_spmd as _run

    nc = _bacc.Bacc("TRN2", target_bir_lowering=False, num_devices=1)
    arrays, args = {}, {}
    for name, value in [(n, inputs[n]) for n in _INS] + list(constants(_np).items()):
        v = _np.ascontiguousarray(value)
        arrays[f"in_{name}_dram"] = v
        args[name] = nc.dram_tensor(f"in_{name}_dram", v.shape, _mybir.dt.from_np(v.dtype), kind="ExternalInput").ap()
    args["out"] = nc.dram_tensor("out_dram", (1, S, D), _mybir.dt.float32, kind="ExternalOutput").ap()
    program(nc, args)
    r = _run(nc, [arrays], core_ids=[0])
    return r.results[0]["out_dram"]
```

```python
from contextlib import ExitStack

import concourse.bass as bass
from concourse import mybir

F32 = mybir.dt.float32
F32R = mybir.dt.float32r
ALU = mybir.AluOpType
ACT = mybir.ActivationFunctionType
AX = mybir.AxisListType

P = 128
S = 512
D = 1024
KT = D // P
NT = S // P
EPS = 1e-6
NEG = -1e30

D_FF = 2816
FT = D_FF // P
ML_H = 4
SW_H = 8
SW_KV = 2
SW_G = SW_H // SW_KV
GATE_COL = 1536
SQ_COL = 1544
SK_COL = 2056
SV_COL = 2184
GA_COL = 2312
GB_COL = 3336
FT2 = 4 * D // P
HALF2 = FT2 // 2
SSD_H = 6
MLA_H = 6
MLA_D = 96
DT_COL = 1536
CQ_COL = 1542
KR_COL = 2182
MLA_SCALE = 1.0 / float(MLA_D) ** 0.5

RAW_SLOTS = 2
SPLIT_SLOTS = 4
TILE_BANKS = 4
AHEAD = SPLIT_SLOTS - 1
SLAB = 1024

B1_SLABS, B1_TILES = 192, 180
B2_SLABS, B2_TILES = 96, 88
S_FFN1, S_IN, S_GATE, S_A, S_B, S_OUT, S_FFN2, S_PLE = 0, 66, 84, 100, 104, 108, 116, 182
T_FFN1, T_IN, T_GATE, T_A, T_B, T_OUT, T_FFN2, T_PLE = 0, 52, 70, 86, 94, 102, 110, 162
S2_IN, S2_QB, S2_KVB, S2_OUT, S2_MLP = 0, 18, 21, 24, 32
T2_IN, T2_QB, T2_KVB, T2_OUT, T2_MLP = 0, 18, 24, 30, 38
ORDER2 = [0, 1, 2, 3, 7, 8, 9, 10, 11, 12, 4, 5, 6, 13, 14, 15, 16, 17]
U_DT, U_Z, U_C = 9, 10, 13

R_FFN1, R_MIX, R_FFN2, R_PLE, R_MLOUT, R_QN, R_KN, R1 = 0, 8, 16, 24, 32, 36, 37, 38
Q_MIX, Q_MLP, Q_CQ, Q_CKV, Q_SSD, Q_GV, Q_CB, Q_CW, R2 = 0, 8, 16, 19, 21, 24, 26, 31, 51

C_IDENT, C_SEL, C_DUP0, C_DUP1, C_MQS, C_MSQ, C_ROT, C_TRI, C_BACK = [P * n for n in range(9)]
CONSTS = 9 * P

TOEP = 384


class Block1:
    base_slab, slabs, base_tile, tiles = 0, B1_SLABS, 0, B1_TILES
    norms, base_norm = 4, 0


class Block2:
    base_slab, slabs = 2 * B1_SLABS, B2_SLABS
    base_tile, tiles = 2 * B1_TILES, B2_TILES
    norms, base_norm = 2, 8


class Last:
    norms, base_norm = 0, 12


def at(layer, per_layer, const, i=None, step=0):
    e = const if layer is None else layer * per_layer + const
    return e if i is None else e + i * step


def program(nc, a):
    ctx = ExitStack()
    with ctx:
        cursor = [16512]

        def place(name, shape, dt=F32, offset=None):
            size = 4
            for n in shape[1:]:
                size *= n
            if offset is None:
                offset = cursor[0]
                cursor[0] += (size + 31) // 32 * 32
            return nc.alloc_sbuf_tensor_at(name, shape, dt, offset=offset)

        def sem(name):
            return ctx.enter_context(nc.semaphore(name))

        x_sb = place("x_sb", [P, KT, S])
        xh = place("xh", [P, KT, S], F32R)
        xl = place("xl", [P, KT, S], F32R)
        raw = [place(f"raw{n}", [P, SLAB]) for n in range(RAW_SLOTS)]
        wh = [place(f"wh{n}", [P, SLAB], F32R) for n in range(SPLIT_SLOTS)]
        wl = [place(f"wl{n}", [P, SLAB], F32R) for n in range(SPLIT_SLOTS)]
        tmp_all = place("tmp_all", [P, 4, S])
        tmp = [tmp_all[:, n, :] for n in range(4)]
        rstd = place("rstd", [P, S])
        acc = place("acc", [P, S])
        var = place("var", [P, S])
        const = place("const", [P, CONSTS])
        sel4 = place("sel4", [ML_H, P])
        ones = place("ones", [P, P])
        p1 = place("p1", [P, 2 * R1])
        p2 = place("p2", [P, 2 * R2 + KT])
        par1 = place("par1", [P, R1])
        par2 = place("par2", [P, R2])
        first_gains = place("first_gains", [P, 5 * KT])
        gate_raw = place("gate_raw", [P, KT, 8])
        gate_h = place("gate_h", [P, KT, 8], F32R)
        gate_l = place("gate_l", [P, KT, 8], F32R)
        b_gate = place("b_gate", [ML_H, 2, 2])
        b_gate_now = place("b_gate_now", [ML_H, 2])
        sinks = place("sinks", [P, 2, SW_H])
        sinks_now = place("sinks_now", [P, SW_H])
        c_col = place("c_col", [P, NT, ML_H])
        small = place("small", [P, 64])
        g_first = small[:, 48:48 + KT]
        d_skip = place("d_skip", [P, 2, 3])
        d_skip_now = place("d_skip_now", [P, 3])
        dt_bias = place("dt_bias", [SSD_H, 2])
        dt_a = place("dt_a", [SSD_H, 2])
        dt_now = place("dt_now", [SSD_H, 2])
        bs_rows = place("bs_rows", [4, 2, P])
        bs_now = place("bs_now", [4, P])
        a_col = place("a_col", [P, NT, SSD_H])
        dt_col = place("dt_col", [P, NT, SSD_H])
        bias_at = cursor[0]
        bias = place("bias", [P, SW_H, 2 * P])
        rope = place("rope", [MLA_D, 2, S], offset=bias_at)
        region = cursor[0]

        def at_kb(name, kb, shape, dt=F32):
            return place(name, shape, dt, offset=region + int(kb * 1024))

        hh = at_kb("hh", 0, [P, FT, S], F32R)
        hl = at_kb("hl", 44, [P, FT, S], F32R)
        x_tok = at_kb("x_tok", 0, [P, NT, D])
        rows1 = at_kb("rows1", 16, [R1, 2, P])
        rows2 = at_kb("rows2", 17, [R2, 2, P])
        rows3 = at_kb("rows3", 18, [KT, P])
        onehot = at_kb("onehot", 19, [32, TOEP])
        pad = at_kb("pad", 21, [SW_H, TOEP])
        rel = at_kb("rel", 23, [32, SW_H])
        toep = at_kb("toep", 24, [SW_H, TOEP])
        proj = at_kb("proj", 0, [P, 18, S])
        hah = at_kb("hah", 0, [P, ML_H, S], F32R)
        hal = at_kb("hal", 8, [P, ML_H, S], F32R)
        hbh = at_kb("hbh", 16, [P, 4, S], F32R)
        mv_tok = at_kb("mv_tok", 36, [P, NT, S])
        sv_tok = at_kb("sv_tok", 36, [P, NT, P])
        kk = at_kb("kk", 38, [P, SW_KV, S])
        num_sb = at_kb("num_sb", 50, [P, ML_H, S])
        hbl = at_kb("hbl", 50, [P, 4, S], F32R)
        ml_w = at_kb("ml_w", 58, [P, 1280])
        ml_p = at_kb("ml_p", 63, [P, 1280])
        neg_m = at_kb("neg_m", 76, [P, S])
        neg_md = at_kb("neg_md", 78, [P, S])
        gate = [at_kb(f"gate{n}", kb, [P, S])
                for n, kb in enumerate((80, 82, 84, 86, 44, 46, 48, 42, 58, 60, 62, 64, 66))] + tmp[0:3]
        ml_rows = [at_kb(f"ml_row{n}", 68 + 2 * n, [ML_H, S]) for n in range(4)]
        ml_rows += [at_kb(f"ml_row{4 + n}", 58 + 2 * n, [ML_H, S]) for n in range(5)]
        qk_sq = at_kb("qk_sq", 58, [P, 5, S])
        lg = at_kb("lg", 68, [P, 2, SW_G, 2 * P])
        pt_sb = at_kb("pt_sb", 76, [P, 2, SW_G, P])
        mh = at_kb("mh", 24, [P, KT, S], F32R)
        ml = at_kb("ml", 0, [P, KT, S], F32R)
        gate_sg = at_kb("gate_sg", 0, [P, KT, S])
        p_tok = at_kb("p_tok", 16, [P, NT, 2 * P])
        pth = at_kb("pth", 20, [P, 2, S], F32R)
        ptl = at_kb("ptl", 24, [P, 2, S], F32R)
        proj2 = at_kb("proj2", 0, [P, 18, S])
        q96 = at_kb("q96", 0, [MLA_D, MLA_H, S])
        k96 = at_kb("k96", 12, [MLA_D, MLA_H, S])
        conv = at_kb("conv", 36, [P, 5, S])
        xs_tok = at_kb("xs_tok", 46, [P, NT, 384])
        v_tok = at_kb("v_tok", 46, [P, NT, 384])
        cqh = at_kb("cqh", 52, [P, 3, S], F32R)
        cql = at_kb("cql", 58, [P, 3, S], F32R)
        ckh = at_kb("ckh", 64, [P, 2, S], F32R)
        ckl = at_kb("ckl", 68, [P, 2, S], F32R)
        gv_sq = at_kb("gv_sq", 72, [P, 2, S])
        gv_tok = at_kb("gv_tok", 76, [P, NT, 2 * P])
        ws_t = at_kb("ws_t", 80, [P, 4, P])
        ws_raw = at_kb("ws_raw", 82, [P, 4, P])
        cb = at_kb("cb", 72, [P, 1280])
        sd_w = at_kb("sd_w", 77, [P, 1280])
        sd_p = at_kb("sd_p", 82, [P, 1280])
        y_sq = at_kb("y_sq", 77, [P, 3, S])
        c_sq = at_kb("c_sq", 14, [P, 5, S])
        k_rot = at_kb("k_rot", 26, [P, S])
        rot_sin = at_kb("rot_sin", 28, [P, S])
        v_ft = at_kb("v_ft", 30, [P, 2, S])
        prob = at_kb("prob", 60, [P, 4, S])
        prob_t = [at_kb(f"prob_t{n}", kb, [P, NT, S]) for n, kb in ((0, 72), (1, 52))]
        y_sb = at_kb("y_sb", 16, [P, KT, S])
        out_tok = at_kb("out_tok", 32, [P, NT, D])
        assert region + 88 * 1024 <= nc.sbuf_usable_end, (region + 88 * 1024, nc.sbuf_usable_end)

        ident = const[:, C_IDENT:C_IDENT + P]
        dup = [const[:, c:c + P] for c in (C_DUP0, C_DUP1)]
        mask_qs = const[:, C_MQS:C_MQS + P]
        mask_sq = const[:, C_MSQ:C_MSQ + P]
        rot96 = const[0:MLA_D, C_ROT:C_ROT + MLA_D]
        tri_st = const[:, C_TRI:C_TRI + P]

        bank = [ctx.enter_context(nc.psum_tensor(f"bank{n}", [P, S], F32)) for n in range(4)]
        mb = ctx.enter_context(nc.psum_tensor("mb", [P, 4, S], F32))
        B4, B5, B6, B7 = (mb[:, n, :] for n in range(4))

        scratch = nc.dram_tensor("toeplitz_rows", [SW_H, P, TOEP], F32, kind="Internal").ap()

        names = """split_done slab_used hi_ready tile_ready tile_evacuated setup_x setup_const setup_small setup_rel
            setup_t setup_copied rel_psum toep_row toep_out toep_in consts_ready
            x_final sq_ready ss_ready ss_psum inv_var rstd_ready xl_ready
            silu_done hidden_ready gate_landed gate_split gates_psum gate_pre log1p ml_rows_done emt_done
            v_turned v_copied c_turned c_copied bc_ready bc_copied w_ready sc_ready p_ready pv_done abs_done
            head_done num_sq ml_ss ml_inv ml_rs ml_bc ml_bc_read mo_done ha_rounded ha_ready
            qk_squared qk_ss qk_inv qk_rs qk_bc qk_bc_read qk_normed kk_psum kk_copied
            lg_ready lg_read mx_ready ex_ready pn_ready pt_ready pt_copied o_ready o_done
            sig_done mixed_ready p_landed p_turned pt_split sg_done kr_landed
            gelu_done gv_squared gv_ss gv_inv gv_rs gv_normed gv_turned gv_copied ws_landed ws_turned ws_copied
            gm_psum gm_done conv_done conv_silu z_silu xs_turned xs_copied
            dt_pre dt_log dt_rows_done dcol_turned dcol_copied cb_ready cb_copied abc_ready abc_copied sw_ready
            sp_ready y_psum y_done y_squared y_ss y_inv y_rs y_bc y_bc_read y_scaled y_rounded ssd_done
            c_squared c_ss c_inv c_rs c_bc c_scaled c_split rope_landed rot_psum rot_read rot_done
            kv_done key_rows vt_psum vt_copied al_ready am_ready ae_ready ap_ready at_ready at_copied ao_ready ao_done
            fin_y fin_turned fin_copied stored""".split()
        sm = {n: sem(n) for n in names}
        raw_landed = [sem(f"raw_landed{n}") for n in range(RAW_SLOTS)]
        s = type("Sems", (), sm)

        def tiles_out(B, L, t, i=None, step=0):
            return at(L, B.tiles, B.base_tile + t + 1 + TILE_BANKS, i, step)

        def tiles_in(B, L, t, i=None, step=0):
            return at(L, B.tiles, B.base_tile + t + 1, i, step)

        def norm_no(B, L, k):
            return at(L, B.norms, B.base_norm + k + 1)

        def half_no(B, L, k, half):
            return at(L, 2 * B.norms, 2 * (B.base_norm + k) + half + 1)

        block = ctx.enter_context(nc.Block())

        @block.sync
        def _(sp):
            def load(B, L, n, view, src, i=None, step=0):
                need = sp.lower_val(at(L, B.slabs, B.base_slab + n + 1, i, step))
                sp.dma_start(view(raw[n % RAW_SLOTS]), src).wait_op(s.split_done, need, "sem-ge")\
                  .then_inc(raw_landed[n % RAW_SLOTS], 16)

            def as3(kt, c):
                return lambda r: r[:, 0:kt * c].rearrange("p (k c) -> p k c", k=kt)

            def cols(w, L, c0, width, i=None, step=0):
                c = c0 if i is None else i * step + c0
                sl = slice(c0, c0 + width) if i is None else bass.ds(c, width)
                return w[bass.ds(L, 1), :, sl].rearrange("l (k p) c -> p (l k) c", p=P)

            def rows2c(w, L, r0, c0, i=None, step=0):
                sl = slice(r0, r0 + 2 * P) if i is None else bass.ds(i * step + r0, 2 * P)
                return w[bass.ds(L, 1), sl, c0:c0 + S].rearrange("l (k p) c -> p (l k) c", p=P)

            sp.dma_start(const[:], a["const_pack"]).then_inc(s.setup_const, 16)
            sp.dma_start(x_tok[:], a["x"].rearrange("b (t p) d -> p (b t) d", p=P)).then_inc(s.setup_x, 16)

            def ffn(L, wi, wo, n):
                with sp.Fori(0, FT // 2) as i:
                    for f in range(2):
                        for part in range(2):
                            load(Block1, L, n + 2 * f + part, as3(KT, P),
                                 cols(wi, L, part * D_FF + f * P, P, i, 2 * P), i, 4)
                for half in range(2):
                    n0 = n + 2 * FT + half * (FT // 2)
                    with sp.Fori(0, 2) as i:
                        for q in range(4):
                            load(Block1, L, n0 + q, as3(2, S), rows2c(wo, L, q * 2 * P, half * S, i, 8 * P), i, 4)
                    for q in range(8, FT // 2):
                        load(Block1, L, n0 + q, as3(2, S), rows2c(wo, L, q * 2 * P, half * S))

            with sp.Fori(0, 2) as L:
                need = sp.lower_val(L + 1)
                with nc.allow_non_contiguous_dma("eight columns"):
                    sp.dma_start(gate_raw[:], cols(a["w_in"], L, GATE_COL, 8)).wait_op(s.gate_split, need, "sem-ge")\
                      .then_inc(s.gate_landed, 16)
                ffn(L, a["ffn1_wi"], a["ffn1_wo"], S_FFN1)
                with sp.Fori(0, 3) as i:
                    for u in range(4):
                        load(Block1, L, S_IN + u, as3(KT, P), cols(a["w_in"], L, u * P, P, i, 4 * P), i, 4)
                for u in range(6):
                    load(Block1, L, S_IN + 12 + u, as3(KT, P), cols(a["w_in"], L, SQ_COL + u * P, P))
                with sp.Fori(0, 4) as i:
                    for u in range(4):
                        load(Block1, L, S_GATE + u, as3(KT, P), cols(a["w_in"], L, GA_COL + u * P, P, i, 4 * P), i, 4)
                for n, w in ((S_A, "w_a"), (S_B, "w_b")):
                    for u in range(4):
                        load(Block1, L, n + u, as3(4, 2 * P), cols(a[w], L, u * 2 * P, 2 * P))
                with sp.Fori(0, 2) as i:
                    for j in range(4):
                        load(Block1, L, S_OUT + j, as3(KT, P), cols(a["w_out"], L, j * P, P, i, 4 * P), i, 4)
                ffn(L, a["ffn2_wi"], a["ffn2_wo"], S_FFN2)
                for j in range(KT):
                    if j == 5:
                        need = sp.lower_val(tiles_out(Block1, L, T_FFN2 + 51))
                        sp.dma_start(p_tok[:], a["p"][bass.ds(L, 1), 0].rearrange("l (t p) c -> p (l t) c", p=P))\
                          .wait_op(s.tile_evacuated, need, "sem-ge").then_inc(s.p_landed, 16)
                    load(Block1, L, S_PLE + j, as3(KT, P), cols(a["w_ple_gate"], L, j * P, P))
                for d in range(2):
                    load(Block1, L, S_PLE + 8 + d, as3(2, S), cols(a["w_ple"], L, d * S, S))

            sp.wait_ge(s.lg_read, 16)
            sp.dma_start(rope[:], a["rope_pack"]).then_inc(s.rope_landed, 16)
            with sp.Fori(0, 2) as L:
                B = Block2
                w_in = a["w_in_2"]
                view = lambda c0, c1: (lambda r: r[:, 0:KT * MLA_D].rearrange("p (k c) -> p k c", k=KT)[:, :, c0:c1])
                for u, tile in enumerate(ORDER2):
                    if u == 4:
                        need = sp.lower_val(at(L, B.tiles, B.base_tile + TILE_BANKS))
                        sp.dma_start(ws_raw[:], a["gmlp_w_s_2"][bass.ds(L, 1)].rearrange("l h t s -> t (l h) s"))\
                          .wait_op(s.tile_evacuated, need, "sem-ge").then_inc(s.ws_landed, 16)
                    if u == U_DT:
                        with nc.allow_non_contiguous_dma("six columns"):
                            load(B, L, S2_IN + u, view(0, SSD_H), cols(w_in, L, DT_COL, SSD_H))
                            sp.dma_start(view(64, MLA_D)(raw[(S2_IN + u) % RAW_SLOTS]), cols(w_in, L, KR_COL, 32))\
                              .then_inc(s.kr_landed, 16)
                    else:
                        c0 = tile * P if tile < 12 else CQ_COL + (tile - 13) * P
                        load(B, L, S2_IN + u, as3(KT, P), cols(w_in, L, c0, P))
                for u in range(3):
                    load(B, L, S2_QB + u, as3(3, 2 * MLA_D), cols(a["mla_w_qb_2"], L, u * 2 * MLA_D, 2 * MLA_D))
                for u in range(3):
                    load(B, L, S2_KVB + u, as3(2, 2 * P), cols(a["mla_w_kvb_2"], L, u * 2 * P, 2 * P))
                with sp.Fori(0, 2) as i:
                    for j in range(4):
                        load(B, L, S2_OUT + j, as3(KT, P), cols(a["w_out_2"], L, j * P, P, i, 4 * P), i, 4)
                for half in range(2):
                    n0 = S2_MLP + half * 2 * HALF2
                    with sp.Fori(0, HALF2 // 4) as i:
                        for f in range(4):
                            load(B, L, n0 + f, as3(KT, P),
                                 cols(a["mlp_w1_2"], L, (half * HALF2 + f) * P, P, i, 4 * P), i, 4)
                    for dh in range(2):
                        with sp.Fori(0, 2) as i:
                            for q in range(4):
                                load(B, L, n0 + HALF2 + 8 * dh + q, as3(2, S),
                                     rows2c(a["mlp_w2_2"], L, half * HALF2 * P + q * 2 * P, dh * S, i, 8 * P), i, 4)

            for t in range(NT):
                sp.wait_ge(s.fin_copied, 2 * t + 2)
                sp.dma_start(a["out"][0, t * P:(t + 1) * P, :], out_tok[:, t, :]).then_inc(s.stored, 16)
            sp.wait_ge(s.stored, 16 * NT)

        @block.gpsimd
        def _(gp):
            gp.memset(ones[:], 1.0).then_inc(s.consts_ready, 1)
            gp.sem_inc(s.split_done, RAW_SLOTS)
            gp.sem_inc(s.slab_used, AHEAD)
            gp.sem_inc(s.tile_evacuated, TILE_BANKS)
            gp.sem_inc(s.gate_split, 1)
            total = 2 * (B1_SLABS + B2_SLABS)
            with gp.Fori(0, total // SPLIT_SLOTS) as n:
                for j in range(SPLIT_SLOTS):
                    gp.wait_ge(s.hi_ready, n * SPLIT_SLOTS + j + 1)
                    gp.tensor_tensor(wl[j][:], raw[j % RAW_SLOTS][:], wh[j][:].bitcast(F32), ALU.subtract)\
                      .then_inc(s.split_done, 1)

        @block.tensor
        def _(pe):
            def take_slab(B, L, n, i=None, step=0):
                pe.wait_ge(s.split_done, at(L, B.slabs, B.base_slab + n + 1 + RAW_SLOTS, i, step))
                return wh[n % SPLIT_SLOTS], wl[n % SPLIT_SLOTS]

            def open_tile(B, L, t, i=None, step=0):
                pe.wait_ge(s.tile_evacuated, at(L, B.tiles, B.base_tile + t + 1, i, step))
                return bank[(B.base_tile + t) % TILE_BANKS]

            def three(out, ah, al, bh, bl, first, last, new=False):
                one = pe.matmul(out, ah, bh, start=first, stop=False)
                if new:
                    one.then_inc(s.slab_used, 1)
                pe.matmul(out, ah, bl, start=False, stop=False)
                return pe.matmul(out, al, bh, start=False, stop=last)

            def unit(B, L, n, t, rh, rl, i=None, step=0, tstep=None, wait_k=None, width=P, kts=KT, c0=0, pitch=P,
                     new=True, inc=1, part_ready=s.xl_ready):
                tstep = step if tstep is None else tstep
                if new:
                    take_slab(B, L, n, i, step)
                out = open_tile(B, L, t, i, tstep)
                h, l = wh[n % SPLIT_SLOTS], wl[n % SPLIT_SLOTS]
                for k in range(kts):
                    if wait_k is not None:
                        pe.wait_ge(part_ready, wait_k(k))
                    c = k * pitch + c0
                    first = pe.matmul(out[0:width, :], h[:, c:c + width], rh[:, k, :], start=k == 0, stop=False)
                    if new and k == 0:
                        first.then_inc(s.slab_used, 1)
                    pe.matmul(out[0:width, :], h[:, c:c + width], rl[:, k, :], start=False, stop=False)
                    if k < kts - 1:
                        pe.matmul(out[0:width, :], l[:, c:c + width], rh[:, k, :], start=False, stop=False)
                last = pe.matmul(out[0:width, :], l[:, c:c + width], rh[:, kts - 1, :], start=False, stop=True)
                last.then_inc(s.tile_ready, inc)
                return last

            def xl_wait(B, L, k):
                base = B.base_norm * KT
                return lambda kt: at(L, B.norms * KT, base + k * KT + kt + 1)

            def sum_squares(B, L, k):
                pe.wait_ge(s.ss_ready, half_no(B, L, k, 1))
                pe.matmul(B4, ones[:], acc[:], start=True, stop=True).then_inc(s.ss_psum, 1)

            def first_units(B, L, n, t, k):
                ready = xl_wait(B, L, k)
                for half in range(2):
                    if half:
                        sum_squares(B, L, k)
                    for u in range(4):
                        if not half:
                            take_slab(B, L, n + u)
                            open_tile(B, L, t + u)
                        out = bank[(B.base_tile + t + u) % TILE_BANKS][:]
                        h, l = wh[(n + u) % SPLIT_SLOTS], wl[(n + u) % SPLIT_SLOTS]
                        for kt in range(4 * half, 4 * half + 4):
                            if u == 0:
                                pe.wait_ge(s.xl_ready, ready(kt))
                            c = kt * P
                            last = three(out, h[:, c:c + P], l[:, c:c + P], xh[:, kt, :], xl[:, kt, :], kt == 0,
                                         kt == KT - 1, new=kt == 4 * half and (u > 0) == (half > 0))
                        if half:
                            last.then_inc(s.tile_ready, 1)

            def turn(out, in_, k=P):
                if k == P:
                    return pe.transpose(out, in_, ident)
                return pe.matmul(out, in_, const[0:k, C_IDENT:C_IDENT + k], start=True, stop=True)

            pe.wait_ge(s.setup_rel, 3 * 16)
            pe.matmul(B7[0:SW_H, 0:TOEP], rel[:], onehot[:], start=True, stop=True).then_inc(s.rel_psum, 1)
            pe.wait_ge(s.setup_const, 16)
            pe.wait_ge(s.consts_ready, 1)
            pe.wait_ge(s.setup_x, 16)
            for j in range(KT):
                if j == 3:
                    pe.wait_ge(s.toep_row, 1)
                if j >= 4:
                    pe.wait_ge(s.setup_copied, j - 3)
                for t in range(NT):
                    last = turn(mb[:, j % 4, t * P:(t + 1) * P], x_tok[:, t, j * P:(j + 1) * P])
                last.then_inc(s.setup_t, 1)
            pe.wait_ge(s.setup_small, 16 * N_SMALL)
            pe.wait_ge(s.setup_copied, 6)
            for l in range(2):
                turn(B4[:, l * R1:(l + 1) * R1], rows1[:, l, :], R1)
                turn(B5[:, l * R2:(l + 1) * R2], rows2[:, l, :], R2)
            turn(B5[:, 2 * R2:2 * R2 + KT], rows3[:], KT).then_inc(s.setup_t, 1)

            def ffn(L, k, n, t, wh_count):
                first_units(Block1, L, n, t, k)
                with pe.Fori(1, FT // 2) as i:
                    for u in range(4):
                        unit(Block1, L, n + u, t + u, xh, xl, i, 4)
                for half in range(2):
                    n0, t0 = n + 2 * FT + half * (FT // 2), t + 2 * FT + 4 * half

                    def down(q, i=None):
                        take_slab(Block1, L, n0 + q, i, 4)
                        h, l = wh[(n0 + q) % SPLIT_SLOTS], wl[(n0 + q) % SPLIT_SLOTS]
                        if half == 0:
                            pe.wait_ge(s.hidden_ready, at(L, 2 * FT, wh_count + 2 * q + 2, i, 8))
                        for kk_ in range(2):
                            kt = 2 * q + kk_ if i is None else i * 8 + (2 * q + kk_)
                            first, end = i is None and q == 0 and kk_ == 0, q == FT // 2 - 1 and kk_ == 1
                            for d in range(4):
                                if first:
                                    open_tile(Block1, L, t0 + d)
                                out = bank[(t0 + d) % TILE_BANKS][:]
                                c = kk_ * S + d * P
                                last = three(out, h[:, c:c + P], l[:, c:c + P], hh[:, kt, :], hl[:, kt, :], first, end,
                                             new=kk_ == 0 and d == 0)
                                if end:
                                    last.then_inc(s.tile_ready, 1)

                    down(0)
                    with pe.Fori(0, 2) as i:
                        for q in range(1, 5):
                            down(q, i)
                    for q in range(9, FT // 2):
                        down(q)

            def mlstm(L):
                pe.wait_ge(s.gate_split, at(L, 1, 2))
                pe.wait_ge(s.inv_var, norm_no(Block1, L, 1))
                for g, out in ((0, B4), (1, B5)):
                    for k in range(KT):
                        last = three(out[0:ML_H, :], gate_h[:, k, 4 * g:4 * g + 4], gate_l[:, k, 4 * g:4 * g + 4],
                                     xh[:, k, :], xl[:, k, :], k == 0, k == KT - 1)
                last.then_inc(s.gates_psum, 1)
                pe.wait_ge(s.tile_evacuated, tiles_out(Block1, L, T_IN + 11))
                for t in range(NT):
                    if t >= 2:
                        pe.wait_ge(s.v_copied, at(L, 5, t - 1))
                    for j in range(4):
                        last = turn(mb[:, 2 + t % 2, j * P:(j + 1) * P], proj[:, 4 + j, t * P:(t + 1) * P])
                    last.then_inc(s.v_turned, 1)
                for u in range(12, 15):
                    more_in(L, u)
                pe.wait_ge(s.ml_rows_done, at(L, 1, 1))
                for t in range(NT):
                    last = turn(B5[:, ML_H * t:ML_H * t + ML_H], ml_rows[5][:, t * P:(t + 1) * P], ML_H)
                last.then_inc(s.c_turned, 1)
                more_in(L, 15)
                pe.wait_ge(s.emt_done, at(L, 1, 1))

                def minus_m(h):
                    if h:
                        pe.wait_ge(s.p_ready, at(L, 16, 4 * h))
                    if h < ML_H:
                        lhs, rhs = const[0:ML_H, C_IDENT + h:C_IDENT + h + 1].to_broadcast([ML_H, P]), acc[0:ML_H, :]
                    else:
                        lhs, rhs = sel4[:], var[0:ML_H, :]
                    pe.matmul(B4, lhs, rhs, start=True, stop=True).then_inc(s.bc_ready, 1)

                minus_m(0)
                for u in range(16, 18):
                    more_in(L, u)
                for h in range(ML_H):
                    tile, half = h // 2, 64 * (h % 2)

                    def scores(j):
                        if j == 1:
                            pe.wait_ge(s.bc_copied, at(L, ML_H, h + 1))
                        elif j:
                            pe.wait_ge(s.p_ready, at(L, 16, 4 * h + j - 1))
                        elif h:
                            pe.wait_ge(s.p_ready, at(L, 16, 4 * h - 1))
                        else:
                            pe.wait_ge(s.c_copied, at(L, 1, 1))
                        pe.matmul(mb[:, 1 - j % 2, 0:S - j * P], proj[half:half + 64, 2 + tile, j * P:(j + 1) * P],
                                  proj[half:half + 64, tile, j * P:S], start=True, stop=True).then_inc(s.sc_ready, 1)

                    def values(j):
                        if j == 0 and h:
                            pe.wait_ge(s.num_sq, at(L, ML_H, h))
                        if j == 0 and not h:
                            pe.wait_ge(s.v_copied, at(L, 5, 4))
                        pe.wait_ge(s.p_ready, at(L, 16, 4 * h + j + 1))
                        o = ML_OFF[j]
                        pj = ml_p[:, o:o + S - j * P]
                        pe.matmul(B6[:, j * P:S], mv_tok[:, j, h * P:(h + 1) * P], pj, start=j == 0, stop=j == 3)
                        pe.matmul(B7[32 * h:32 * h + 32, j * P:S], ones[:, 0:32], pj, start=j == 0, stop=j == 3)\
                          .then_inc(s.pv_done, 1)

                    scores(0)
                    for j in range(1, 4):
                        scores(j)
                        values(j - 1)
                    minus_m(h + 1)
                    values(3)
                    gate_unit(L, 2 * h)
                    if h < ML_H - 1:
                        gate_unit(L, 2 * h + 1)
                pe.wait_ge(s.num_sq, at(L, ML_H, ML_H))
                for h in range(ML_H):
                    last = pe.matmul(B5[32 * h:32 * h + 32, :], ones[:, 0:32], tmp[h][:], start=True, stop=True)
                last.then_inc(s.ml_ss, 1)

            def more_in(L, u):
                unit(Block1, L, S_IN + u, T_IN + u, xh, xl)

            def gate_unit(L, g, half=None):
                n, t = S_GATE + g, T_GATE + g
                if half is None:
                    unit(Block1, L, n, t, xh, xl)
                    return
                if half == 0:
                    take_slab(Block1, L, n)
                    open_tile(Block1, L, t)
                h, l = wh[n % SPLIT_SLOTS], wl[n % SPLIT_SLOTS]
                for kt in range(4 * half, 4 * half + 4):
                    c = kt * P
                    last = three(bank[(Block1.base_tile + t) % TILE_BANKS][:], h[:, c:c + P], l[:, c:c + P], xh[:, kt, :],
                                 xl[:, kt, :], kt == 0, kt == KT - 1, new=kt == 0)
                if half:
                    last.then_inc(s.tile_ready, 1)

            def branch(L, n, t, h, l, ds=(0, 1)):
                for d in ds:
                    unit(Block1, L, n, t + d, h, l, kts=4, c0=d * P, pitch=2 * P, new=d == 0)

            def swa(L):
                pe.wait_ge(s.qk_squared, at(L, 1, 1))
                for u in range(5):
                    out = B6[32 * u:32 * u + 32, :] if u < 4 else B7[0:32, :]
                    if u == 4:
                        pe.wait_ge(s.abs_done, at(L, 1, 1))
                    last = pe.matmul(out, const[:, C_SEL:C_SEL + 32], qk_sq[:, u, :], start=True, stop=True)
                last.then_inc(s.qk_ss, 1)
                gate_unit(L, 7)
                gate_unit(L, 8)
                pe.wait_ge(s.ml_rs, at(L, 1, 1))
                pe.wait_ge(s.qk_inv, at(L, 1, 1))
                for h in range(ML_H):
                    pe.matmul(mb[:, h, :], const[:, C_IDENT + 32 * h:C_IDENT + 32 * h + 1].to_broadcast([P, P]), acc[:],
                              start=True, stop=True).then_inc(s.ml_bc, 1)
                pe.wait_ge(s.qk_rs, at(L, 1, 1))
                for u in range(5):
                    if u < 4:
                        pe.wait_ge(s.ml_bc_read, at(L, ML_H, u + 1))
                    else:
                        pe.wait_ge(s.qk_bc_read, at(L, 5, 1))
                    src = var[32 * u:32 * u + 32, :] if u < 4 else tmp[3][0:32, :]
                    r = 32 * (u % 4)
                    pe.matmul(mb[:, u % 4, :], const[r:r + 32, C_BACK:C_BACK + P], src, start=True, stop=True)\
                      .then_inc(s.qk_bc, 1)
                gate_unit(L, 9)
                pe.wait_ge(s.qk_normed, at(L, 1, 1))
                for g in range(SW_KV):
                    last = pe.matmul(mb[:, 2 + g, :], dup[g], proj[:, 16, :], start=True, stop=True)
                last.then_inc(s.kk_psum, 1)
                for t in range(NT):
                    last = turn(B5[:, t * P:(t + 1) * P], proj[:, 17, t * P:(t + 1) * P])
                last.then_inc(s.v_turned, 1)
                pe.wait_ge(s.kk_copied, at(L, 1, 1))
                pe.wait_ge(s.v_copied, at(L, 5, 5))

                def logits(b):
                    n, g = b // SW_KV, b % SW_KV
                    if b:
                        pe.wait_ge(s.lg_read, at(L, 8, b))
                    lo = 0 if n else P
                    for i in range(SW_G):
                        h = g * SW_G + i
                        half = 64 * (h % 2)
                        out = mb[:, i % 2, (i // 2) * 2 * P + lo:(i // 2) * 2 * P + 2 * P]
                        last = pe.matmul(out, proj[half:half + 64, 12 + h // 2, n * P:(n + 1) * P],
                                         kk[half:half + 64, g, (n - 1) * P + lo:(n + 1) * P], start=True, stop=True)
                    last.then_inc(s.lg_ready, 1)

                logits(0)
                for b in range(8):
                    n, g = b // SW_KV, b % SW_KV
                    if b < 7:
                        logits(b + 1)

                    def between(half):
                        if b < 6:
                            gate_unit(L, 10 + b, half)
                        else:
                            if half == 0:
                                pe.wait_ge(s.ha_ready, at(L, 1, 1))
                            branch(L, S_A + b - 6, T_A + 2 * (b - 6), hah, hal, (half,))

                    between(0)
                    sides = (0, 1) if n else (1,)
                    pe.wait_ge(s.pn_ready, at(L, 8, b + 1))
                    if b:
                        pe.wait_ge(s.o_done, at(L, 8, b))
                    for side in sides:
                        for i in range(SW_G):
                            last = turn(mb[:, 2 + side, i * P:(i + 1) * P], lg[:, b % 2, i, side * P:(side + 1) * P])
                    last.then_inc(s.pt_ready, 1)
                    between(1)
                    pe.wait_ge(s.pt_copied, at(L, 8, b + 1))
                    for par in range(2):
                        for side in sides:
                            rhs = pt_sb[:, side].rearrange("p (i two) q -> p two i q", two=2)[:, par]
                            last = pe.matmul(B6[64 * par:64 * par + 64, 0:2 * P].rearrange("p (i q) -> p i q", i=2),
                                             sv_tok[:, n - 1 + side, g * 64:g * 64 + 64], rhs,
                                             start=side == sides[0], stop=side == 1)
                    last.then_inc(s.o_ready, 1)

            def gated(L):
                for u in range(2, 4):
                    branch(L, S_A + u, T_A + 2 * u, hah, hal)
                for u in range(4):
                    if u == 0:
                        pe.wait_ge(s.o_done, at(L, 8, 8))
                    branch(L, S_B + u, T_B + 2 * u, hbh, hbl)
                for j in range(KT):
                    unit(Block1, L, S_OUT + j, T_OUT + j, mh, ml, part_ready=s.mixed_ready,
                         wait_k=(lambda k: at(L, KT, k + 1)) if j == 0 else None)

            def ple(L):
                first_units(Block1, L, S_PLE, T_PLE, 3)
                for j in range(4, 6):
                    unit(Block1, L, S_PLE + j, T_PLE + j, xh, xl)
                pe.wait_ge(s.p_landed, at(L, 16, 16))
                pe.wait_ge(s.inv_var, norm_no(Block1, L, 3))
                for k in range(2):
                    for t in range(NT):
                        last = turn(mb[:, k, t * P:(t + 1) * P], p_tok[:, t, k * P:(k + 1) * P])
                last.then_inc(s.p_turned, 1)
                for j in range(6, KT):
                    unit(Block1, L, S_PLE + j, T_PLE + j, xh, xl)
                pe.wait_ge(s.pt_split, at(L, 1, 1))
                for j in range(KT):
                    end = j == KT - 1
                    unit(Block1, L, S_PLE + 8 + j // 4, T_PLE + KT + j, pth, ptl, kts=2, c0=(j % 4) * P, pitch=S,
                         new=j % 4 == 0, inc=3 if end else 1)

            with pe.Fori(0, 2) as L:
                ffn(L, 0, S_FFN1, T_FFN1, 0)
                first_units(Block1, L, S_IN, T_IN, 1)
                with pe.Fori(1, 3) as i:
                    for u in range(4):
                        unit(Block1, L, S_IN + u, T_IN + u, xh, xl, i, 4)
                mlstm(L)
                swa(L)
                gated(L)
                ffn(L, 2, S_FFN2, T_FFN2, FT)
                ple(L)

            def more_in2(L, u):
                wide = MLA_D if u == U_DT else P
                unit(Block2, L, S2_IN + u, T2_IN + u, xh, xl, width=wide, pitch=wide)

            def query_unit(L, h):
                unit(Block2, L, S2_QB + h // 2, T2_QB + h, cqh, cql, kts=3, width=MLA_D, c0=(h % 2) * MLA_D,
                     pitch=2 * MLA_D, new=h % 2 == 0)

            def gmlp(L):
                for u in range(4, 6):
                    more_in2(L, u)
                pe.wait_ge(s.gv_squared, at(L, 1, 1))
                pe.wait_ge(s.inv_var, norm_no(Block2, L, 0))
                for k in range(2):
                    last = pe.matmul(B4, ones[:], gv_sq[:, k, :], start=k == 0, stop=k == 1)
                last.then_inc(s.gv_ss, 1)
                pe.wait_ge(s.ws_landed, at(L, 16, 16))
                for h in range(4):
                    last = turn(B7[:, h * P:(h + 1) * P], ws_raw[:, h, :])
                last.then_inc(s.ws_turned, 1)
                for u in range(6, 8):
                    more_in2(L, u)
                pe.wait_ge(s.gv_normed, at(L, 1, 1))
                for t in range(NT):
                    for k in range(2):
                        o = (t % 2) * 2 * P + k * P
                        last = turn(mb[:, 1 + t // 2, o:o + P], proj2[:, 2 + k, t * P:(t + 1) * P])
                last.then_inc(s.gv_turned, 1)
                for u in range(8, 10):
                    more_in2(L, u)
                pe.wait_ge(s.gv_copied, at(L, 1, 1))
                pe.wait_ge(s.ws_copied, at(L, 1, 1))
                for k in range(2):
                    for c in range(NT):
                        for par in range(2):
                            h = 2 * k + par
                            out = mb[64 * par:64 * par + 64, k, c * P:(c + 1) * P]
                            pe.matmul(out, gv_tok[:, c, h * 64:h * 64 + 64], ws_t[:, h, :], start=True, stop=False)
                            last = pe.matmul(out, const[0:4, C_IDENT + h:C_IDENT + h + 1].to_broadcast([4, 64]),
                                             bs_now[:], start=False, stop=True)
                last.then_inc(s.gm_psum, 1)

            def ssd(L):
                more_in2(L, U_Z)
                pe.wait_ge(s.conv_silu, at(L, 1, 1))
                pe.wait_ge(s.gm_done, at(L, 1, 1))
                for t in range(NT):
                    for k in range(3):
                        last = turn(mb[:, t, k * P:(k + 1) * P], conv[:, k, t * P:(t + 1) * P])
                last.then_inc(s.xs_turned, 1)
                more_in2(L, U_Z + 1)
                pe.wait_ge(s.dt_rows_done, at(L, 1, 1))
                pe.wait_ge(s.xs_copied, at(L, 1, 1))
                for t in range(NT):
                    turn(B5[:, t * SSD_H:(t + 1) * SSD_H], acc[0:SSD_H, t * P:(t + 1) * P], SSD_H)
                    last = turn(B5[:, 64 + t * SSD_H:64 + (t + 1) * SSD_H], var[0:SSD_H, t * P:(t + 1) * P], SSD_H)
                last.then_inc(s.dcol_turned, 1)

                def products(g):
                    for j in range(NT):
                        c = 4 * g + j
                        if c >= 2:
                            pe.wait_ge(s.cb_copied, at(L, 8, c - 1))
                        elif c == 0:
                            pe.wait_ge(s.dcol_copied, at(L, 1, 1))
                        if c == 5:
                            pe.wait_ge(s.y_done, at(L, 3, 1))
                        pe.matmul(mb[:, 1 + j % 2, 0:S - j * P], conv[64 * g:64 * g + 64, 3, j * P:(j + 1) * P],
                                  conv[64 * g:64 * g + 64, 4, j * P:S], start=True, stop=True).then_inc(s.cb_ready, 1)

                def decays(h):
                    if h:
                        pe.wait_ge(s.abc_copied, at(L, SSD_H, h))
                    pe.matmul(B4, const[0:SSD_H, C_IDENT + h:C_IDENT + h + 1].to_broadcast([SSD_H, P]), acc[0:SSD_H, :],
                              start=True, stop=True).then_inc(s.abc_ready, 1)

                decays(0)
                more_in2(L, U_Z + 2)
                more_in2(L, U_C)
                for h in range(SSD_H):
                    tile, half = h // 2, 64 * (h % 2)
                    if h % 3 == 0:
                        products(h // 3)
                    if h < SSD_H - 1:
                        decays(h + 1)
                    if h < 4:
                        more_in2(L, U_C + 1 + h)
                    else:
                        if h == 4:
                            pe.wait_ge(s.c_squared, at(L, 1, 1))
                            pe.wait_ge(s.cb_copied, at(L, 8, 8))
                            for k in range(3):
                                pe.matmul(B5[0:64, :], ones[:, 0:64], c_sq[:, k, :], start=k == 0, stop=k == 2)
                            for k in range(2):
                                last = pe.matmul(B5[64:P, :], ones[:, 0:64], c_sq[:, 3 + k, :], start=k == 0, stop=k == 1)
                            last.then_inc(s.c_ss, 1)
                            pe.wait_ge(s.c_split, at(L, 1, 1))
                        for q in (2 * (h - 4), 2 * (h - 4) + 1):
                            query_unit(L, q)
                    if h == SSD_H - 1:
                        pe.wait_ge(s.c_rs, at(L, 1, 1))
                        pe.wait_ge(s.abc_copied, at(L, SSD_H, SSD_H))
                        for g in range(2):
                            last = pe.matmul(mb[:, g, :], const[:, C_IDENT + 64 * g:C_IDENT + 64 * g + 1].to_broadcast([P, P]),
                                             tmp[2][:], start=True, stop=True)
                        last.then_inc(s.c_bc, 1)
                    out = mb[half:half + 64, 2 + tile % 2, :]
                    for j in range(NT):
                        pe.wait_ge(s.sp_ready, at(L, 24, 4 * h + j + 1))
                        if j == 0 and h == 4:
                            pe.wait_ge(s.y_done, at(L, 3, 1))
                        o = ML_OFF[j]
                        last = pe.matmul(out[:, j * P:S], xs_tok[:, j, h * 64:h * 64 + 64], sd_p[:, o:o + S - j * P],
                                         start=j == 0, stop=j == 3)
                    last.then_inc(s.y_psum, 1)

            def mla(L):
                B = Block2
                for h in range(4, MLA_H):
                    query_unit(L, h)
                pe.wait_ge(s.rope_landed, 16)
                pe.wait_ge(s.c_scaled, at(L, 1, 1))
                pe.matmul(B5[0:MLA_D, :], rot96, proj2[0:MLA_D, 12, :], start=True, stop=True).then_inc(s.rot_psum, 1)
                pe.wait_ge(s.y_squared, at(L, 1, 1))
                for half, k in ((0, 0), (64, 2)):
                    out = B7[half:half + 64, :]
                    pe.matmul(out, ones[:, 0:64], y_sq[:, k, :], start=True, stop=False)
                    last = pe.matmul(out, ones[half:half + 64, 0:64], y_sq[half:half + 64, 1, :], start=False, stop=True)
                last.then_inc(s.y_ss, 1)

                def key_value_unit(h):
                    unit(B, L, S2_KVB + h // 2, T2_KVB + h, ckh, ckl, kts=2, c0=(h % 2) * P, pitch=2 * P, new=h % 2 == 0)

                for h in range(3):
                    key_value_unit(h)
                pe.wait_ge(s.y_rs, at(L, 1, 1))
                for g in range(2):
                    last = pe.matmul(mb[:, 2 + g, :], const[:, C_IDENT + 64 * g:C_IDENT + 64 * g + 1].to_broadcast([P, P]),
                                     tmp[0][:], start=True, stop=True)
                last.then_inc(s.y_bc, 1)
                for h in range(MLA_H):
                    if h + 3 < MLA_H:
                        key_value_unit(h + 3)
                    if h == 0:
                        pe.wait_ge(s.y_bc_read, at(L, 1, 1))
                    pe.wait_ge(s.tile_evacuated, tiles_out(B, L, T2_QB + h))
                    pe.wait_ge(s.rot_read, at(L, 1 + MLA_H, max(1, h)))
                    pe.matmul(mb[0:MLA_D, 2 + (h + 1) % 2, :], rot96, q96[:, h, :], start=True, stop=True)\
                      .then_inc(s.rot_psum, 1)
                    pe.wait_ge(s.kv_done, at(L, MLA_H, h + 1))
                    if h >= 2:
                        pe.wait_ge(s.vt_copied, at(L, MLA_H, h - 1))
                    for t in range(NT):
                        last = pe.matmul(mb[:, h % 2, t * 64:(t + 1) * 64], v_ft[64:P, h % 2, t * P:(t + 1) * P],
                                         const[64:P, C_IDENT + 64:C_IDENT + P], start=True, stop=True)
                    last.then_inc(s.vt_psum, 1)
                pe.wait_ge(s.rot_done, at(L, 1 + MLA_H, 1 + MLA_H))
                pe.wait_ge(s.vt_copied, at(L, MLA_H, MLA_H))
                pe.wait_ge(s.key_rows, at(L, 1, 1))

                def logits(c):
                    h, n = c // NT, c % NT
                    if c >= TILE_BANKS:
                        pe.wait_ge(s.ae_ready, at(L, 24, c - TILE_BANKS + 1))
                    out = bank[c % TILE_BANKS]
                    pe.matmul(out[:, 0:(n + 1) * P], q96[:, h, n * P:(n + 1) * P], k96[:, h, 0:(n + 1) * P],
                              start=True, stop=False)
                    pe.matmul(out[:, n * P:(n + 1) * P], ident, mask_qs, start=False, stop=True).then_inc(s.al_ready, 1)

                def turned(c):
                    n = c % NT
                    pe.wait_ge(s.ap_ready, at(L, 24, c + 1))
                    if c >= 2:
                        pe.wait_ge(s.at_copied, at(L, 24, c - 1))
                    for j in range(n + 1):
                        last = turn(mb[:, c % 2, j * P:(j + 1) * P], prob[:, c % 4, j * P:(j + 1) * P])
                    last.then_inc(s.at_ready, 1)

                def head_out(h):
                    half = 64 * (h % 2)
                    pe.wait_ge(s.at_copied, at(L, 24, 4 * h + 4))
                    if h >= 2:
                        pe.wait_ge(s.ao_done, at(L, MLA_H, h - 1))
                    for j in range(NT):
                        last = pe.matmul(mb[half:half + 64, 2 + h % 2, j * P:S], v_tok[:, j, h * 64:h * 64 + 64],
                                         prob_t[h % 2][:, j, j * P:S], start=j == 0, stop=j == 3)
                    last.then_inc(s.ao_ready, 1)

                for c in range(3):
                    logits(c)
                for c in range(NT * MLA_H):
                    if c + 3 < NT * MLA_H:
                        logits(c + 3)
                    turned(c)
                    if c >= NT and c % NT == 0:
                        head_out(c // NT - 1)
                head_out(MLA_H - 1)

            with pe.Fori(0, 2) as L:
                B = Block2
                first_units(B, L, S2_IN, T2_IN, 0)
                gmlp(L)
                ssd(L)
                mla(L)
                pe.wait_ge(s.ao_done, at(L, MLA_H, MLA_H))
                for j in range(KT):
                    unit(B, L, S2_OUT + j, T2_OUT + j, xh, xl)
                for half in range(2):
                    n0, t0 = S2_MLP + half * 2 * HALF2, T2_MLP + half * (HALF2 + 8)
                    if half == 0:
                        first_units(B, L, n0, t0, 1)
                    with pe.Fori(1 - half, HALF2 // 4) as i:
                        for u in range(4):
                            unit(B, L, n0 + u, t0 + u, xh, xl, i, 4)
                    for dh in range(2):
                        n1, t1 = n0 + HALF2 + 8 * dh, t0 + HALF2 + 4 * dh

                        def down(q, i=None):
                            take_slab(B, L, n1 + q, i, 4)
                            h, l = wh[(n1 + q) % SPLIT_SLOTS], wl[(n1 + q) % SPLIT_SLOTS]
                            if dh == 0:
                                pe.wait_ge(s.hidden_ready,
                                           at(L, FT2, 4 * FT + half * HALF2 + 2 * q + 2, i, 8))
                            for kk_ in range(2):
                                kt = 2 * q + kk_ if i is None else i * 8 + (2 * q + kk_)
                                first, end = i is None and q == 0 and kk_ == 0, q == 7 and kk_ == 1
                                for d in range(4):
                                    if first:
                                        open_tile(B, L, t1 + d)
                                    out = bank[(B.base_tile + t1 + d) % TILE_BANKS][:]
                                    c = kk_ * S + d * P
                                    last = three(out, h[:, c:c + P], l[:, c:c + P], hh[:, kt, :], hl[:, kt, :],
                                                 first, end, new=kk_ == 0 and d == 0)
                                    if end:
                                        last.then_inc(s.tile_ready, 3 if half and dh and d == 3 else 1)

                        for q in range(8):
                            down(q)

            sum_squares(Last, None, 0)
            pe.wait_ge(s.fin_y, 1)
            for c in range(2 * NT):
                t, side = c // 2, c % 2
                if c >= 4:
                    pe.wait_ge(s.fin_copied, c - 3)
                for j in range(4):
                    last = turn(mb[:, c % 4, j * P:(j + 1) * P], y_sb[:, 4 * side + j, t * P:(t + 1) * P])
                last.then_inc(s.fin_turned, 1)

        @block.scalar
        def _(act):
            def round_hi(B, L, n, i=None, step=0):
                if n >= B.slabs:
                    return
                act.wait_ge(raw_landed[n % RAW_SLOTS],
                            at(L, 8 * B.slabs, 8 * (B.base_slab + n - n % 2) + 16, i, 8 * step))
                act.wait_ge(s.slab_used, at(L, B.slabs, B.base_slab + n + 1, i, step))
                if B is Block2 and n == S2_IN + U_DT:
                    act.wait_ge(s.kr_landed, at(L, 16, 16))
                act.activation(wh[n % SPLIT_SLOTS][:], raw[n % RAW_SLOTS][:], ACT.Copy).then_inc(s.hi_ready, 1)

            def ahead(B, L, n, count, i=None, step=0):
                for k in range(count):
                    round_hi(B, L, n + k + AHEAD, i, step)

            def square_half(B, L, k, half):
                act.wait_ge(s.x_final, half_no(B, L, k, half))
                if half:
                    act.wait_ge(s.ss_ready, half_no(B, L, k, 0))
                act.activation(tmp_all[:], x_sb[:, 4 * half:4 * half + 4, :], ACT.Square).then_inc(s.sq_ready, 1)

            def norm(B, L, k, n):
                square_half(B, L, k, 1)
                if n is not None:
                    ahead(B, L, n, 1)
                act.wait_ge(s.inv_var, norm_no(B, L, k))
                act.activation(rstd[:], var[:], ACT.Sqrt).then_inc(s.rstd_ready, 1)
                if n is not None:
                    ahead(B, L, n + 1, 3)

            def ffn(L, k, n, t, silu0):
                norm(Block1, L, k, n)

                def pair(f, i=None):
                    act.wait_ge(s.tile_evacuated, tiles_out(Block1, L, t + 2 * f, i, 4))
                    act.activation(tmp[f % 2][:], tmp[f % 2][:], ACT.Silu).then_inc(s.silu_done, 1)

                pair(0)
                pair(1)
                with act.Fori(1, FT // 2) as i:
                    for f in range(2):
                        round_hi(Block1, L, n + 2 * f + AHEAD, i, 4)
                        pair(f, i)
                        round_hi(Block1, L, n + 2 * f + 1 + AHEAD, i, 4)
                n0 = n + 2 * FT
                with act.Fori(0, 3) as i:
                    ahead(Block1, L, n0, 4, i, 4)
                square_half(Block1, L, k + 1, 0)
                with act.Fori(3, 5) as i:
                    ahead(Block1, L, n0, 4, i, 4)
                ahead(Block1, L, n0 + 20, 2)

            def mlstm(L):
                act.wait_ge(s.tile_evacuated, tiles_out(Block1, L, T_IN + 11))
                act.activation(proj[:, 8:12, :], proj[:, 8:12, :], ACT.Sigmoid).then_inc(s.mo_done, 1)
                fp, ig, e1, e2 = ml_rows[0:4]
                act.wait_ge(s.gate_pre, at(L, 1, 1))
                act.activation(e1[:], fp[:], ACT.Abs)
                act.drain()
                act.activation(e2[:], e1[:], ACT.Exp, scale=-1.0)
                act.drain()
                act.activation(e1[:], e2[:], ACT.Ln, bias=1.0).then_inc(s.log1p, 1)
                ahead(Block1, L, S_IN + 12, 3)
                act.wait_ge(s.ml_rows_done, at(L, 1, 1))
                act.activation(var[0:ML_H, :], ml_rows[7][:], ACT.Exp, scale=-1.0).then_inc(s.emt_done, 1)
                ahead(Block1, L, S_IN + 15, 1)

                def weights(h):
                    act.wait_ge(s.bc_copied, at(L, ML_H, h + 1))
                    if h == 0:
                        act.wait_ge(s.c_copied, at(L, 1, 1))
                    for j in range(NT):
                        if h:
                            act.wait_ge(s.p_ready, at(L, 16, 4 * h - 3 + j))
                        o = ML_OFF[j]
                        last = act.activation(ml_w[:, o:o + P], neg_md[:, j * P:(j + 1) * P], ACT.Exp,
                                              bias=c_col[:, j, h:h + 1])
                        if j < NT - 1:
                            last = act.activation(ml_w[:, o + P:o + S - j * P], neg_m[:, (j + 1) * P:S], ACT.Exp,
                                                  bias=c_col[:, j, h:h + 1])
                        last.then_inc(s.w_ready, 1)

                weights(0)
                ahead(Block1, L, S_IN + 16, 2)
                for h in range(ML_H):
                    if h < ML_H - 1:
                        weights(h + 1)
                    act.wait_ge(s.head_done, at(L, ML_H, h + 1))
                    act.activation(tmp[h][:], B6, ACT.Square).then_inc(s.num_sq, 1)
                    if h < ML_H - 1:
                        ahead(Block1, L, S_GATE + 2 * h, 2)
                act.activation(acc[:], B7, ACT.Abs).then_inc(s.abs_done, 1)

            def swa(L):
                act.wait_ge(s.tile_evacuated, tiles_out(Block1, L, T_IN + 17))
                act.activation(qk_sq[:], proj[:, 12:17, :], ACT.Square).then_inc(s.qk_squared, 1)
                ahead(Block1, L, S_GATE + 6, 2)
                act.wait_ge(s.ml_inv, at(L, 1, 1))
                act.activation(acc[:], acc[:], ACT.Sqrt).then_inc(s.ml_rs, 1)
                act.wait_ge(s.qk_inv, at(L, 1, 1))
                act.activation(var[:], var[:], ACT.Sqrt)
                act.activation(tmp[3][0:32, :], tmp[3][0:32, :], ACT.Sqrt).then_inc(s.qk_rs, 1)
                act.wait_ge(s.ml_bc_read, at(L, ML_H, ML_H))
                act.activation(hah[:], num_sb[:], ACT.Copy).then_inc(s.ha_rounded, 1)
                gates(L, 0)
                ahead(Block1, L, S_GATE + 8, 2)
                for b in range(8):
                    n = b // SW_KV
                    lo = 0 if n else P
                    act.wait_ge(s.mx_ready, at(L, 8, b + 1))
                    for i in range(SW_G):
                        act.activation(lg[:, b % 2, i, lo:2 * P], lg[:, b % 2, i, lo:2 * P], ACT.Exp,
                                       bias=small[:, 4 + i:5 + i], accum_out=small[:, 12 + i:13 + i])
                    act.activation(small[:, 16:20], small[:, 8:12], ACT.Exp).then_inc(s.ex_ready, 1)
                    ahead(Block1, L, S_GATE + 10 + b, 1)

            def gates(L, branch):
                act.wait_ge(s.tile_evacuated, tiles_out(Block1, L, T_GATE + 8 * branch + 7))
                for j in range(KT):
                    g = gate[8 * branch + j]
                    act.activation(g[:], g[:], ACT.Sigmoid).then_inc(s.sig_done, 1)

            def gated(L):
                ahead(Block1, L, S_A + 2, 2)
                gates(L, 1)
                ahead(Block1, L, S_B, 4)
                ahead(Block1, L, S_OUT, 5)
                square_half(Block1, L, 2, 0)
                ahead(Block1, L, S_OUT + 5, 3)

            def ple(L):
                norm(Block1, L, 3, S_PLE)
                for j in range(KT):
                    act.wait_ge(s.tile_evacuated, tiles_out(Block1, L, T_PLE + j))
                    act.activation(gate_sg[:, j, :], gate_sg[:, j, :], ACT.Sigmoid).then_inc(s.sg_done, 1)
                    if j >= 4:
                        round_hi(Block1, L, S_PLE + j + AHEAD)
                square_half(Block1, L, Block1.norms, 0)

            for dst, name in ((rel, "rel_bias"), (onehot, "onehot"), (pad, "pad")):
                act.dma_start(dst[:], a[name]).then_inc(s.setup_rel, 16)
            act.wait_ge(s.toep_row, 1)
            act.dma_start(scratch, toep[:, None, :].to_broadcast([SW_H, P, TOEP]))\
               .then_inc(s.toep_out, 16)
            for dst, r0, n, name in ((rows1, R_FFN1, 8, "ffn1_norm"), (rows1, R_MIX, 8, "mix_norm"),
                                     (rows1, R_FFN2, 8, "ffn2_norm"), (rows1, R_PLE, 8, "ple_norm"),
                                     (rows2, Q_MIX, 8, "norm_mix_g_2"), (rows2, Q_MLP, 8, "norm_mlp_g_2"),
                                     (rows2, Q_CQ, 3, "mla_q_norm_g_2"), (rows2, Q_CKV, 2, "mla_kv_norm_g_2"),
                                     (rows2, Q_SSD, 3, "ssd_norm_g_2"), (rows2, Q_GV, 2, "gmlp_v_norm_g_2"),
                                     (rows2, Q_CB, 5, "ssd_conv_b_2")):
                act.dma_start(dst[r0:r0 + n, :, :], a[name].rearrange("l (r c) -> r l c", c=P)).then_inc(s.setup_small, 16)
            act.dma_start(rows1[R_MLOUT:R_MLOUT + ML_H, :, :], a["ml_out_norm"].rearrange("l h c -> h l c"))\
               .then_inc(s.setup_small, 16)
            for r0, name in ((R_QN, "q_norm"), (R_KN, "k_norm")):
                for half in range(2):
                    act.dma_start(rows1[r0:r0 + 1, :, half * 64:half * 64 + 64], a[name].rearrange("(o l) c -> o l c", o=1))\
                       .then_inc(s.setup_small, 16)
            act.dma_start(rows2[Q_CW:Q_CW + 20, :, :], a["ssd_conv_w_2"].rearrange("l k (r c) -> (k r) l c", c=P))\
               .then_inc(s.setup_small, 16)
            act.dma_start(rows3[:], a["final_norm_g_2"].rearrange("(r c) -> r c", c=P)).then_inc(s.setup_small, 16)
            with nc.allow_non_contiguous_dma("parameters of a few bytes"):
                for dst, name in ((b_gate[:, :, 0:1], "b_igate"), (b_gate[:, :, 1:2], "b_fgate"),
                                  (dt_bias[:, :, None], "ssd_dt_bias_2"), (dt_a[:, :, None], "ssd_a_log_2")):
                    act.dma_start(dst, a[name].rearrange("l (h o) -> h l o", o=1)).then_inc(s.setup_small, 16)
                act.dma_start(bs_rows[:], a["gmlp_b_s_2"].rearrange("l h t -> h l t")).then_inc(s.setup_small, 16)
                act.dma_start(sinks[:].rearrange("p l h -> p (l h)"),
                              a["sinks"].rearrange("(o l) h -> o (l h)", o=1).to_broadcast([P, 2 * SW_H]))\
                   .then_inc(s.setup_small, 16)
                for half in range(2):
                    src = a["ssd_d_2"].rearrange("l (i two) -> two l i", two=2)[half:half + 1]
                    act.dma_start(d_skip[half * 64:half * 64 + 64], src.to_broadcast([64, 2, 3])).then_inc(s.setup_small, 16)
            act.dma_start(sel4[:], a["sel4"]).then_inc(s.setup_small, 16)
            act.wait_ge(s.toep_out, 16)
            act.dma_start(bias[:], bass.AP(scratch.tensor, P - 1, [[TOEP - 1, P], [P * TOEP, SW_H], [1, 2 * P]]))\
               .then_inc(s.toep_in, 16)
            square_half(Block1, None, 0, 0)
            with act.Fori(0, 2) as L:
                for n in range(AHEAD):
                    round_hi(Block1, L, n)
                ffn(L, 0, S_FFN1, T_FFN1, 0)
                norm(Block1, L, 1, S_IN)
                ahead(Block1, L, S_IN + 4, 8)
                mlstm(L)
                swa(L)
                gated(L)
                ffn(L, 2, S_FFN2, T_FFN2, FT)
                ple(L)

            def gmlp(L):
                for u in range(4):
                    act.wait_ge(s.tile_evacuated, tiles_out(Block2, L, T2_IN + u))
                    last = act.activation(proj2[:, u, :], proj2[:, u, :], ACT.Gelu_apprx_tanh)
                last.then_inc(s.gelu_done, 1)
                act.drain()
                act.activation(gv_sq[:], proj2[:, 2:4, :], ACT.Square).then_inc(s.gv_squared, 1)
                ahead(Block2, L, S2_IN + 4, 2)
                act.wait_ge(s.gv_inv, at(L, 1, 1))
                act.activation(tmp[1][:], tmp[0][:], ACT.Sqrt).then_inc(s.gv_rs, 1)
                ahead(Block2, L, S2_IN + 6, 4)

            def ssd(L):
                act.wait_ge(s.conv_done, at(L, 1, 1))
                act.activation(conv[:], conv[:], ACT.Silu).then_inc(s.conv_silu, 1)
                ahead(Block2, L, S2_IN + U_Z, 1)
                act.wait_ge(s.dt_pre, at(L, 1, 1))
                act.activation(tmp[3][0:SSD_H, :], tmp[2][0:SSD_H, :], ACT.Abs)
                act.drain()
                act.activation(tmp[1][0:SSD_H, :], tmp[3][0:SSD_H, :], ACT.Exp, scale=-1.0)
                act.activation(small[0:SSD_H, 1:2], dt_now[:, 1:2], ACT.Exp)
                act.drain()
                act.activation(tmp[3][0:SSD_H, :], tmp[1][0:SSD_H, :], ACT.Ln, bias=1.0).then_inc(s.dt_log, 1)
                ahead(Block2, L, S2_IN + U_Z + 1, 1)

                def weights(h):
                    act.wait_ge(s.abc_copied, at(L, SSD_H, h + 1))
                    for j in range(NT):
                        if h:
                            act.wait_ge(s.sp_ready, at(L, 24, 4 * h - 3 + j))
                        o = ML_OFF[j]
                        last = act.activation(sd_w[:, o:o + P], tmp[1][:, j * P:(j + 1) * P], ACT.Exp,
                                              bias=a_col[:, j, h:h + 1])
                        if j < NT - 1:
                            last = act.activation(sd_w[:, o + P:o + S - j * P], tmp[0][:, (j + 1) * P:S], ACT.Exp,
                                                  bias=a_col[:, j, h:h + 1])
                        last.then_inc(s.sw_ready, 1)

                weights(0)
                ahead(Block2, L, S2_IN + U_Z + 2, 2)
                act.wait_ge(s.tile_evacuated, tiles_out(Block2, L, T2_IN + U_Z + 2))
                act.activation(proj2[:, 4:7, :], proj2[:, 4:7, :], ACT.Silu).then_inc(s.z_silu, 1)
                for h in range(SSD_H):
                    if h < SSD_H - 1:
                        weights(h + 1)
                    if h == 3:
                        act.wait_ge(s.tile_evacuated, tiles_out(Block2, L, T2_IN + U_C + 4))
                        act.activation(c_sq[:], proj2[:, 13:18, :], ACT.Square).then_inc(s.c_squared, 1)
                    ahead(Block2, L, S2_IN + U_C + 1 + h, 1)
                    if h == 4:
                        act.wait_ge(s.c_inv, at(L, 1, 1))
                        act.activation(tmp[2][:], tmp[2][:], ACT.Sqrt).then_inc(s.c_rs, 1)
                act.wait_ge(s.c_bc, at(L, 1, 1))
                act.activation(acc[:], B4, ACT.Copy)
                act.activation(var[:], B5, ACT.Copy).then_inc(s.c_scaled, 1)

            def mla(L):
                act.wait_ge(s.y_done, at(L, 3, 3))
                act.activation(y_sq[:], conv[:, 0:3, :], ACT.Square).then_inc(s.y_squared, 1)
                ahead(Block2, L, S2_QB + 2, 1)
                act.wait_ge(s.rot_done, at(L, 1 + MLA_H, 1))
                act.activation(k96[64:MLA_D, :, :], k_rot[64:MLA_D, None, :].to_broadcast([32, MLA_H, S]), ACT.Copy)\
                   .then_inc(s.key_rows, 1)
                act.wait_ge(s.y_inv, at(L, 1, 1))
                act.activation(tmp[0][:], tmp[0][:], ACT.Sqrt).then_inc(s.y_rs, 1)
                act.wait_ge(s.y_scaled, at(L, 1, 1))
                act.activation(xh[:, 2:5, :], tmp_all[:, 1:4, :], ACT.Copy).then_inc(s.y_rounded, 1)
                ahead(Block2, L, S2_KVB, 2)
                for h in range(MLA_H):
                    act.wait_ge(s.vt_psum, at(L, MLA_H, h + 1))
                    act.activation(v_tok[:, :, h * 64:h * 64 + 64], mb[:, h % 2, 0:NT * 64].rearrange("p (t c) -> p t c", t=NT),
                                   ACT.Copy).then_inc(s.vt_copied, 1)
                    if h == 0:
                        ahead(Block2, L, S2_KVB + 2, 1)

                def copied(c):
                    h, n = c // NT, c % NT
                    act.wait_ge(s.at_ready, at(L, 24, c + 1))
                    if n == 0 and h >= 2:
                        act.wait_ge(s.ao_ready, at(L, MLA_H, h - 1))
                    act.activation(prob_t[h % 2][:, 0:n + 1, n * P:(n + 1) * P],
                                   mb[:, c % 2, 0:(n + 1) * P].rearrange("p (j q) -> p j q", j=n + 1), ACT.Copy)\
                       .then_inc(s.at_copied, 1)

                for c in range(NT * MLA_H):
                    n = c % NT
                    act.wait_ge(s.am_ready, at(L, 24, c + 1))
                    if c >= 4:
                        act.wait_ge(s.at_ready, at(L, 24, c - 3))
                    w = (n + 1) * P
                    act.activation(prob[:, c % 4, 0:w], bank[c % TILE_BANKS][:, 0:w], ACT.Exp,
                                   bias=small[:, 32 + n:33 + n], scale=MLA_SCALE,
                                   accum_out=small[:, 36 + n:37 + n]).then_inc(s.ae_ready, 1)
                    if c:
                        copied(c - 1)
                copied(NT * MLA_H - 1)

            with act.Fori(0, 2) as L:
                B = Block2
                for n in range(AHEAD):
                    round_hi(B, L, n)
                norm(B, L, 0, S2_IN)
                gmlp(L)
                ssd(L)
                mla(L)
                ahead(B, L, S2_OUT, 8)
                square_half(B, L, 1, 0)
                norm(B, L, 1, S2_MLP)
                with act.Fori(1, 2 * FT2 // 4 - 2) as i:
                    ahead(B, L, S2_MLP, 4, i, 4)
                ahead(B, L, B2_SLABS - 8, 2)
                square_half(B, L, B.norms, 0)
                ahead(B, L, B2_SLABS - 6, 6)
            norm(Last, None, 0, None)

        @block.vector
        def _(dve):
            def split(hi, lo, src):
                dve.tensor_copy(hi, src)
                dve.drain()
                return dve.tensor_tensor(lo, src, hi.bitcast(F32), ALU.subtract)

            def invert(out, sums, scale):
                dve.tensor_scalar(out, sums, scale, EPS, ALU.mult, ALU.add)
                dve.drain()
                return dve.reciprocal(out, out)

            def read_tile(B, L, t, out, scale, i=None, step=0, rows=(0, P), inc=1):
                dve.wait_ge(s.tile_ready, tiles_in(B, L, t, i, step))
                r0, r1 = rows
                return dve.tensor_tensor(out, bank[(B.base_tile + t) % TILE_BANKS][r0:r1, :], scale[r0:r1, :], ALU.mult)\
                          .then_inc(s.tile_evacuated, inc)

            def x_times_gain(j, g):
                dve.tensor_scalar(xh[:, j, :], x_sb[:, j, :], g[:, j:j + 1], None, ALU.mult)
                dve.drain()
                dve.scalar_tensor_tensor(out=xl[:, j, :], in0=x_sb[:, j, :], scalar=g[:, j:j + 1],
                                         in1=xh[:, j, :].bitcast(F32), op0=ALU.mult, op1=ALU.subtract)\
                   .then_inc(s.xl_ready, 1)

            def sum_half(B, L, k, half):
                dve.wait_ge(s.sq_ready, half_no(B, L, k, half))
                last = dve.tensor_reduce((acc, var)[half][:], tmp_all[:].rearrange("p j t -> p t j"), AX.X, ALU.add)
                if half:
                    dve.drain()
                    last = dve.tensor_tensor(acc[:], acc[:], var[:], ALU.add)
                last.then_inc(s.ss_ready, 1)

            def first_half(B, L, k, g):
                dve.drain().then_inc(s.x_final, 1)
                if g is not None:
                    for j in range(4):
                        x_times_gain(j, g)
                sum_half(B, L, k, 0)

            def norm(B, L, k, g):
                dve.drain().then_inc(s.x_final, 1)
                if g is not None:
                    for j in range(4, 6):
                        x_times_gain(j, g)
                sum_half(B, L, k, 1)
                if g is not None:
                    for j in range(6, KT):
                        x_times_gain(j, g)
                dve.wait_ge(s.ss_psum, norm_no(B, L, k))
                invert(var[:], B4, 1.0 / D).then_inc(s.inv_var, 1)

            def scaled_tile(B, L, k, t, out, i=None, step=0, rows=(0, P), inc=1):
                dve.wait_ge(s.rstd_ready, norm_no(B, L, k))
                return read_tile(B, L, t, out, rstd, i, step, rows, inc)

            def add_x(B, L, t, j, scale=1.0, inc=1):
                dve.wait_ge(s.tile_ready, tiles_in(B, L, t))
                dve.scalar_tensor_tensor(out=x_sb[:, j, :], in0=bank[(B.base_tile + t) % TILE_BANKS][:], scalar=scale,
                                         in1=x_sb[:, j, :], op0=ALU.mult, op1=ALU.add).then_inc(s.tile_evacuated, inc)

            dve.wait_ge(s.rel_psum, 1)
            dve.tensor_tensor(toep[:], B7[0:SW_H, 0:TOEP], pad[:], ALU.add).then_inc(s.toep_row, 1)
            for j in range(KT):
                dve.wait_ge(s.setup_t, j + 1)
                dve.tensor_copy(x_sb[:, j, :], mb[:, j % 4, :]).then_inc(s.setup_copied, 1)
            dve.wait_ge(s.setup_t, KT + 1)
            dve.tensor_copy(p1[:], B4[:, 0:2 * R1])
            dve.tensor_copy(p2[:], B5[:, 0:2 * R2 + KT])
            dve.drain()
            for n, (table, c) in enumerate(((p1, R_FFN1), (p1, R1 + R_FFN1), (p2, Q_MIX), (p2, R2 + Q_MIX), (p2, 2 * R2))):
                dve.tensor_copy(first_gains[:, n * KT:(n + 1) * KT], table[:, c:c + KT])
            dve.tensor_copy(g_first, p1[:, R_FFN1:R_FFN1 + KT])
            dve.drain()
            first_half(Block1, None, 0, g_first)

            def ffn(L, k, g, g_next, t, silu0):
                norm(Block1, L, k, g)
                dve.wait_ge(s.toep_out, 16)
                dve.drain()

                def pair(f, i=None):
                    gs, us = tmp[f % 2], tmp[2 + f % 2]
                    scaled_tile(Block1, L, k, t + 2 * f, gs[:], i, 4)
                    scaled_tile(Block1, L, k, t + 2 * f + 1, us[:], i, 4)
                    dve.drain()
                    dve.wait_ge(s.silu_done, at(L, 2 * FT, silu0 + f + 1, i, 2))
                    dve.tensor_tensor(us[:], us[:], gs[:], ALU.mult)
                    dve.drain()
                    j = f if i is None else i * 2 + f
                    split(hh[:, j, :], hl[:, j, :], us[:]).then_inc(s.hidden_ready, 1)

                with dve.Fori(0, FT // 2) as i:
                    for f in range(2):
                        pair(f, i)
                for j in range(KT):
                    add_x(Block1, L, t + 2 * FT + j, j, 0.5)
                    if j == 3:
                        first_half(Block1, L, k + 1, g_next)

            def mlstm(L):
                fp, ig, e1, e2, fc, cc, mm, mt, lf = ml_rows
                dve.wait_ge(s.gates_psum, at(L, 1, 1))
                dve.tensor_tensor(ig[:], B4[0:ML_H, :], rstd[0:ML_H, :], ALU.mult)
                dve.tensor_tensor(fp[:], B5[0:ML_H, :], rstd[0:ML_H, :], ALU.mult)
                dve.drain()
                dve.tensor_scalar(ig[:], ig[:], b_gate_now[:, 0:1], None, ALU.add)
                dve.tensor_scalar(fp[:], fp[:], b_gate_now[:, 1:2], None, ALU.add).then_inc(s.gate_pre, 1)
                for t in range(NT):
                    dve.wait_ge(s.v_turned, at(L, 5, t + 1))
                    dve.tensor_copy(mv_tok[:, t, :], mb[:, 2 + t % 2, :]).then_inc(s.v_copied, 1)
                dve.tensor_scalar(lf[:], fp[:], 0.0, None, ALU.min)
                dve.drain()
                dve.wait_ge(s.log1p, at(L, 1, 1))
                dve.tensor_tensor(lf[:], lf[:], e1[:], ALU.subtract)
                dve.drain()
                dve.tensor_tensor_scan(fc[:], ones[0:ML_H, 0:1].to_broadcast([ML_H, S]), lf[:], 0.0, ALU.mult, ALU.add)
                dve.drain()
                dve.tensor_tensor(cc[:], ig[:], fc[:], ALU.subtract)
                dve.drain()
                dve.tensor_tensor_scan(mm[:], cc[:], cc[:], 0.0, ALU.max, ALU.max)
                dve.drain()
                dve.tensor_scalar(acc[0:ML_H, :], mm[:], -1.0, None, ALU.mult)
                dve.tensor_tensor(mt[:], mm[:], fc[:], ALU.add).then_inc(s.ml_rows_done, 1)
                for u in range(12, 15):
                    more_in(L, u)
                dve.wait_ge(s.c_turned, at(L, 1, 1))
                dve.tensor_copy(c_col[:].rearrange("p t h -> p (t h)"), B5[:, 0:NT * ML_H]).then_inc(s.c_copied, 1)
                more_in(L, 15)

                def minus_m(h):
                    dve.wait_ge(s.bc_ready, at(L, ML_H + 1, h + 1))
                    dve.tensor_copy(neg_m[:], B4)
                    dve.tensor_tensor(neg_md[:].rearrange("p (t q) -> p t q", t=NT), B4.rearrange("p (t q) -> p t q", t=NT),
                                      mask_sq[:, None, :].to_broadcast([P, NT, P]), ALU.add).then_inc(s.bc_copied, 1)

                minus_m(0)
                for u in range(16, 18):
                    more_in(L, u)
                dve.wait_ge(s.mo_done, at(L, 1, 1))
                for h in range(ML_H):
                    for j in range(NT):
                        e = 4 * h + j
                        dve.wait_ge(s.w_ready, at(L, 16, e + 1))
                        dve.wait_ge(s.sc_ready, at(L, 16, e + 1))
                        if h:
                            dve.wait_ge(s.pv_done, at(L, 16, e - 3))
                        o, w = ML_OFF[j], S - j * P
                        dve.scalar_tensor_tensor(out=ml_p[:, o:o + w], in0=mb[:, 1 - j % 2, 0:w], scalar=0.125,
                                                 in1=ml_w[:, o:o + w], op0=ALU.mult, op1=ALU.mult).then_inc(s.p_ready, 1)
                    if h < ML_H - 1:
                        minus_m(h + 1)
                    dve.wait_ge(s.pv_done, at(L, 16, 4 * h + 4))
                    dve.scalar_tensor_tensor(out=num_sb[:, h, :], in0=B6, scalar=par1[:, R_MLOUT + h:R_MLOUT + h + 1],
                                             in1=proj[:, 8 + h, :], op0=ALU.mult, op1=ALU.mult).then_inc(s.head_done, 1)
                    if h < ML_H - 1:
                        for g in (2 * h, 2 * h + 1):
                            gate_tile(L, g)
                dve.wait_ge(s.abs_done, at(L, 1, 1))
                dve.wait_ge(s.bc_ready, at(L, ML_H + 1, ML_H + 1))
                dve.tensor_tensor(acc[:], acc[:], B4, ALU.max)
                dve.drain()
                dve.scalar_tensor_tensor(out=acc[:], in0=acc[:], scalar=EPS, in1=acc[:], op0=ALU.mult, op1=ALU.mult)
                gate_tile(L, 6)
                dve.drain()
                dve.wait_ge(s.ml_ss, at(L, 1, 1))
                dve.scalar_tensor_tensor(out=acc[:], in0=B5, scalar=1.0 / P, in1=acc[:], op0=ALU.mult, op1=ALU.add)
                dve.drain()
                dve.reciprocal(acc[:], acc[:]).then_inc(s.ml_inv, 1)

            def more_in(L, u):
                scaled_tile(Block1, L, 1, T_IN + u, proj[:, u, :])

            def gate_tile(L, g):
                scaled_tile(Block1, L, 1, T_GATE + g, gate[g][:])

            def a_tile(L, j):
                dve.wait_ge(s.sig_done, at(L, 16, j + 1))
                read_tile(Block1, L, T_A + j, gate[j][:], gate[j])

            def swa(L):
                dve.wait_ge(s.qk_ss, at(L, 1, 1))
                dve.tensor_scalar(var[:], B6, 1.0 / 64, EPS, ALU.mult, ALU.add)
                dve.tensor_scalar(tmp[3][0:32, :], B7[0:32, :], 1.0 / 64, EPS, ALU.mult, ALU.add)
                dve.drain()
                dve.reciprocal(var[:], var[:])
                dve.reciprocal(tmp[3][0:32, :], tmp[3][0:32, :]).then_inc(s.qk_inv, 1)
                dve.tensor_scalar(small[:, 0:1], par1[:, R_QN:R_QN + 1], 0.125, None, ALU.mult)
                gate_tile(L, 7)
                gate_tile(L, 8)
                for h in range(ML_H):
                    dve.wait_ge(s.ml_bc, at(L, ML_H, h + 1))
                    dve.tensor_tensor(num_sb[:, h, :], num_sb[:, h, :], mb[:, h, :], ALU.mult).then_inc(s.ml_bc_read, 1)
                for u in range(5):
                    gain = small[:, 0:1] if u < 4 else par1[:, R_KN:R_KN + 1]
                    dve.wait_ge(s.qk_bc, at(L, 5, u + 1))
                    dve.scalar_tensor_tensor(out=proj[:, 12 + u, :], in0=proj[:, 12 + u, :], scalar=gain,
                                             in1=mb[:, u % 4, :], op0=ALU.mult, op1=ALU.mult).then_inc(s.qk_bc_read, 1)
                dve.drain().then_inc(s.qk_normed, 1)
                gate_tile(L, 9)
                dve.wait_ge(s.kk_psum, at(L, 1, 1))
                for g in range(SW_KV):
                    last = dve.tensor_copy(kk[:, g, :], mb[:, 2 + g, :])
                last.then_inc(s.kk_copied, 1)
                dve.wait_ge(s.v_turned, at(L, 5, 5))
                dve.tensor_copy(sv_tok[:].rearrange("p t c -> p (t c)"), B5).then_inc(s.v_copied, 1)

                def of_side(buf, side):
                    return buf.rearrange("p (i two) k -> p two i k", two=2)[:, side]

                def biased(b):
                    n, g = b // SW_KV, b % SW_KV
                    lo = 0 if n else P
                    buf = lg[:, b % 2, :, lo:2 * P]
                    dve.wait_ge(s.lg_ready, at(L, 8, b + 1))
                    for side in range(2):
                        last = dve.tensor_tensor(of_side(lg[:, b % 2], side)[:, :, lo:2 * P],
                                                 mb[:, side, :].rearrange("p (i k) -> p i k", i=2)[:, :, lo:2 * P],
                                                 of_side(bias[:, g * SW_G:(g + 1) * SW_G], side)[:, :, lo:2 * P], ALU.add)
                    last.then_inc(s.lg_read, 1)
                    dve.drain()
                    dve.tensor_reduce(small[:, 20:24], buf, AX.X, ALU.max)
                    dve.drain()
                    dve.tensor_tensor(small[:, 20:24], small[:, 20:24], sinks_now[:, g * SW_G:g * SW_G + SW_G], ALU.max)
                    dve.drain()
                    dve.tensor_scalar(small[:, 4:8], small[:, 20:24], -1.0, None, ALU.mult)
                    dve.tensor_tensor(small[:, 8:12], sinks_now[:, g * SW_G:g * SW_G + SW_G], small[:, 20:24],
                                      ALU.subtract).then_inc(s.mx_ready, 1)

                biased(0)
                dve.wait_ge(s.ha_rounded, at(L, 1, 1))
                dve.tensor_tensor(hal[:], num_sb[:], hah[:].bitcast(F32), ALU.subtract).then_inc(s.ha_ready, 1)
                dve.drain()
                for b in range(8):
                    n, g = b // SW_KV, b % SW_KV
                    lo = 0 if n else P
                    dve.wait_ge(s.ex_ready, at(L, 8, b + 1))
                    dve.tensor_tensor(small[:, 24:28], small[:, 12:16], small[:, 16:20], ALU.add)
                    dve.drain()
                    dve.reciprocal(small[:, 28:32], small[:, 24:28])
                    dve.drain()
                    for i in range(SW_G):
                        last = dve.tensor_scalar(lg[:, b % 2, i, lo:2 * P], lg[:, b % 2, i, lo:2 * P],
                                                 small[:, 28 + i:29 + i], None, ALU.mult)
                    last.then_inc(s.pn_ready, 1)
                    if b < 7:
                        biased(b + 1)
                    dve.wait_ge(s.pt_ready, at(L, 8, b + 1))
                    for side in ((0, 1) if n else (1,)):
                        last = dve.tensor_copy(pt_sb[:, side].rearrange("p i q -> p (i q)"), mb[:, 2 + side, :])
                    last.then_inc(s.pt_copied, 1)
                    if b < 6:
                        gate_tile(L, 10 + b)
                    else:
                        for j in (2 * (b - 6), 2 * (b - 6) + 1):
                            a_tile(L, j)
                    dve.wait_ge(s.o_ready, at(L, 8, b + 1))
                    src = B6[:, 0:2 * P].rearrange("p (i q) -> p i q", i=2)
                    split(hbh[:, 2 * g:2 * g + 2, n * P:(n + 1) * P], hbl[:, 2 * g:2 * g + 2, n * P:(n + 1) * P], src)\
                        .then_inc(s.o_done, 1)

            def gated(L):
                for j in range(4, KT):
                    a_tile(L, j)
                for j in range(KT):
                    ga, gb = gate[j], gate[KT + j]
                    dve.wait_ge(s.sig_done, at(L, 16, KT + j + 1))
                    read_tile(Block1, L, T_B + j, gb[:], gb)
                    dve.drain()
                    dve.tensor_tensor(ga[:], ga[:], gb[:], ALU.add)
                    dve.drain()
                    split(mh[:, j, :], ml[:, j, :], ga[:]).then_inc(s.mixed_ready, 1)
                for j in range(KT):
                    add_x(Block1, L, T_OUT + j, j)
                    if j == 3:
                        first_half(Block1, L, 2, par1[:, R_FFN2:R_FFN2 + KT])

            def ple(L):
                norm(Block1, L, 3, par1[:, R_PLE:R_PLE + KT])
                for j in range(6):
                    scaled_tile(Block1, L, 3, T_PLE + j, gate_sg[:, j, :])
                dve.wait_ge(s.p_turned, at(L, 1, 1))
                for k in range(2):
                    last = split(pth[:, k, :], ptl[:, k, :], mb[:, k, :])
                last.then_inc(s.pt_split, 1)
                for j in range(6, KT):
                    scaled_tile(Block1, L, 3, T_PLE + j, gate_sg[:, j, :])
                for j in range(KT):
                    dve.wait_ge(s.sg_done, at(L, KT, j + 1))
                    read_tile(Block1, L, T_PLE + KT + j, gate_sg[:, j, :], gate_sg[:, j, :], inc=3 if j == KT - 1 else 1)
                    dve.drain()
                    dve.tensor_tensor(x_sb[:, j, :], x_sb[:, j, :], gate_sg[:, j, :], ALU.add)
                    if j == 3:
                        dve.tensor_copy(g_first, first_gains[:, bass.ds(L * KT + KT, KT)])
                        first_half(Block1, L, Block1.norms, g_first)

            with dve.Fori(0, 2) as L:
                dve.tensor_copy(par1[:], p1[:, bass.ds(L * R1, R1)])
                dve.drain()
                ffn(L, 0, g_first, par1[:, R_MIX:R_MIX + KT], T_FFN1, 0)
                norm(Block1, L, 1, par1[:, R_MIX:R_MIX + KT])
                dve.tensor_copy(b_gate_now[:, None, :], b_gate[:, bass.ds(L, 1), :])
                dve.tensor_copy(sinks_now[:, None, :], sinks[:, bass.ds(L, 1), :])
                dve.drain()
                dve.wait_ge(s.gate_landed, at(L, 16, 16))
                split(gate_h[:], gate_l[:], gate_raw[:]).then_inc(s.gate_split, 1)
                for u in range(12):
                    more_in(L, u)
                mlstm(L)
                dve.wait_ge(s.toep_in, 16)
                swa(L)
                gated(L)
                ffn(L, 2, par1[:, R_FFN2:R_FFN2 + KT], par1[:, R_PLE:R_PLE + KT], T_FFN2, FT)
                ple(L)

            def more_in2(L, u):
                tile = ORDER2[u]
                rows = (0, MLA_D) if u == U_DT else (0, P)
                scaled_tile(Block2, L, 0, T2_IN + u, proj2[rows[0]:rows[1], tile, :], rows=rows)

            def convolve(L, k):
                more_in2(L, 4 + k)
                w = lambda tap: par2[:, Q_CW + 5 * tap + k:Q_CW + 5 * tap + k + 1]
                dve.drain()
                dve.tensor_scalar(conv[:, k, :], proj2[:, 7 + k, :], w(3), par2[:, Q_CB + k:Q_CB + k + 1], ALU.mult,
                                  ALU.add)
                for tap in range(3):
                    lag = 3 - tap
                    dve.drain()
                    last = dve.scalar_tensor_tensor(out=conv[:, k, lag:S], in0=proj2[:, 7 + k, 0:S - lag], scalar=w(tap),
                                                    in1=conv[:, k, lag:S], op0=ALU.mult, op1=ALU.add)
                return last

            def gmlp(L):
                for u in range(4):
                    more_in2(L, u)
                for k in range(2):
                    convolve(L, k)
                dve.wait_ge(s.gv_ss, at(L, 1, 1))
                invert(tmp[0][:], B4, 1.0 / (2 * P)).then_inc(s.gv_inv, 1)
                dve.wait_ge(s.ws_turned, at(L, 1, 1))
                dve.tensor_tensor(ws_t[:], B7.rearrange("p (h t) -> p h t", h=4),
                                  tri_st[:, None, :].to_broadcast([P, 4, P]), ALU.mult).then_inc(s.ws_copied, 1)
                convolve(L, 2)
                dve.wait_ge(s.gv_rs, at(L, 1, 1))
                for k in range(2):
                    last = dve.scalar_tensor_tensor(out=proj2[:, 2 + k, :], in0=proj2[:, 2 + k, :],
                                                    scalar=par2[:, Q_GV + k:Q_GV + k + 1], in1=tmp[1][:], op0=ALU.mult,
                                                    op1=ALU.mult)
                last.then_inc(s.gv_normed, 1)
                convolve(L, 3)
                dve.wait_ge(s.gv_turned, at(L, 1, 1))
                for q in range(2):
                    last = dve.tensor_copy(gv_tok[:, 2 * q:2 * q + 2, :].rearrange("p t c -> p (t c)"), mb[:, 1 + q, :])
                last.then_inc(s.gv_copied, 1)
                convolve(L, 4).then_inc(s.conv_done, 1)
                more_in2(L, U_DT)
                dve.drain()
                dve.tensor_scalar(tmp[2][0:SSD_H, :], proj2[0:SSD_H, 12, :], dt_now[:, 0:1], None, ALU.add)\
                   .then_inc(s.dt_pre, 1)
                dve.wait_ge(s.gm_psum, at(L, 1, 1))
                for k in range(2):
                    last = dve.tensor_tensor(proj2[:, k, :], mb[:, k, :], proj2[:, k, :], ALU.mult)
                last.then_inc(s.gm_done, 1)

            def ssd(L):
                pre, e1 = tmp[2][0:SSD_H, :], tmp[3][0:SSD_H, :]
                more_in2(L, U_Z)
                dve.wait_ge(s.xs_turned, at(L, 1, 1))
                for t in range(NT):
                    last = dve.tensor_copy(xs_tok[:, t, :], mb[:, t, 0:384])
                last.then_inc(s.xs_copied, 1)
                dve.wait_ge(s.dt_log, at(L, 1, 1))
                dve.scalar_tensor_tensor(out=var[0:SSD_H, :], in0=pre, scalar=0.0, in1=e1, op0=ALU.max, op1=ALU.add)
                dve.tensor_scalar(small[0:SSD_H, 2:3], small[0:SSD_H, 1:2], -1.0, None, ALU.mult)
                dve.drain()
                dve.tensor_scalar(tmp[0][0:SSD_H, :], var[0:SSD_H, :], small[0:SSD_H, 2:3], None, ALU.mult)
                dve.drain()
                dve.tensor_tensor_scan(acc[0:SSD_H, :], ones[0:SSD_H, 0:1].to_broadcast([SSD_H, S]), tmp[0][0:SSD_H, :], 0.0,
                                       ALU.mult, ALU.add).then_inc(s.dt_rows_done, 1)
                more_in2(L, U_Z + 1)
                dve.wait_ge(s.dcol_turned, at(L, 1, 1))
                dve.tensor_scalar(a_col[:].rearrange("p t h -> p (t h)"), B5[:, 0:NT * SSD_H], -1.0, None, ALU.mult)
                dve.tensor_copy(dt_col[:].rearrange("p t h -> p (t h)"), B5[:, 64:64 + NT * SSD_H]).then_inc(s.dcol_copied, 1)
                dve.drain()

                def products(g):
                    for j in range(NT):
                        o, w = ML_OFF[j], S - j * P
                        dve.wait_ge(s.cb_ready, at(L, 8, 4 * g + j + 1))
                        dve.tensor_copy(cb[:, o:o + w], mb[:, 1 + j % 2, 0:w]).then_inc(s.cb_copied, 1)

                def decays(h):
                    dve.wait_ge(s.abc_ready, at(L, SSD_H, h + 1))
                    dve.tensor_copy(tmp[0][:], B4)
                    dve.tensor_tensor(tmp[1][:].rearrange("p (t q) -> p t q", t=NT), B4.rearrange("p (t q) -> p t q", t=NT),
                                      mask_sq[:, None, :].to_broadcast([P, NT, P]), ALU.add).then_inc(s.abc_copied, 1)

                def latent(k):
                    more_in2(L, U_C + k)
                    hi, lo = (cqh[:, k, :], cql[:, k, :]) if k < 3 else (ckh[:, k - 3, :], ckl[:, k - 3, :])
                    g = par2[:, Q_CQ + k:Q_CQ + k + 1]
                    dve.drain()
                    dve.tensor_scalar(hi, proj2[:, 13 + k, :], g, None, ALU.mult)
                    dve.drain()
                    return dve.scalar_tensor_tensor(out=lo, in0=proj2[:, 13 + k, :], scalar=g, in1=hi.bitcast(F32),
                                                    op0=ALU.mult, op1=ALU.subtract)

                decays(0)
                more_in2(L, U_Z + 2)
                latent(0)
                for h in range(SSD_H):
                    tile = h // 2
                    if h % 3 == 0:
                        products(h // 3)
                        dve.drain()
                    for j in range(NT):
                        o, w = ML_OFF[j], S - j * P
                        dve.wait_ge(s.sw_ready, at(L, 24, 4 * h + j + 1))
                        if h and j == 0:
                            dve.wait_ge(s.y_psum, at(L, SSD_H, h))
                        dve.scalar_tensor_tensor(out=sd_p[:, o:o + w], in0=cb[:, o:o + w], scalar=dt_col[:, j, h:h + 1],
                                                 in1=sd_w[:, o:o + w], op0=ALU.mult, op1=ALU.mult).then_inc(s.sp_ready, 1)
                    if h < SSD_H - 1:
                        decays(h + 1)
                    if h < 3:
                        latent(1 + h)
                    elif h == 3:
                        latent(4).then_inc(s.c_split, 1)
                    elif h == 4:
                        dve.wait_ge(s.c_ss, at(L, 1, 1))
                        dve.tensor_scalar(tmp[2][0:64, :], B5[0:64, :], 1.0 / 384, EPS, ALU.mult, ALU.add)
                        dve.tensor_scalar(tmp[2][64:P, :], B5[64:P, :], 1.0 / 256, EPS, ALU.mult, ALU.add)
                        dve.drain()
                        dve.reciprocal(tmp[2][:], tmp[2][:]).then_inc(s.c_inv, 1)
                        for k in range(2):
                            split(xh[:, k, :], xl[:, k, :], proj2[:, k, :])
                        dve.drain()
                    if h % 2:
                        dve.wait_ge(s.y_psum, at(L, SSD_H, h + 1))
                        if h == 1:
                            dve.wait_ge(s.z_silu, at(L, 1, 1))
                        dve.scalar_tensor_tensor(out=conv[:, tile, :], in0=conv[:, tile, :], scalar=d_skip_now[:, tile:tile + 1],
                                                 in1=mb[:, 2 + tile % 2, :], op0=ALU.mult, op1=ALU.add)
                        dve.drain()
                        dve.tensor_tensor(conv[:, tile, :], proj2[:, 4 + tile, :], conv[:, tile, :], ALU.mult)\
                           .then_inc(s.y_done, 1)

            def mla(L):
                B = Block2
                dve.wait_ge(s.c_scaled, at(L, 1, 1))
                for h in range(4):
                    read_tile(B, L, T2_QB + h, q96[:, h, :], acc, rows=(0, MLA_D))
                rows = slice(64, MLA_D)
                dve.wait_ge(s.rot_psum, at(L, 1 + MLA_H, 1))
                dve.tensor_tensor(rot_sin[rows, :], B5[rows, :], rope[rows, 1, :], ALU.mult).then_inc(s.rot_read, 1)
                dve.tensor_tensor(k_rot[rows, :], proj2[rows, 12, :], rope[rows, 0, :], ALU.mult)
                dve.drain()
                dve.tensor_tensor(k_rot[rows, :], k_rot[rows, :], rot_sin[rows, :], ALU.add).then_inc(s.rot_done, 1)
                dve.wait_ge(s.y_ss, at(L, 1, 1))
                dve.tensor_scalar(tmp[0][:], B7, 1.0 / 192, EPS, ALU.mult, ALU.add)
                dve.drain()
                dve.reciprocal(tmp[0][:], tmp[0][:]).then_inc(s.y_inv, 1)
                for h in range(4, MLA_H):
                    read_tile(B, L, T2_QB + h, q96[:, h, :], acc, rows=(0, MLA_D))
                dve.wait_ge(s.y_bc, at(L, 1, 1))
                for k, scale in ((0, B6), (2, B7), (1, tmp[0][:])):
                    last = dve.scalar_tensor_tensor(out=tmp[1 + k][:], in0=conv[:, k, :], in1=scale, op0=ALU.mult,
                                                    scalar=par2[:, Q_SSD + k:Q_SSD + k + 1], op1=ALU.mult)
                    if k == 2:
                        last.then_inc(s.y_bc_read, 1)
                dve.drain().then_inc(s.y_scaled, 1)
                for h in range(MLA_H):
                    t = T2_KVB + h
                    src = bank[(B.base_tile + t) % TILE_BANKS]
                    dve.wait_ge(s.tile_ready, tiles_in(B, L, t))
                    if h >= 2:
                        dve.wait_ge(s.vt_psum, at(L, MLA_H, h - 1))
                    dve.tensor_tensor(k96[0:64, h, :], src[0:64, :], var[0:64, :], ALU.mult)
                    dve.tensor_tensor(v_ft[64:P, h % 2, :], src[64:P, :], var[64:P, :], ALU.mult).then_inc(s.tile_evacuated, 1)
                    dve.drain().then_inc(s.kv_done, 1)
                    rotate(L, h)
                    if h == 0:
                        dve.wait_ge(s.y_rounded, at(L, 1, 1))
                        dve.tensor_tensor(xl[:, 2:5, :], tmp_all[:, 1:4, :], xh[:, 2:5, :].bitcast(F32), ALU.subtract)\
                           .then_inc(s.ssd_done, 1)

                def biggest(c):
                    n = c % NT
                    dve.wait_ge(s.al_ready, at(L, 24, c + 1))
                    dve.tensor_reduce(small[:, 40 + n:41 + n], bank[c % TILE_BANKS][:, 0:(n + 1) * P], AX.X, ALU.max)
                    dve.drain()
                    dve.tensor_scalar(small[:, 32 + n:33 + n], small[:, 40 + n:41 + n], -MLA_SCALE, None, ALU.mult)\
                       .then_inc(s.am_ready, 1)

                def normed(c):
                    n = c % NT
                    dve.wait_ge(s.ae_ready, at(L, 24, c + 1))
                    dve.reciprocal(small[:, 44 + n:45 + n], small[:, 36 + n:37 + n])
                    dve.drain()
                    w = (n + 1) * P
                    dve.tensor_scalar(prob[:, c % 4, 0:w], prob[:, c % 4, 0:w], small[:, 44 + n:45 + n], None, ALU.mult)\
                       .then_inc(s.ap_ready, 1)

                def head_split(h):
                    half = 64 * (h % 2)
                    dve.wait_ge(s.ao_ready, at(L, MLA_H, h + 1))
                    split(xh[half:half + 64, 5 + h // 2, :], xl[half:half + 64, 5 + h // 2, :],
                          mb[half:half + 64, 2 + h % 2, :]).then_inc(s.ao_done, 1)

                blocks = NT * MLA_H
                biggest(0)
                biggest(1)
                for c in range(blocks):
                    if c + 2 < blocks:
                        biggest(c + 2)
                    normed(c)
                    if c >= NT and c % NT == 1:
                        head_split(c // NT - 1)
                head_split(MLA_H - 1)

            def rotate(L, h):
                dve.wait_ge(s.rot_psum, at(L, 1 + MLA_H, h + 2))
                dve.tensor_tensor(rot_sin[0:MLA_D, :], mb[0:MLA_D, 2 + (h + 1) % 2, :], rope[:, 1, :], ALU.mult)\
                   .then_inc(s.rot_read, 1)
                dve.tensor_tensor(q96[:, h, :], q96[:, h, :], rope[:, 0, :], ALU.mult)
                dve.drain()
                dve.tensor_tensor(q96[:, h, :], q96[:, h, :], rot_sin[0:MLA_D, :], ALU.add).then_inc(s.rot_done, 1)
                dve.drain()

            with dve.Fori(0, 2) as L:
                B = Block2
                dve.tensor_copy(par2[:], p2[:, bass.ds(L * R2, R2)])
                dve.drain()
                norm(B, L, 0, g_first)
                dve.tensor_copy(d_skip_now[:, None, :], d_skip[:, bass.ds(L, 1), :])
                dve.tensor_copy(dt_now[:, 0:1], dt_bias[:, bass.ds(L, 1)])
                dve.tensor_copy(dt_now[:, 1:2], dt_a[:, bass.ds(L, 1)])
                dve.tensor_copy(bs_now[:, None, :], bs_rows[:, bass.ds(L, 1), :])
                dve.drain()
                gmlp(L)
                ssd(L)
                mla(L)
                for j in range(KT):
                    add_x(B, L, T2_OUT + j, j)
                first_half(B, L, 1, par2[:, Q_MLP:Q_MLP + KT])
                norm(B, L, 1, par2[:, Q_MLP:Q_MLP + KT])
                for half in range(2):
                    t0 = T2_MLP + half * (HALF2 + 8)
                    with dve.Fori(0, HALF2 // 4) as i:
                        for f in range(4):
                            ta, tb = tmp[f % 2], tmp[2 + f % 2]
                            scaled_tile(B, L, 1, t0 + f, ta[:], i, 4)
                            dve.drain()
                            dve.scalar_tensor_tensor(out=tb[:], in0=ta[:], scalar=0.0, in1=ta[:], op0=ALU.max, op1=ALU.mult)
                            dve.drain()
                            j = i * 4 + f
                            split(hh[:, j, :], hl[:, j, :], tb[:]).then_inc(s.hidden_ready, 1)
                    for j in range(KT):
                        add_x(B, L, t0 + HALF2 + j, j, inc=3 if half and j == KT - 1 else 1)
                        if half and j == 3:
                            dve.tensor_copy(g_first, first_gains[:, bass.ds(L * KT + 3 * KT, KT)])
                            first_half(B, L, B.norms, g_first)

            norm(Last, None, 0, None)
            dve.wait_ge(s.rstd_ready, 13)
            for j in range(KT):
                last = dve.scalar_tensor_tensor(out=y_sb[:, j, :], in0=x_sb[:, j, :], scalar=p2[:, 2 * R2 + j:2 * R2 + j + 1],
                                                in1=rstd[:], op0=ALU.mult, op1=ALU.mult)
            last.then_inc(s.fin_y, 1)
            for c in range(2 * NT):
                t, side = c // 2, c % 2
                dve.wait_ge(s.fin_turned, c + 1)
                dve.tensor_copy(out_tok[:, t, side * S:(side + 1) * S], mb[:, c % 4, :]).then_inc(s.fin_copied, 1)


ML_OFF = [0, 512, 896, 1152]
N_SMALL = 11 + 1 + 4 + 2 + 4 + 2 + 2 + 1


def constants(np):
    pack = np.zeros((P, CONSTS), np.float32)
    r = np.arange(P)
    pack[:, C_IDENT:C_IDENT + P] = np.eye(P)
    for half in range(2):
        pack[64 * half:64 * half + 64, C_SEL + 16 * half:C_SEL + 16 * half + 16] = 1.0
        pack[16 * half::32, C_BACK + 64 * half:C_BACK + 64 * half + 64] = 1.0
    sel4 = (np.arange(ML_H)[:, None] == r[None, :] // 32).astype(np.float32)
    pack[:, C_DUP0:C_DUP0 + P] = r[:, None] == r[None, :] % 64
    pack[:, C_DUP1:C_DUP1 + P] = r[:, None] == 64 + r[None, :] % 64
    pack[:, C_MQS:C_MQS + P] = np.where(r[None, :] <= r[:, None], 0.0, NEG)
    pack[:, C_MSQ:C_MSQ + P] = np.where(r[None, :] >= r[:, None], 0.0, NEG)
    for i in range(16):
        pack[80 + i, C_ROT + 64 + i] = -1.0
        pack[64 + i, C_ROT + 80 + i] = 1.0
    pack[:, C_TRI:C_TRI + P] = r[None, :] >= r[:, None]
    dist = 255 - np.arange(TOEP)
    far = 16 + (np.log(np.maximum(dist, 1) / 16) / np.log(128 / 16) * 16).astype(np.int32)
    bucket = np.where(dist < 16, dist, np.minimum(far, 31))
    inside = (dist >= 0) & (dist < P)
    onehot = ((np.arange(32)[:, None] == bucket[None, :]) & inside[None, :]).astype(np.float32)
    pad = np.broadcast_to(np.where(inside, 0.0, NEG).astype(np.float32), (SW_H, TOEP)).copy()
    rope = np.zeros((MLA_D, 2, S), np.float32)
    rope[:, 0] = 1.0
    inv_freq = np.power(np.float32(10000.0), -np.arange(16, dtype=np.float32) / np.float32(16))
    ang = np.arange(S, dtype=np.float32)[:, None] * inv_freq[None, :]
    for part in (64, 80):
        rope[part:part + 16, 0] = np.cos(ang).T
        rope[part:part + 16, 1] = np.sin(ang).T
    return {"const_pack": pack, "sel4": sel4, "onehot": onehot, "pad": pad, "rope_pack": rope}


_INS = ['x', 'p', 'ffn1_norm', 'ffn1_wi', 'ffn1_wo', 'mix_norm', 'w_in', 'b_igate', 'b_fgate', 'ml_out_norm', 'q_norm',
        'k_norm', 'sinks', 'rel_bias', 'w_a', 'w_b', 'w_out', 'ffn2_norm', 'ffn2_wi', 'ffn2_wo', 'ple_norm', 'w_ple_gate',
        'w_ple', 'norm_mix_g_2', 'w_in_2', 'gmlp_v_norm_g_2', 'gmlp_w_s_2', 'gmlp_b_s_2', 'ssd_conv_w_2', 'ssd_conv_b_2',
        'ssd_dt_bias_2', 'ssd_a_log_2', 'ssd_d_2', 'ssd_norm_g_2', 'mla_q_norm_g_2', 'mla_w_qb_2', 'mla_kv_norm_g_2',
        'mla_w_kvb_2', 'w_out_2', 'norm_mlp_g_2', 'mlp_w1_2', 'mlp_w2_2', 'final_norm_g_2']


def kernel(**inputs):
    import numpy as _np
    import concourse.bacc as _bacc
    from concourse import mybir as _mybir
    from concourse.bass_utils import run_bass_kernel_spmd as _run

    nc = _bacc.Bacc("TRN2", target_bir_lowering=False, num_devices=1)
    arrays, args = {}, {}
    for name, value in [(n, inputs[n]) for n in _INS] + list(constants(_np).items()):
        v = _np.ascontiguousarray(value)
        arrays[f"in_{name}_dram"] = v
        args[name] = nc.dram_tensor(f"in_{name}_dram", v.shape, _mybir.dt.from_np(v.dtype), kind="ExternalInput").ap()
    args["out"] = nc.dram_tensor("out_dram", (1, S, D), _mybir.dt.float32, kind="ExternalOutput").ap()
    program(nc, args)
    r = _run(nc, [arrays], core_ids=[0])
    return r.results[0]["out_dram"]
```
